# Optimizing a Trainium2 kernel written in Bass

```python
import math
import jax, jax.numpy as jnp
from jax import lax
import numpy as np

D_MODEL = 1024
BATCH = 1
SEQ = 2048
DEPTH = 1
DEC_BATCH = 8
DEC_SEQ = 8
PAST_LEN = 16384
PAGE_SIZE = 128

MIX_W = D_MODEL
N_HEADS_ATT = 8
N_KV_HEADS = 2
HEAD_DIM_ATT = 64
GQA_GROUP = N_HEADS_ATT // N_KV_HEADS
ATT_W = N_HEADS_ATT * HEAD_DIM_ATT
WINDOW = 128
ATT_BLOCK = WINDOW
NUM_BUCKETS = 32
MAX_DISTANCE = 128
N_HEADS_MLSTM = 4
DV_MLSTM = (MIX_W - ATT_W) // N_HEADS_MLSTM
DK_MLSTM = DV_MLSTM // 2
MLSTM_W = N_HEADS_MLSTM * DV_MLSTM
MLSTM_CHUNK = 64
D_FF = 4 * D_MODEL
EPS = 1e-6
SPLIT_SIZES = (ATT_W, N_KV_HEADS * HEAD_DIM_ATT, N_KV_HEADS * HEAD_DIM_ATT,
               N_HEADS_MLSTM * DK_MLSTM, N_HEADS_MLSTM * DK_MLSTM, MLSTM_W, MLSTM_W,
               2 * N_HEADS_MLSTM)
IN_COLS = sum(SPLIT_SIZES)

kernel_name = 'hymba_swa_sink_mlstm_decode_step'

def rmsnorm(x, g):
    xf = x.astype(jnp.float32)
    y = xf * lax.rsqrt(jnp.mean(xf * xf, axis=-1, keepdims=True) + EPS)
    return (y * g.astype(jnp.float32)).astype(x.dtype)

def t5_bucket(dist):
    max_exact = NUM_BUCKETS // 2
    d = jnp.maximum(dist, 0)
    ratio = jnp.maximum(d, 1).astype(jnp.float32) / max_exact
    large = max_exact + (jnp.log(ratio) / math.log(MAX_DISTANCE / max_exact)
                         * (NUM_BUCKETS - max_exact)).astype(jnp.int32)
    large = jnp.minimum(large, NUM_BUCKETS - 1)
    return jnp.where(d < max_exact, d, large)

def in_projection(x, g_norm, w_in, b_gates):
    h = rmsnorm(x, g_norm)
    z = jnp.einsum('btd,dc->btc', h, w_in)
    idx = list(np.cumsum(SPLIT_SIZES)[:-1])
    qa, ka, va, qm, km, vm, om, gates = jnp.split(z, idx, axis=-1)
    B, T = x.shape[:2]
    qa = qa.reshape(B, T, N_KV_HEADS, GQA_GROUP, HEAD_DIM_ATT)
    ka = ka.reshape(B, T, N_KV_HEADS, HEAD_DIM_ATT)
    va = va.reshape(B, T, N_KV_HEADS, HEAD_DIM_ATT)
    qm = qm.reshape(B, T, N_HEADS_MLSTM, DK_MLSTM)
    km = km.reshape(B, T, N_HEADS_MLSTM, DK_MLSTM) * (DK_MLSTM ** -0.5)
    vm = vm.reshape(B, T, N_HEADS_MLSTM, DV_MLSTM)
    om = jax.nn.sigmoid(om.reshape(B, T, N_HEADS_MLSTM, DV_MLSTM))
    g = gates.astype(jnp.float32) + b_gates.astype(jnp.float32)
    ig = g[..., :N_HEADS_MLSTM]
    lf = jax.nn.log_sigmoid(g[..., N_HEADS_MLSTM:])
    return qa, ka, va, qm, km, vm, om, ig, lf

def attend_sinks(q, k, v, dist, valid, sinks, rel_bias):
    tq, tk = dist.shape
    s = jnp.einsum('...qhgd,...khd->...hgqk', q, k).astype(jnp.float32) * (HEAD_DIM_ATT ** -0.5)
    bias = rel_bias[t5_bucket(dist)].astype(jnp.float32)
    bias = bias.transpose(2, 0, 1).reshape(N_KV_HEADS, GQA_GROUP, tq, tk)
    s = jnp.where(valid, s + bias, -jnp.inf)
    sink = sinks.astype(jnp.float32).reshape(N_KV_HEADS, GQA_GROUP, 1, 1)
    m = jnp.maximum(s.max(axis=-1, keepdims=True), sink)
    p = jnp.exp(s - m)
    p = p / (p.sum(axis=-1, keepdims=True) + jnp.exp(sink - m))
    return jnp.einsum('...hgqk,...khd->...qhgd', p.astype(v.dtype), v)

def swa_prompt(qa, ka, va, sinks, rel_bias):
    B, S = qa.shape[:2]
    nb = S // ATT_BLOCK
    qb = qa.reshape(B, nb, ATT_BLOCK, N_KV_HEADS, GQA_GROUP, HEAD_DIM_ATT)

    def band(a):
        ab = a.reshape(B, nb, ATT_BLOCK, N_KV_HEADS, HEAD_DIM_ATT)
        prev = jnp.concatenate([jnp.zeros_like(ab[:, :1]), ab[:, :-1]], axis=1)
        return jnp.concatenate([prev, ab], axis=2)

    kk, vv = band(ka), band(va)
    qi = jnp.arange(ATT_BLOCK)[:, None]
    kj = jnp.arange(2 * ATT_BLOCK)[None, :]
    dist = qi + ATT_BLOCK - kj
    in_win = (dist >= 0) & (dist <= WINDOW)
    has_prev = (jnp.arange(nb)[:, None, None] > 0) | (kj >= ATT_BLOCK)[None]
    valid = (in_win[None] & has_prev)[None, :, None, None]
    o = attend_sinks(qb, kk, vv, dist, valid, sinks, rel_bias)
    return o.reshape(B, S, ATT_W)

def swa_sample(qa, ka, va, ck, cv, sinks, rel_bias):
    B, T = qa.shape[:2]
    W = ck.shape[1]
    kk = jnp.concatenate([ck.astype(ka.dtype), ka], axis=1)
    vv = jnp.concatenate([cv.astype(va.dtype), va], axis=1)
    dist = (W + jnp.arange(T))[:, None] - jnp.arange(W + T)[None, :]
    valid = (dist >= 0) & (dist <= WINDOW)
    o = attend_sinks(qa, kk, vv, dist, valid, sinks, rel_bias)
    return o.reshape(B, T, ATT_W), kk[:, -W:], vv[:, -W:]

def mlstm_chunk(carry, inp):
    C, n, m = carry
    q, k, v, ig, lf = inp
    L = q.shape[-2]
    tri = jnp.tril(jnp.ones((L, L), dtype=bool))
    b = jnp.cumsum(lf, axis=-1)
    logD = jnp.where(tri, b[..., :, None] - b[..., None, :] + ig[..., None, :], -jnp.inf)
    m_t = jnp.maximum(b + m[..., None], logD.max(axis=-1))
    D = jnp.exp(logD - m_t[..., None])
    inter = jnp.exp(b + m[..., None] - m_t)
    S = jnp.einsum('bhtd,bhsd->bhts', q, k) * D
    num = inter[..., None] * jnp.einsum('bhtd,bhde->bhte', q, C) + jnp.einsum('bhts,bhse->bhte', S, v)
    den = inter * jnp.einsum('bhtd,bhd->bht', q, n) + S.sum(axis=-1)
    h = num / jnp.maximum(jnp.abs(den), jnp.exp(-m_t))[..., None]
    m_new = m_t[..., -1]
    w = jnp.exp(b[..., -1:] - b + ig - m_new[..., None])
    decay = jnp.exp(b[..., -1] + m - m_new)
    C_new = decay[..., None, None] * C + jnp.einsum('bhs,bhsd,bhse->bhde', w, k, v)
    n_new = decay[..., None] * n + jnp.einsum('bhs,bhsd->bhd', w, k)
    return (C_new, n_new, m_new), h

def mlstm_sequence(q, k, v, ig, lf, C0, n0, m0):
    B, T = q.shape[:2]
    L = math.gcd(T, MLSTM_CHUNK)
    nc = T // L

    def to_chunks(a):
        a = a.astype(jnp.float32).reshape((B, nc, L, N_HEADS_MLSTM) + a.shape[3:])
        return jnp.moveaxis(a, (1, 3), (0, 2))

    xs = (to_chunks(q), to_chunks(k), to_chunks(v), to_chunks(ig), to_chunks(lf))
    carry0 = (C0.astype(jnp.float32), n0.astype(jnp.float32), m0.astype(jnp.float32))
    carry, h = lax.scan(mlstm_chunk, carry0, xs)
    h = jnp.moveaxis(h, (0, 2), (1, 3)).reshape(B, T, N_HEADS_MLSTM, DV_MLSTM)
    return h, carry

def merge_heads(att, h_m, o_m, g_att, g_m, w_out):
    B, T = att.shape[:2]
    a = rmsnorm(att, g_att)
    hm = o_m.astype(jnp.float32) * h_m
    hm = rmsnorm(hm, g_m.reshape(N_HEADS_MLSTM, DV_MLSTM)).reshape(B, T, MLSTM_W).astype(a.dtype)
    mix = jnp.concatenate([a, hm], axis=-1)
    return jnp.einsum('btc,cd->btd', mix, w_out)

def channel_mlp(x, g, w_up, w_down):
    h = rmsnorm(x, g)
    u = jnp.maximum(jnp.einsum('btd,df->btf', h, w_up), 0)
    return jnp.einsum('btf,fd->btd', u * u, w_down)

def setup_inputs(seed: int = 0) -> dict:
    key = jax.random.key(seed)
    ks = jax.random.split(key, 24)
    f32 = jnp.float32
    nrm = lambda k, shape, scale: scale * jax.random.normal(k, shape, f32)
    win_cache = min(WINDOW, PAST_LEN)
    return {
        'x_prompt': nrm(ks[0], (BATCH, SEQ, D_MODEL), 1.0),
        'x_sample': nrm(ks[1], (DEC_BATCH, DEC_SEQ, D_MODEL), 1.0),
        'cache_k_win': nrm(ks[2], (DEPTH, DEC_BATCH, win_cache, N_KV_HEADS, HEAD_DIM_ATT), 1.0),
        'cache_v_win': nrm(ks[3], (DEPTH, DEC_BATCH, win_cache, N_KV_HEADS, HEAD_DIM_ATT), 1.0),
        'state_C': nrm(ks[4], (DEPTH, DEC_BATCH, N_HEADS_MLSTM, DK_MLSTM, DV_MLSTM), 0.3),
        'state_n': nrm(ks[5], (DEPTH, DEC_BATCH, N_HEADS_MLSTM, DK_MLSTM), 0.3),
        'state_m': 1.0 + nrm(ks[6], (DEPTH, DEC_BATCH, N_HEADS_MLSTM), 0.5),
        'rel_bias': nrm(ks[7], (NUM_BUCKETS, N_HEADS_ATT), 0.5),
        'norm_mix': 1.0 + nrm(ks[8], (DEPTH, D_MODEL), 0.02),
        'w_in': nrm(ks[9], (DEPTH, D_MODEL, IN_COLS), D_MODEL ** -0.5),
        'b_gates': jnp.concatenate([nrm(ks[10], (DEPTH, N_HEADS_MLSTM), 0.1),
                                    3.0 + nrm(ks[11], (DEPTH, N_HEADS_MLSTM), 0.1)], axis=-1),
        'attn_sinks': nrm(ks[12], (DEPTH, N_HEADS_ATT), 0.5),
        'norm_attn_out': 1.0 + nrm(ks[13], (DEPTH, ATT_W), 0.02),
        'norm_mlstm_out': 1.0 + nrm(ks[14], (DEPTH, MLSTM_W), 0.02),
        'w_out': nrm(ks[15], (DEPTH, MIX_W, D_MODEL), MIX_W ** -0.5),
        'norm_mlp': 1.0 + nrm(ks[16], (DEPTH, D_MODEL), 0.02),
        'w_up': nrm(ks[17], (DEPTH, D_MODEL, D_FF), D_MODEL ** -0.5),
        'w_down': nrm(ks[18], (DEPTH, D_FF, D_MODEL), D_FF ** -0.5),
        'norm_final': 1.0 + nrm(ks[19], (D_MODEL,), 0.02),
    }

def reference(x_prompt, x_sample, cache_k_win, cache_v_win, state_C, state_n, state_m,
              rel_bias, norm_mix, w_in, b_gates, attn_sinks, norm_attn_out, norm_mlstm_out,
              w_out, norm_mlp, w_up, w_down, norm_final):
    yp, ys = x_prompt, x_sample
    Bp, S = yp.shape[:2]
    win_p = min(WINDOW, S)
    kwp, vwp, Cp_l, np_l, mp_l = [], [], [], [], []
    kws, vws, Cs_l, ns_l, ms_l = [], [], [], [], []
    for l in range(DEPTH):
        qa, ka, va, qm, km, vm, om, ig, lf = in_projection(yp, norm_mix[l], w_in[l], b_gates[l])
        att = swa_prompt(qa, ka, va, attn_sinks[l], rel_bias)
        C0 = jnp.zeros((Bp, N_HEADS_MLSTM, DK_MLSTM, DV_MLSTM), jnp.float32)
        n0 = jnp.zeros((Bp, N_HEADS_MLSTM, DK_MLSTM), jnp.float32)
        m0 = jnp.zeros((Bp, N_HEADS_MLSTM), jnp.float32)
        hm, (Cp, npv, mp) = mlstm_sequence(qm, km, vm, ig, lf, C0, n0, m0)
        yp = yp + merge_heads(att, hm, om, norm_attn_out[l], norm_mlstm_out[l], w_out[l])
        yp = yp + channel_mlp(yp, norm_mlp[l], w_up[l], w_down[l])
        kwp.append(ka[:, -win_p:])
        vwp.append(va[:, -win_p:])
        Cp_l.append(Cp)
        np_l.append(npv)
        mp_l.append(mp)
        qa, ka, va, qm, km, vm, om, ig, lf = in_projection(ys, norm_mix[l], w_in[l], b_gates[l])
        att, kw_new, vw_new = swa_sample(qa, ka, va, cache_k_win[l], cache_v_win[l], attn_sinks[l], rel_bias)
        hm, (Cs, nsv, msv) = mlstm_sequence(qm, km, vm, ig, lf, state_C[l], state_n[l], state_m[l])
        ys = ys + merge_heads(att, hm, om, norm_attn_out[l], norm_mlstm_out[l], w_out[l])
        ys = ys + channel_mlp(ys, norm_mlp[l], w_up[l], w_down[l])
        kws.append(kw_new)
        vws.append(vw_new)
        Cs_l.append(Cs)
        ns_l.append(nsv)
        ms_l.append(msv)
    y_prompt = rmsnorm(yp, norm_final)
    y_sample = rmsnorm(ys, norm_final)
    return (y_prompt, y_sample,
            jnp.stack(kwp), jnp.stack(vwp), jnp.stack(Cp_l), jnp.stack(np_l), jnp.stack(mp_l),
            jnp.stack(kws), jnp.stack(vws), jnp.stack(Cs_l), jnp.stack(ns_l), jnp.stack(ms_l))


_drawn_inputs = setup_inputs


def setup_inputs(seed=0):
    import zlib

    import numpy as np

    out = dict(_drawn_inputs(seed))
    spreads = {}
    factors = {'attn_sinks': 8.0,
     'norm_attn_out': 5.334,
     'norm_mlstm_out': 5.588,
     'norm_mlp': 3.784,
     'norm_final': 2.839}
    for name, (base, spread) in spreads.items():
        noise = np.random.default_rng([zlib.crc32(name.encode()), seed]).standard_normal(out[name].shape)
        drawn = base * np.exp(spread * noise) if base else spread * noise
        out[name] = __import__('jax').numpy.asarray(drawn.astype(out[name].dtype))
    for name, factor in factors.items():
        out[name] = (out[name] * factor).astype(out[name].dtype)
    return out
```

```python
import math
from contextlib import ExitStack

import concourse.bass as bass
from concourse import mybir

F32 = mybir.dt.float32
F32R = mybir.dt.float32r
ALU = mybir.AluOpType
ACT = mybir.ActivationFunctionType
AX_X = mybir.AxisListType.X

P = 128
D = 1024
KT = D // P
SEQ = 2048
DECB, DECT = 8, 8
NS = DECB * DECT
H, KVH, DH = 8, 2, 64
GQ = H // KVH
WIN = 128
HM, DK, DV = 4, 64, 128
FF = 4 * D
NBUCKET = 32
EPS = 1e-6
LEAST = -3e38
MASKED = -1e30

C_QA, C_KA, C_VA, C_QM, C_KM, C_VM = 0, 512, 640, 768, 1024, 1280
C_END = 2312

NQ = 4
TQ = SEQ // NQ
BLK = TQ // P
TMAX = TQ + NS

FM_TILES = [(0, 1), (2, 3), (4,), (5, 6), (7,), (8,)]
FM_COLS = [C_QA, C_QA + 256, C_KA, C_QM, C_KM, C_KM + P]
N_FM = 9
TMW = 290
N_TM, N_OP, OPW = 4, 4, 256
FC = 512
NC = FF // FC
U_F, U_T, U_O, U_M = 0, 6, 10, 14
UNITS = U_M + 4 * NC
PIECES = 2 * UNITS
RAW = 2
UNIT_BUFS = 2
WMAX = KT * TMW


def unit_of(u):
    if u < U_T:
        return "F", u, P * len(FM_TILES[u])
    if u < U_O:
        return "T", u - U_T, TMW
    if u < U_M:
        return "O", u - U_O, OPW
    return "M", u - U_M, 256


def dmas_of(u):
    return 2 if u == U_T else 1


LANDED, _n = [], [0] * RAW
for _p in range(PIECES):
    _n[_p % RAW] += dmas_of(_p // 2)
    LANDED.append(_n[_p % RAW])
LANDED_PER = list(_n)


S_IN = 16 * (1 + 16 + 3 + 4 + 32)

PER_VEC, PER_ACT = 124, 12


class Signal:

    def __init__(self, sem, per, first=0):
        self.sem, self.per, self.first = sem, per, first
        self.n = 0

    def at(self, q, n):
        v = q * self.per + n + self.first
        assert not isinstance(v, int) or v > 0
        return v

    def more(self):
        self.n += 1
        return self.n

    def next(self, q):
        return self.at(q, self.more())


def tokens_of(last):
    if last:
        return TMAX, [(j, P) for j in range(BLK)] + [(BLK, NS)], [(0, TMAX // 2), (TMAX // 2, TMAX // 2)]
    return TQ, [(j, P) for j in range(BLK)], [(0, TQ)]


MLP_HEAD = [("U", 0)]
MLP_BODY = 3
MLP_TAIL = [("U", NC - 1), ("D", NC - 2), ("D", NC - 1)]


def hymba_layer(nc, x_prompt, x_sample, cache_k_win, cache_v_win, state_C, state_n, state_m, rel_bias,
                norm_mix, w_in, b_gates, attn_sinks, norm_attn_out, norm_mlstm_out, w_out, norm_mlp,
                w_up, w_down, norm_final, c_square, c_bucket, c_sample,
                y_prompt, y_sample, kwin_prompt, vwin_prompt, C_prompt, n_prompt, m_prompt,
                kwin_sample, vwin_sample, C_sample, n_sample, m_sample):
    ctx = ExitStack()
    with ctx:
        def sb(name, shape, dt=F32, where=ctx):
            return where.enter_context(nc.sbuf_tensor(name, shape, dt))

        raw = [sb(f"w_raw{s}", [P, WMAX // 2]) for s in range(RAW)]
        w_hi = [sb(f"w_hi{b}", [P, WMAX], F32R) for b in range(UNIT_BUFS)]
        w_lo = [sb(f"w_lo{b}", [P, WMAX], F32R) for b in range(UNIT_BUFS)]
        a_hi = sb("a_hi", [P, KT, TMAX], F32R)
        a_lo = sb("a_lo", [P, KT, TMAX], F32R)
        x1 = sb("x1", [P, BLK + 1, D])
        square = sb("square", [P, 5, P])
        ident, triu, ntriu, cmask, ones = (square[:, i, :] for i in range(5))
        bias = sb("bias", [P, H, 2 * P])
        bias0 = sb("bias0", [P, H, P])
        gains = sb("gains", [P, 3, KT])
        g_final = sb("g_final", [P, D])
        nsink = sb("nsink", [P, H])
        sink = sb("sink", [P, H])
        bgate = sb("bgate", [P, 2 * HM])
        kk = sb("kk", [P, 2, P + TMAX])
        vv = sb("vv", [P, BLK + 2, KVH * DH])
        Cst = sb("Cst", [P, 2, DV + 1])
        mp = sb("mp", [HM, BLK + 1])
        wide = sb("wide", [P, H, 2 * P])
        PT = sb("PT", [P, 4, 4 * P])
        st = sb("st", [P, 160])
        rows = sb("rows", [96, BLK, P])
        kwin = sb("kwin", [P, KVH * DH])
        Mrow, grow, brow, Mswap = (wide[0:HM, 2 * i:2 * i + 2, :].rearrange("p a (b t) -> p (a b) t", t=P) for i in range(4))
        Mrel = sb("Mrel", [HM, BLK, P])
        gz = sb("gz", [P, BLK + 1, 2 * HM])
        lf = sb("lf", [P, BLK + 1, HM])
        cols = sb("cols", [P, 3, BLK, HM])
        knew = sb("knew", [NS, KVH * DH])
        ms = sb("ms", [HM, 2, DECB])
        sinkc = sb("sinkc", [P, 4])
        nsinkc = sb("nsinkc", [P, 4])
        srow = sb("srow", [HM, 5, NS])
        phase = ExitStack()
        zT = sb("zT", [P, 8, TMAX], where=phase)
        vm = sb("vm", [P, BLK + 1, HM, DV + 1], where=phase)
        om = sb("om", [P, BLK + 1, HM * DV], where=phase)
        DT = sb("DT", [P, HM, P], where=phase)
        ST = sb("ST", [P, HM, P], where=phase)
        ib = sb("ib", [P, 2, P], where=phase)
        qI = sb("qI", [P, 2, P], where=phase)
        kw = sb("kw", [P, HM, DK], where=phase)
        hm = sb("hm", [P, HM, DV], where=phase)
        og = sb("og", [P, HM, DV], where=phase)
        ogain = sb("ogain", [P, 4 * P], where=phase)
        osq = sb("osq", [P, 4 * P], where=phase)
        osum = sb("osum", [P, P], where=phase)
        phase.close()
        phase = ExitStack()
        u_hi = [sb(f"u_hi{b}", [P, 4, TMAX], F32R, phase) for b in range(2)]
        u_lo = [sb(f"u_lo{b}", [P, 4, TMAX], F32R, phase) for b in range(2)]
        relu = sb("relu", [P, 2, TMAX], where=phase)
        usq = sb("usq", [P, 2, TMAX], where=phase)
        phase.close()
        def flat(t):
            return t[(slice(None),) * len(t.shape)].rearrange("p a b c -> p (a b c)" if len(t.shape) == 4 else "p a b -> p (a b)")

        s_p = flat(wide)[:, 0:768].rearrange("p (n k) -> p n k", n=4)
        ck = flat(wide)[:, 1024:2048].rearrange("p (b c) -> p b c", b=DECB)
        s_pt = flat(PT)[:, 0:1024].rearrange("p (n k) -> p n k", n=4)
        kwm = flat(PT)[:, 1024:2048].rearrange("p (b c) -> p b c", b=4)
        s_bias = flat(bias)[:, 0:768].rearrange("p (n k) -> p n k", n=4)
        ckT = flat(bias)[:, 1024:2048].rearrange("p (b c) -> p b c", b=DECB)
        qIm = flat(bias0).rearrange("p (b i t) -> p b i t", b=DECB, i=2)
        Cs = vm[:, 0:BLK, :, :].rearrange("p j h e -> p (j h) e")
        omf = flat(om)
        cv = omf[:, 0:1024].rearrange("p (b c) -> p b c", b=DECB)
        qs = omf[:, 1024:1280].rearrange("p (b h t) -> p b h t", b=DECB, h=GQ)
        osn = omf[:, 1280:1536]
        osg = omf[:, 1536:1792].rearrange("p (h t) -> p h t", h=GQ)
        smask = omf[0:NS, 1792:1984].rearrange("p (n t) -> p n t", n=3)
        ofseq = omf[0:NS, 1984:1992]
        zs = slice(TQ, TMAX)
        ps = [ctx.enter_context(nc.psum_tensor(f"ps{b}", [P, 512], F32)) for b in range(8)]
        bias_dram = nc.dram_tensor("bias_rows", [H, P, 3 * P], F32, kind="Internal").ap()

        def signal(name, per, first=0):
            return Signal(ctx.enter_context(nc.semaphore(name)), per, first)

        const_in = signal("const_in", 0)
        setup = signal("setup", 0)
        bias_row = signal("bias_row", 0)
        bias_sb = signal("bias_sb", 0)
        bias_out = signal("bias_out", 0)
        bias_in = signal("bias_in", 0)
        w_landed = [signal(f"w_landed{s}", 16 * LANDED_PER[s]) for s in range(RAW)]
        w_high = signal("w_high", PIECES)
        w_split = signal("w_split", PIECES, RAW)
        x_in = [signal(f"x_in{j}", 16 * (j < BLK)) for j in range(BLK + 1)]
        ssq = signal("ssq", 3 * BLK, 1)
        var = signal("var", 3 + 2 * BLK)
        guess = signal("guess", 3 + 2 * BLK)
        normed = signal("normed", 2 * BLK)
        turned = signal("turned", 4 * BLK)
        gained = signal("gained", 6 * BLK)
        high = signal("high", 6 * BLK)
        split = signal("split", 6 * BLK)
        fm_out, fm_read = signal("fm_out", N_FM), signal("fm_read", N_FM)
        swapped = signal("swapped", 32)
        tm_out, tm_read = signal("tm_out", 4 * BLK), signal("tm_read", 4 * BLK)
        op_out, op_read = signal("op_out", 4 * BLK), signal("op_read", 4 * BLK)
        up_out, up_read = signal("up_out", 4 * NC, 1), signal("up_read", 4 * NC, 1)
        u_sq = signal("u_sq", 4 * NC)
        u_high, u_split = signal("u_high", 4 * NC), signal("u_split", 4 * NC)
        dn_out, dn_read = signal("dn_out", 2 * BLK * NC, 1), signal("dn_read", 2 * BLK * NC, 1)
        y_made = signal("y_made", BLK, 1)
        y_out = [signal(f"y_out{j}", 16 * 2, 1) for j in range(2)]
        fin_out = signal("fin_out", 0)
        f_abs, l_one, lf_ok = signal("f_abs", 1), signal("l_one", 1), signal("lf_ok", 1)
        g_rows, r_rows, g_cols, c_cols = signal("g_rows", 1), signal("r_rows", 1), signal("g_cols", 1), signal("c_cols", 3)
        sc_out, sc_read = signal("sc_out", 2 * BLK), signal("sc_read", H * BLK)
        negmax, sumexp, es_arg, es_ok = signal("negmax", BLK), signal("sumexp", H * BLK), signal("es_arg", BLK), signal("es_ok", BLK)
        p_ok = signal("p_ok", H * BLK)
        pt_out, pt_vec, pt_act = signal("pt_out", 4 * BLK), signal("pt_vec", 2 * BLK, 1), signal("pt_act", 2 * BLK, 1)
        o_out, o_sq, o_sum, o_ss = signal("o_out", BLK), signal("o_sq", BLK), signal("o_sum", BLK), signal("o_ss", BLK)
        m_out, m_add, ib_ok, d_ok = signal("m_out", BLK), signal("m_add", BLK), signal("ib_ok", BLK), signal("d_ok", BLK)
        s_out, s_ok = signal("s_out", BLK), signal("s_ok", BLK)
        k_out, kw_ok = signal("k_out", BLK), signal("kw_ok", BLK)
        qi_ok, n_out, n_read = signal("qi_ok", BLK), signal("n_out", BLK), signal("n_read", BLK)
        c_out, c_ok = signal("c_out", BLK), signal("c_ok", BLK, 1)
        e_o = signal("e_o", BLK)
        h_ok, h_sq, hn_ok, h_out = signal("h_ok", BLK), signal("h_sq", BLK), signal("hn_ok", BLK), signal("h_out", BLK)
        carried = signal("carried", 2, 1)
        (s_in, s_bias0, s_abs, s_lone, s_lf, s_rows, s_rowsok, s_rrows, s_cols, s_ccols, s_kout, s_kok, s_qin, s_sout, s_nmax, s_sum,
         s_esa, s_esok, s_mout, s_ib, s_dadd, s_d, s_tout, s_k2, s_st, s_q, s_kw, s_eo, s_h, s_hsq, s_hn, s_hout,
         s_p_ok, s_ptout, s_ptv, s_pta, s_o, s_os, s_on, s_osq, s_osum, s_oss, s_kwm, s_c, s_cok, s_new, s_res, s_nst) = (
            signal("s_" + n, 0) for n in (
                "in bias0 abs lone lf rows rowsok rrows cols ccols kout kok qin sout nmax sum "
                "esa esok mout ib dadd d tout k2 st q kw eo h hsq hn hout "
                "p_ok ptout ptv pta o os on osq osum oss kwm c cok new res nst").split())
        bias_ps, setup0, bias0_ok, vec_end = signal("bias_ps", 0), signal("setup0", 0), signal("bias0_ok", 1, 1), signal("vec_end", 0)
        kwin_ps, kwin_ok = signal("kwin_ps", 0), signal("kwin_ok", 0)
        vec = signal("vec", PER_VEC)
        act = signal("act", PER_ACT)

        bucket = bias[0:NBUCKET + 1, 0:2, :].rearrange("p a b -> p (a b)")[:, 0:3 * P]
        bias_by_distance = bias[0:H, 2:4, :].rearrange("p a b -> p (a b)")[:, 0:3 * P]
        rel_rows = bias[0:NBUCKET + 1, 4, 0:H]

        def unit_shape(u):
            kind, i, w = unit_of(u)
            return (4, 512) if kind == "M" and mlp_unit(i)[0] == "D" else (KT, w)

        def mlp_unit(m):
            order = MLP_HEAD + [(k, c) for i in range(MLP_BODY) for k, c in (("U", 2 * i + 1), ("D", 2 * i), ("U", 2 * i + 2), ("D", 2 * i + 1))] + MLP_TAIL
            kind, c = order[m // 2]
            return kind, c, m % 2

        chunk_parity = {}
        kinds = MLP_HEAD + [(k, c) for i in range(MLP_BODY) for k, c in (("U", 2 * i + 1), ("D", 2 * i), ("U", 2 * i + 2), ("D", 2 * i + 1))] + MLP_TAIL
        for n, (kind, c) in enumerate(kinds):
            chunk_parity[U_M + 2 * n] = chunk_parity[U_M + 2 * n + 1] = c % 2

        block = ctx.enter_context(nc.Block())

        def give_first(eng, *signals):
            for sig in signals:
                eng.sem_inc(sig.sem, sig.first)

        @block.sync
        def _(sp):
            for dst, src in ((square[:, :, :], c_square),                              (bias[0:NBUCKET, 4, 0:H], rel_bias), (bucket, c_bucket),
                             (g_final[:, :], norm_final.partition_broadcast(P)),
                             (sink[:, :], attn_sinks[0, :].partition_broadcast(P)),
                             (bgate[:, :], b_gates[0, :].partition_broadcast(P))):
                sp.dma_start(dst, src).then_inc(const_in.sem, 16)
            with nc.allow_non_contiguous_dma("a few gains, one element a row"):
                for dst, g in ((gains[:, 0, :], norm_mix), (gains[:, 2, :], norm_mlp), (gains[:, 1, 0:4], norm_attn_out), (gains[:, 1, 4:8], norm_mlstm_out)):
                    sp.dma_start(dst, g[0, :].rearrange("(k p) -> p k", p=P)).then_inc(const_in.sem, 16)
            def load(q, p, src, shift=0):
                s = p % RAW
                sp.wait_ge(w_split.sem, w_split.at(q, p + 1 - RAW + shift))
                n = src.shape[1] * src.shape[2]
                dst = raw[s][:, 0:n].rearrange("p (a b) -> p a b", b=src.shape[2])
                sp.dma_start(dst, src).then_inc(w_landed[s].sem, 16)

            def mlp_piece(q, p, kind, c, half, k, shift=0):
                if kind == "U":
                    src = w_up[0, k * 512:(k + 1) * 512, bass.ds(c * FC + half * 256, 256)].rearrange("(a p) n -> p a n", p=P)
                else:
                    src = w_down[0, bass.ds(c * FC + k * 256, 256), half * 512:(half + 1) * 512].rearrange("(a p) n -> p a n", p=P)
                load(q, p, src, shift)

            def quarter(q):
                for u in range(U_M):
                    kind, i, w = unit_of(u)
                    for k in range(2):
                        p = 2 * u + k
                        r = slice(k * 512, (k + 1) * 512)
                        if kind == "F":
                            src = w_in[0, r, FM_COLS[i]:FM_COLS[i] + w]
                        elif kind == "O":
                            src = w_out[0, r, i * OPW:(i + 1) * OPW]
                        elif i:
                            c = C_VM + i * TMW - P
                            src = w_in[0, r, c:c + TMW]
                        else:
                            s = p % RAW
                            sp.wait_ge(w_split.sem, w_split.at(q, p + 1 - RAW))
                            dst = raw[s][:, 0:4 * TMW].rearrange("p (a b) -> p a b", b=TMW)
                            for a, b, c in ((0, P, C_VA), (P, TMW, C_VM)):
                                sp.dma_start(dst[:, :, a:b], w_in[0, r, c:c + b - a].rearrange("(a p) n -> p a n", p=P)).then_inc(w_landed[s].sem, 16)
                            continue
                        load(q, p, src.rearrange("(a p) n -> p a n", p=P))
                p = 2 * U_M
                for m in range(2):
                    for k in range(2):
                        mlp_piece(q, p, "U", 0, m, k)
                        p += 1
                with sp.Fori(0, MLP_BODY) as i:
                    at = p
                    for kind, c in (("U", 2 * i + 1), ("D", 2 * i), ("U", 2 * i + 2), ("D", 2 * i + 1)):
                        for half in range(2):
                            for k in range(2):
                                mlp_piece(q, at, kind, c, half, k, 16 * i)
                                at += 1
                p += 16 * MLP_BODY
                for kind, c in MLP_TAIL:
                    for half in range(2):
                        for k in range(2):
                            mlp_piece(q, p, kind, c, half, k)
                            p += 1

            with sp.Fori(0, NQ - 1) as q:
                quarter(q)
            quarter(NQ - 1)

        def split_len(u):
            a, b = unit_shape(u)
            return a * b // 2

        def mlp_walk(eng, q, last, step):
            u = U_M
            for kind, c in MLP_HEAD:
                for half in range(2):
                    step(kind, c, half, u, 0)
                    u += 1
            with eng.Fori(0, MLP_BODY) as i:
                v = u
                for kind, c in (("U", 2 * i + 1), ("D", 2 * i), ("U", 2 * i + 2), ("D", 2 * i + 1)):
                    for half in range(2):
                        step(kind, c, half, v, i)
                        v += 1
            u += 8 * MLP_BODY
            for kind, c in MLP_TAIL:
                for half in range(2):
                    step(kind, c, half, u, 0)
                    u += 1

        def y_tile(j):
            return wide[:, 4 * (j % 2):4 * (j % 2) + 4, :].rearrange("p a b -> p (a b)")

        def xn_tile(j):
            return y_tile(j)

        def score_at(h):
            return 2 * (h % 2) + h // GQ, (h // 2) % 2 * 2 * P

        def turned_at(b):
            return b // 2 + 2 * (b % 2)

        def tmp_tile(n):
            return PT[:, n % 2, :]

        @block.gpsimd
        def _(pool):
            pool.wait_ge(bias_sb.sem, 1)
            pool.dma_start(bias_dram, bias_by_distance.unsqueeze(1).broadcast_to([H, P, 3 * P])).then_inc(bias_out.sem, 16)
            pool.memset(bias0[:, :, :], MASKED).then_inc(setup0.sem, 1)
            pool.wait_ge(bias_out.sem, 16)
            for h in range(H):
                src = bass.AP(bias_dram.tensor, h * 3 * P * P + P - 1, [[3 * P - 1, P], [1, 2 * P]])
                pool.dma_start(bias[:, h, :], src).then_inc(bias_in.sem, 16)

            for dst, src in ((kwin_sample, cache_k_win), (vwin_sample, cache_v_win)):
                pool.dma_start(dst[0, :, 0:WIN - DECT].rearrange("b w g d -> b (w g d)"), src[0, :, DECT:WIN].rearrange("b w g d -> b (w g d)")).then_inc(fin_out.sem, 16)
            with nc.allow_non_contiguous_dma("a few values for the sample group"):
                pool.dma_start(ms[:, 0, :], state_m[0].rearrange("b h -> h b")).then_inc(s_in.sem, 16)
                for b4 in range(4):
                    for n in range(4):
                        src = bass.AP(attn_sinks.tensor, n // 2 * GQ, [[1, GQ], [0, DECT], [1, 1]])
                        pool.dma_start(sinkc[b4 * 32:(b4 + 1) * 32, n:n + 1], src).then_inc(s_in.sem, 16)
            QL = NQ - 1
            pool.wait_ge(c_ok.sem, c_ok.at(QL, BLK))
            pool.wait_ge(h_ok.sem, h_ok.at(QL, BLK))
            pool.wait_ge(pt_out.sem, pt_out.at(QL, 4 * BLK))
            pool.memset(s_bias, MASKED).then_inc(s_bias0.sem, 1)
            pool.dma_start(ck, cache_k_win[0].rearrange("b w g d -> w b (g d)")).then_inc(s_in.sem, 16)
            pool.dma_start(cv, cache_v_win[0].rearrange("b w g d -> w b (g d)")).then_inc(s_in.sem, 16)
            pool.dma_start(omf[0:NS, 1792:1992], c_sample).then_inc(s_in.sem, 16)
            with nc.allow_non_contiguous_dma("n, and short rows of the bias"):
                for par in range(2):
                    rs = slice(par * DK, (par + 1) * DK)
                    pool.dma_start(Cs[rs, :, 0:DV], state_C[0].rearrange("b h d e -> (b h) d e").rearrange("(n g) d e -> g d n e", g=2)[par]).then_inc(s_in.sem, 16)
                    pool.dma_start(Cs[rs, :, DV], state_n[0].rearrange("b h d -> (b h) d").rearrange("(n g) d -> g d n", g=2)[par]).then_inc(s_in.sem, 16)
                pool.wait_ge(s_bias0.sem, s_bias0.at(0, 1))
                W3 = 3 * P
                for g in range(KVH):
                    for half in range(2):
                        for b4 in range(4):
                            rs = slice(b4 * 32, (b4 + 1) * 32)
                            at = g * GQ * P * W3 + P - 1
                            src = bass.AP(bias_dram.tensor, at, [[P * W3, GQ], [W3 - 1, DECT], [1, P]])
                            pool.dma_start(s_bias[rs, 2 * g + half, 0:P], src).then_inc(s_in.sem, 16)
                            src = bass.AP(bias_dram.tensor, at + P, [[P * W3, GQ], [W3 - 1, DECT], [1, DECT]])
                            c = P + (half * 4 + b4) * DECT
                            pool.dma_start(s_bias[rs, 2 * g + half, c:c + DECT], src).then_inc(s_in.sem, 16)
                pool.wait_ge(s_new.sem, s_new.at(0, 1))
                for dst, src in ((kwin_sample, knew[:, :]), (vwin_sample, vv[0:NS, BLK + 1, :])):
                    pool.dma_start(dst[0, :, WIN - DECT:WIN].rearrange("b w g d -> b w (g d)"), src).then_inc(fin_out.sem, 16)
                pool.wait_ge(s_rrows.sem, s_rrows.at(0, 1))
                pool.dma_start(m_sample[0].rearrange("b h -> h b"), ms[:, 1, :]).then_inc(fin_out.sem, 16)
                pool.wait_ge(s_cok.sem, s_cok.at(0, DECB))
                for par in range(2):
                    rs = slice(par * DK, (par + 1) * DK)
                    pool.dma_start(C_sample[0].rearrange("b h d e -> (b h) d e").rearrange("(n g) d e -> g d n e", g=2)[par], Cs[rs, :, 0:DV]).then_inc(s_res.sem, 16)
                    pool.dma_start(n_sample[0].rearrange("b h d -> (b h) d").rearrange("(n g) d -> g d n", g=2)[par], Cs[rs, :, DV]).then_inc(s_res.sem, 16)
            pool.wait_ge(vec_end.sem, vec_end.at(0, 1))
            with nc.allow_non_contiguous_dma("a few state values"):
                for par in range(2):
                    rowsp = Cst[par * DK:(par + 1) * DK, :, :]
                    pool.dma_start(C_prompt[0, 0].rearrange("(i g) d e -> g d i e", g=2)[par], rowsp[:, :, 0:DV]).then_inc(fin_out.sem, 16)
                    pool.dma_start(n_prompt[0, 0].rearrange("(i g) d -> g d i", g=2)[par], rowsp[:, :, DV]).then_inc(fin_out.sem, 16)
                pool.dma_start(m_prompt[0].rearrange("a h -> h a"), mp[:, BLK:BLK + 1]).then_inc(fin_out.sem, 16)
            pool.dma_start(kwin_prompt[0, 0].rearrange("t g d -> t (g d)"), kwin[:, :]).then_inc(fin_out.sem, 16)
            pool.dma_start(vwin_prompt[0, 0].rearrange("t g d -> t (g d)"), vv[:, BLK, :]).then_inc(fin_out.sem, 16)
            pool.wait_ge(fin_out.sem, 16 * 12)
            pool.wait_ge(s_res.sem, 16 * 4)
            pool.wait_ge(y_out[0].sem, y_out[0].at(NQ - 1, 16 * 3))
            pool.wait_ge(y_out[1].sem, y_out[1].at(NQ - 1, 16 * 2))

        @block.scalar
        def _(eng):
            def unit_used(eng, q, last, u, i):
                T, tiles, splits = tokens_of(last)
                NT, NN = len(tiles), len(splits)
                kind, n, w = unit_of(u)
                if kind == "F":
                    eng.wait_ge(fm_out.sem, fm_out.at(q, NN * sum(len(t) for t in FM_TILES[:n + 1])))
                elif kind == "T":
                    eng.wait_ge(tm_out.sem, tm_out.at(q, NT * (n + 1)))
                elif kind == "O":
                    eng.wait_ge(op_out.sem, op_out.at(q, NT * (n + 1)))
                else:
                    kind, c, half = mlp_unit(n)
                    if kind == "U":
                        eng.wait_ge(up_out.sem, up_out.at(q, 4 * NN * c + 2 * NN * (half + 1) + 8 * NN * i))
                    else:
                        eng.wait_ge(dn_out.sem, dn_out.at(q, 2 * NT * c + NT * (half + 1) + 4 * NT * i))

            def split_act(eng, q, last, u, k, i=0):
                p = 2 * u + k
                n = split_len(u)
                eng.wait_ge(w_landed[p % RAW].sem, w_landed[p % RAW].at(q, 16 * LANDED[p] + 16 * 16 // RAW * i))
                if k == 0:
                    before = u - UNIT_BUFS
                    if u == 0 and not (isinstance(q, int) and q == 0):
                        unit_used(eng, q - 1, last, UNITS - 2, 0)
                    elif u == 1:
                        eng.wait_ge(dn_out.sem, dn_out.at(q, 0))
                    elif before == U_M + 1 and not isinstance(i, int):
                        unit_used(eng, q, last, before, 0)
                        eng.wait_ge(dn_out.sem, dn_out.at(q, 4 * len(tokens_of(last)[1]) * i))
                    elif u > 1:
                        unit_used(eng, q, last, before, i)
                b = u % UNIT_BUFS
                eng.activation(w_hi[b][:, k * n:(k + 1) * n], raw[p % RAW][:, 0:n], ACT.Copy).then_inc(w_high.sem, 1)

            def exp(out, in_, **kw):
                return eng.activation(out, in_, ACT.Exp, **kw)

            def guess_rsqrt(q, n, v, y):
                eng.wait_ge(var.sem, var.at(q, n))
                eng.activation(y, v, ACT.Ln).then_inc(act.sem, 1)
                t = act.more()
                eng.wait_ge(act.sem, act.at(q, t))
                exp(y, y, scale=-0.5).then_inc(guess.sem, 1)

            def high_part(q, n, dst, src):
                eng.wait_ge(gained.sem, gained.at(q, n))
                eng.activation(dst, src, ACT.Copy).then_inc(high.sem, 1)

            def norm(q, tiles, base, which):
                NT = len(tiles)
                for j, R in tiles:
                    if which == 0:
                        eng.wait_ge(x_in[j].sem, x_in[j].at(q, 16))
                    elif which == 1:
                        eng.wait_ge(op_read.sem, op_read.at(q, 4 * NT))
                    else:
                        eng.wait_ge(dn_read.sem, dn_read.at(q, 2 * NC * NT))
                    eng.wait_ge(ssq.sem, ssq.at(q, NT * which + j))
                    eng.activation(PT[0:R, 2:4, :].rearrange("p a b -> p (a b)"), x1[0:R, j, :], ACT.Square, accum_out=st[0:R, j:j + 1]).then_inc(ssq.sem, 1)
                guess_rsqrt(q, which + 1 + (2 * NT if which else 0), st[:, 8:8 + BLK + 1], st[:, 16:16 + BLK + 1])
                if which == 2:
                    return
                for m in range(2 * NT):
                    j, R = tiles[m // 2]
                    k = 4 * (m % 2)
                    high_part(q, base + m + 1, a_hi[:, k:k + 4, j * P:j * P + R], tmp_tile(m)[:, 0:4 * R].rearrange("p (k t) -> p k t", k=4))

            def quarter(q, last):
                T, tiles, splits = tokens_of(last)
                NT, NN = len(tiles), len(splits)
                act.n = 0
                for j, R in tiles:
                    src = x_sample.rearrange("b t d -> (b t) d") if j == BLK else x_prompt[0, bass.ds(q * TQ + j * P, P), :]
                    eng.wait_ge(y_made.sem, y_made.at(q, 0))
                    eng.dma_start(x1[0:R, j, :], src).then_inc(x_in[j].sem, 16)
                eng.wait_ge(up_out.sem, up_out.at(q, 0))
                norm(q, tiles, 0, 0)
                eng.wait_ge(dn_out.sem, dn_out.at(q, 0))
                o = 0
                for u in range(U_T):
                    split_act(eng, q, last, u + 1, 0)
                    split_act(eng, q, last, u + 1, 1)
                    for f in FM_TILES[u]:
                        for off, w in splits:
                            o += 1
                            eng.wait_ge(fm_out.sem, fm_out.at(q, o))
                            dst = kk[:, 0, P + off:P + off + w] if f == 4 else zT[:, f - (f > 4), off:off + w]
                            scale = 0.125 if f < 4 or f > 6 else 1.0
                            eng.activation(dst, ps[(o - 1) % 4][:, 0:w], ACT.Copy, scale=scale).then_inc(fm_read.sem, 1)
                    if 4 in FM_TILES[u]:
                        for g in range(2):
                            eng.wait_ge(fm_read.sem, fm_read.at(q, 5 * NN))
                            eng.dma_start(kk[g * DH:(g + 1) * DH, 1, P:P + T], kk[(1 - g) * DH:(2 - g) * DH, 0, P:P + T]).then_inc(swapped.sem, 16)
                for u in range(U_T, U_O):
                    split_act(eng, q, last, u + 1, 0)
                    split_act(eng, q, last, u + 1, 1)
                eng.wait_ge(f_abs.sem, f_abs.at(q, 1))
                e1 = st[:, 32:32 + BLK * HM].rearrange("p (j h) -> p j h", h=HM)
                exp(e1, lf[:, 0:BLK, :], scale=-1.0).then_inc(act.sem, 1)
                t = act.more()
                eng.wait_ge(act.sem, act.at(q, t))
                eng.activation(e1, e1, ACT.Ln, bias=1.0).then_inc(l_one.sem, 1)
                eng.wait_ge(g_cols.sem, g_cols.at(q, 1))
                gc = ps[6][:, 0:BLK * 96].rearrange("p (j r) -> p j r", r=96)
                exp(cols[:, 0, :, :], gc[:, :, 0:HM]).then_inc(c_cols.sem, 1)
                eng.activation(cols[:, 1, :, :], gc[:, :, 32:32 + HM], ACT.Copy).then_inc(c_cols.sem, 1)
                exp(cols[:, 2, :, :], gc[:, :, 64:64 + HM]).then_inc(c_cols.sem, 1)
                for j in range(BLK):
                    cs = slice(j * P, (j + 1) * P)
                    eng.wait_ge(m_out.sem, m_out.at(q, j + 1))
                    for par in range(2):
                        src = ps[4][par * DK:(par + 1) * DK, :].rearrange("p (i g t) -> p g i t", g=2, i=2)[:, par]
                        ins = exp(ib[par * DK:(par + 1) * DK, :, :], src)
                    ins.then_inc(ib_ok.sem, 1)
                    eng.wait_ge(m_add.sem, m_add.at(q, j + 1))
                    eng.wait_ge(c_cols.sem, c_cols.at(q, 3))
                    for h in range(HM):
                        ins = exp(DT[:, h, :], DT[:, h, :], bias=cols[:, 1, j, h:h + 1])
                    ins.then_inc(d_ok.sem, 1)
                    eng.wait_ge(negmax.sem, negmax.at(q, j + 1))
                    for h in range(H):
                        exp(wide[:, h, :], wide[:, h, :], bias=st[:, 64 + h:65 + h], accum_out=st[:, 72 + h:73 + h]).then_inc(sumexp.sem, 1)
                    eng.wait_ge(es_arg.sem, es_arg.at(q, j + 1))
                    exp(st[:, 80:88], st[:, 80:88]).then_inc(es_ok.sem, 1)
                    if j:
                        eng.wait_ge(h_ok.sem, h_ok.at(q, j))
                    exp(og[:, :, :].rearrange("p h e -> p (h e)"), om[:, j, :], scale=-1.0).then_inc(e_o.sem, 1)
                    eng.wait_ge(h_ok.sem, h_ok.at(q, j + 1))
                    eng.activation(og[:, :, :], hm[:, :, :], ACT.Square).then_inc(h_sq.sem, 1)
                    if j:
                        eng.wait_ge(o_out.sem, o_out.at(q, j))
                    for b in (2, 3):
                        eng.wait_ge(pt_out.sem, pt_out.at(q, 4 * j + b + 1))
                        eng.activation(PT[:, b, :], ps[turned_at(b)][:, :], ACT.Copy).then_inc(pt_act.sem, 1)
                    eng.wait_ge(o_out.sem, o_out.at(q, j + 1))
                    eng.activation(osq[:, :], ps[7][:, :], ACT.Square).then_inc(o_sq.sem, 1)
                    high_part(q, 2 * NT + 2 * j + 1, a_hi[:, 0:4, cs], ogain[:, :].rearrange("p (k t) -> p k t", k=4))
                    guess_rsqrt(q, 1 + 2 * j + 1, st[:, 96:97], st[:, 97:98])
                    guess_rsqrt(q, 1 + 2 * j + 2, st[:, 104:108], st[:, 108:112])
                    high_part(q, 2 * NT + 2 * j + 2, a_hi[:, 4:8, cs], ogain[:, :].rearrange("p (k t) -> p k t", k=4))
                if last:
                    sample_act()
                if not last:
                    eng.activation(bias0[:, :, :], bias[:, :, 0:P], ACT.Copy).then_inc(bias0_ok.sem, 1)
                    eng.activation(kk[:, :, 0:P], kk[:, :, TQ:TQ + P], ACT.Copy).then_inc(carried.sem, 1)
                    eng.activation(vv[:, 0, :], vv[:, BLK, :], ACT.Copy).then_inc(carried.sem, 1)
                for u in range(U_O, U_M):
                    split_act(eng, q, last, u + 1, 0)
                    split_act(eng, q, last, u + 1, 1)
                norm(q, tiles, 4 * NT, 1)

                def step(kind, c, half, u, i):
                    end = last and isinstance(i, int) and u == UNITS - 1
                    nq, nu = (q, u + 1) if u + 1 < UNITS else (q + 1, 0)
                    if not end:
                        split_act(eng, nq, last, nu, 0, i)
                        split_act(eng, nq, last, nu, 1, i)
                    if kind == "U":
                        b = chunk_parity[u]
                        if not (isinstance(c, int) and c < 2):
                            eng.wait_ge(dn_out.sem, dn_out.at(q, 2 * NT * (c - 1)))
                        for t in range(2):
                            for s, (off, w) in enumerate(splits):
                                l = (half * 2 + t) * NN + s
                                o = 4 * NN * c + l
                                eng.wait_ge(up_out.sem, up_out.at(q, o + 1))
                                if not (isinstance(c, int) and c == 0 and l < 2):
                                    eng.wait_ge(u_sq.sem, u_sq.at(q, o - 1))
                                    eng.wait_ge(u_high.sem, u_high.at(q, o - 1))
                                eng.activation(relu[:, l % 2, 0:w], ps[l % 4][:, 0:w], ACT.Relu).then_inc(up_read.sem, 1)
                                eng.wait_ge(up_read.sem, up_read.at(q, o + 1))
                                eng.activation(u_hi[b][:, half * 2 + t, off:off + w], relu[:, l % 2, 0:w], ACT.Square).then_inc(u_high.sem, 1)

                mlp_walk(eng, q, last, step)
                norm(q, tiles, 0, 2)
                for j, R in tiles:
                    dst = y_sample.rearrange("b t d -> (b t) d") if j == BLK else y_prompt[0, bass.ds(q * TQ + j * P, P), :]
                    eng.wait_ge(y_made.sem, y_made.at(q, j + 1))
                    eng.dma_start(dst, y_tile(j)[0:R, :]).then_inc(y_out[j % 2].sem, 16)

            def sample_act():
                q, NT, cs, j = NQ - 1, BLK + 1, zs, BLK
                eng.wait_ge(s_abs.sem, s_abs.at(0, 1))
                e1 = st[0:NS, 32:32 + HM]
                exp(e1, lf[0:NS, BLK, :], scale=-1.0).then_inc(act.sem, 1)
                t = act.more()
                eng.wait_ge(act.sem, act.at(q, t))
                eng.activation(e1, e1, ACT.Ln, bias=1.0).then_inc(s_lone.sem, 1)
                eng.wait_ge(s_in.sem, s_in.at(0, S_IN))
                for h in range(H):
                    g, par = h // GQ, h % 2
                    eng.dma_start(qs[g * DH:(g + 1) * DH, :, h % GQ, :], zT[par * DH:(par + 1) * DH, h // 2, zs].rearrange("p (b t) -> p b t", b=DECB)).then_inc(s_qin.sem, 16)
                eng.wait_ge(s_kout.sem, s_kout.at(0, 1))
                for b in range(2):
                    ins = eng.activation(ckT[:, 4 * b:4 * b + 4, :].rearrange("p b c -> p (b c)"), ps[b][:, :], ACT.Copy)
                ins.then_inc(s_kok.sem, 1)
                eng.wait_ge(s_cols.sem, s_cols.at(0, 1))
                gc = ps[6][0:NS, 0:96]
                exp(cols[0:NS, 0, 0, :], gc[:, 0:HM]).then_inc(s_ccols.sem, 1)
                eng.activation(cols[0:NS, 1, 0, :], gc[:, 32:32 + HM], ACT.Copy).then_inc(s_ccols.sem, 1)
                exp(cols[0:NS, 2, 0, :], gc[:, 64:64 + HM]).then_inc(s_ccols.sem, 1)
                eng.wait_ge(s_mout.sem, s_mout.at(0, 1))
                for par in range(2):
                    rs = slice(par * DK, (par + 1) * DK)
                    ins = exp(ib[rs, :, 0:NS], ps[4][rs, 0:HM * NS].rearrange("p (i g t) -> p g i t", g=2, i=2)[:, par])
                ins.then_inc(s_ib.sem, 1)
                eng.wait_ge(s_dadd.sem, s_dadd.at(0, 1))
                eng.wait_ge(s_ccols.sem, s_ccols.at(0, 3))
                for h in range(HM):
                    ins = exp(DT[0:NS, h, 0:NS], DT[0:NS, h, 0:NS], bias=cols[0:NS, 1, 0, h:h + 1])
                ins.then_inc(s_d.sem, 1)
                eng.wait_ge(s_nmax.sem, s_nmax.at(0, 1))
                for n in range(4):
                    exp(s_p[:, n, :], s_p[:, n, :], bias=st[:, 64 + n:65 + n], accum_out=st[:, 72 + n:73 + n]).then_inc(s_sum.sem, 1)
                eng.wait_ge(s_esa.sem, s_esa.at(0, 1))
                exp(st[:, 80:84], st[:, 80:84]).then_inc(s_esok.sem, 1)
                exp(og[0:NS, :, :].rearrange("p h e -> p (h e)"), om[0:NS, BLK, :], scale=-1.0).then_inc(s_eo.sem, 1)
                eng.wait_ge(s_ptout.sem, s_ptout.at(0, 2))
                pv = ps[1][:, :].rearrange("p (n k) -> p n k", n=2)
                eng.activation(s_pt[:, 2:4, 0:P], pv[:, :, 0:P], ACT.Copy)
                eng.activation(s_pt[0:NS, 2:4, P:2 * P], pv[0:NS, :, P:2 * P], ACT.Copy).then_inc(s_pta.sem, 1)
                eng.wait_ge(s_h.sem, s_h.at(0, 1))
                eng.activation(og[0:NS, :, :], hm[0:NS, :, :], ACT.Square).then_inc(s_hsq.sem, 1)
                eng.wait_ge(s_os.sem, s_os.at(0, 1))
                for h in range(H):
                    g, par = h // GQ, h % 2
                    eng.dma_start(osn[par * DH:(par + 1) * DH, (h // 2) * NS:(h // 2 + 1) * NS], osg[g * DH:(g + 1) * DH, h % GQ, :]).then_inc(s_on.sem, 16)
                eng.wait_ge(s_on.sem, s_on.at(0, 16 * H))
                eng.activation(osq[:, 0:4 * NS], osn[:, :], ACT.Square).then_inc(s_osq.sem, 1)
                high_part(q, 2 * NT + 2 * j + 1, a_hi[:, 0:4, cs], ogain[:, 0:4 * NS].rearrange("p (k t) -> p k t", k=4))
                guess_rsqrt(q, 1 + 2 * j + 1, st[0:NS, 96:97], st[0:NS, 97:98])
                guess_rsqrt(q, 1 + 2 * j + 2, st[0:NS, 104:108], st[0:NS, 108:112])
                high_part(q, 2 * NT + 2 * j + 2, a_hi[:, 4:8, cs], ogain[:, 0:4 * NS].rearrange("p (k t) -> p k t", k=4))
                eng.wait_ge(s_res.sem, s_res.at(0, 16 * 4))

            give_first(eng, ssq, up_read, pt_act, carried, bias0_ok, *y_out)
            split_act(eng, 0, False, 0, 0)
            split_act(eng, 0, False, 0, 1)
            eng.wait_ge(setup.sem, setup.at(0, 9))
            with eng.Fori(0, NQ - 1) as q:
                quarter(q, False)
            assert act.n == act.per
            quarter(NQ - 1, True)


        @block.vector
        def _(eng):
            def split_vec(eng, q, u, k, i=0):
                p = 2 * u + k
                n = split_len(u)
                b = u % UNIT_BUFS
                eng.wait_ge(w_high.sem, w_high.at(q, p + 1 + 16 * i))
                eng.tensor_tensor(w_lo[b][:, k * n:(k + 1) * n], raw[p % RAW][:, 0:n],
                                             w_hi[b][:, k * n:(k + 1) * n].bitcast(F32), ALU.subtract).then_inc(w_split.sem, 1)

            def tt(out, a, b, op):
                return eng.tensor_tensor(out, a, b, op)

            def refine(q, n, v, y, out, tmp):
                eng.wait_ge(guess.sem, guess.at(q, n))
                tt(tmp, y, y, ALU.mult).then_inc(vec.sem, 1)
                eng.wait_ge(vec.sem, vec.next(q))
                tt(tmp, tmp, v, ALU.mult).then_inc(vec.sem, 1)
                eng.wait_ge(vec.sem, vec.next(q))
                eng.tensor_scalar(tmp, tmp, -0.5, 1.5, ALU.mult, ALU.add).then_inc(vec.sem, 1)
                eng.wait_ge(vec.sem, vec.next(q))
                tt(out, y, tmp, ALU.mult).then_inc(vec.sem, 1)
                eng.wait_ge(vec.sem, vec.next(q))

            def low_part(q, n, dst, src, hi):
                eng.wait_ge(high.sem, high.at(q, n))
                tt(dst, src, hi.bitcast(F32), ALU.subtract).then_inc(split.sem, 1)

            def norm(q, tiles, base, which):
                NT = len(tiles)
                eng.wait_ge(ssq.sem, ssq.at(q, NT * (which + 1)))
                eng.tensor_scalar(st[:, 8:8 + BLK + 1], st[:, 0:BLK + 1], 1.0 / D, EPS, ALU.mult, ALU.add).then_inc(var.sem, 1)
                n = which + 1 + (2 * NT if which else 0)
                eng.wait_ge(var.sem, var.at(q, n))
                refine(q, n, st[:, 8:8 + BLK + 1], st[:, 16:16 + BLK + 1], st[:, 132:132 + BLK + 1], st[:, 140:140 + BLK + 1])
                if which == 2:
                    for j, R in tiles:
                        eng.wait_ge(y_out[j % 2].sem, y_out[j % 2].at(q, 16 * (j // 2)))
                        eng.scalar_tensor_tensor(y_tile(j)[0:R, :], x1[0:R, j, :], st[0:R, 132 + j:133 + j], g_final[0:R, :], ALU.mult, ALU.mult).then_inc(y_made.sem, 1)
                    return

                def rows_normed(j, R):
                    if j >= 2:
                        eng.wait_ge(turned.sem, turned.at(q, (2 * NT if which else 0) + 2 * (j - 1)))
                    eng.tensor_scalar(xn_tile(j)[0:R, :], x1[0:R, j, :], st[0:R, 132 + j:133 + j], None, ALU.mult).then_inc(normed.sem, 1)

                def low(m):
                    j, R = tiles[m // 2]
                    k = 4 * (m % 2)
                    s = slice(j * P, j * P + R)
                    low_part(q, base + m + 1, a_lo[:, k:k + 4, s], tmp_tile(m)[:, 0:4 * R].rearrange("p (k t) -> p k t", k=4), a_hi[:, k:k + 4, s])

                if which == 0:
                    eng.wait_ge(y_out[0].sem, y_out[0].at(q, 0))
                    eng.wait_ge(y_out[1].sem, y_out[1].at(q, 0))
                rows_normed(*tiles[0])
                rows_normed(*tiles[1])
                for m in range(2 * NT):
                    j, R = tiles[m // 2]
                    k = 4 * (m % 2)
                    eng.wait_ge(turned.sem, turned.at(q, (2 * NT if which else 0) + m + 1))
                    b = 4 + m % 4
                    gain = gains[:, 2 if which else 0, k:k + 4].unsqueeze(2).broadcast_to([P, 4, R])
                    if m >= 2:
                        eng.wait_ge(split.sem, split.at(q, base + m - 1))
                    tt(tmp_tile(m)[:, 0:4 * R].rearrange("p (k t) -> p k t", k=4), ps[b][:, 0:4 * R].rearrange("p (k t) -> p k t", k=4), gain, ALU.mult).then_inc(gained.sem, 1)
                    if m:
                        low(m - 1)
                    if m % 2 and m // 2 + 2 < NT:
                        rows_normed(*tiles[m // 2 + 2])
                low(2 * NT - 1)

            def tm_parts(i):
                a, b = i * TMW, (i + 1) * TMW
                ends = [(0, P, lambda j, s: vv[:, j + 1, s])]
                for h in range(HM):
                    ends.append((P * (h + 1), P * (h + 2), lambda j, s, h=h: vm[:, j, h, s]))
                ends += [(640, 1152, lambda j, s: om[:, j, s]), (1152, 1160, lambda j, s: gz[:, j, s])]
                for lo, hi, dst in ends:
                    if max(a, lo) < min(b, hi):
                        yield max(a, lo) - a, min(b, hi) - a, slice(max(a, lo) - lo, min(b, hi) - lo), dst

            def gates(q, R, tiles, n, w, buffers, absd, l_one, lf_ok, g_rows):
                nt = tiles.stop - tiles.start
                tt(gz[0:R, tiles, :], gz[0:R, tiles, :], bgate[0:R, :].unsqueeze(1).broadcast_to([R, nt, 2 * HM]), ALU.add).then_inc(vec.sem, 1)
                eng.wait_ge(vec.sem, vec.next(q))
                f = gz[0:R, tiles, HM:2 * HM]
                eng.scalar_tensor_tensor(lf[0:R, tiles, :], f, -1.0, f, ALU.mult, ALU.max).then_inc(absd.sem, 1)
                eng.wait_ge(l_one.sem, l_one.at(q, 1))
                e1 = st[0:R, 32:32 + nt * HM].rearrange("p (j h) -> p j h", h=HM)
                eng.scalar_tensor_tensor(lf[0:R, tiles, :], f, 0.0, e1, ALU.min, ALU.subtract).then_inc(lf_ok.sem, 1)
                eng.wait_ge(g_rows.sem, g_rows.at(q, 1))
                Mrow, grow, brow, Mswap = buffers
                eng.tensor_copy(grow, ps[4][0:HM, 0:n * w].rearrange("p (j t) -> p j t", j=n)).then_inc(vec.sem, 1)
                eng.wait_ge(vec.sem, vec.next(q))
                eng.tensor_copy(brow, ps[5][0:HM, 0:n * w].rearrange("p (j t) -> p j t", j=n)).then_inc(vec.sem, 1)
                eng.wait_ge(vec.sem, vec.next(q))
                src = grow
                for r in range(w.bit_length() - 1):
                    s, dst = 1 << r, (Mrow, Mswap)[r % 2]
                    eng.tensor_copy(dst[:, :, 0:s], src[:, :, 0:s])
                    tt(dst[:, :, s:w], src[:, :, s:w], src[:, :, 0:w - s], ALU.max).then_inc(vec.sem, 1)
                    eng.wait_ge(vec.sem, vec.next(q))
                    src = dst

            def stabilise(q, n, w, before, buffers, rel, out, ready):
                Mrow, grow, brow, _ = buffers
                tt(Mrow, Mrow, before, ALU.max).then_inc(vec.sem, 1)
                eng.wait_ge(vec.sem, vec.next(q))
                tt(rel, before, Mrow, ALU.subtract).then_inc(vec.sem, 1)
                eng.wait_ge(vec.sem, vec.next(q))
                eng.scalar_tensor_tensor(out(0), Mrow, -1.0, brow, ALU.mult, ALU.subtract).then_inc(vec.sem, 1)
                eng.wait_ge(vec.sem, vec.next(q))
                tt(out(32), grow, before, ALU.subtract).then_inc(vec.sem, 1)
                eng.wait_ge(vec.sem, vec.next(q))
                tt(out(64), grow, Mrow[:, :, w - 1:w].broadcast_to([HM, n, w]), ALU.subtract).then_inc(ready.sem, 1)

            def prompt_gates(q):
                buffers = (Mrow, grow, brow, Mswap)
                gates(q, P, slice(0, BLK), BLK, P, buffers, f_abs, l_one, lf_ok, g_rows)
                eng.tensor_copy(mp[:, 0:1], mp[:, BLK:BLK + 1]).then_inc(vec.sem, 1)
                eng.wait_ge(vec.sem, vec.next(q))
                for j in range(BLK):
                    eng.scalar_tensor_tensor(mp[:, j + 1:j + 2], Mrow[:, j, P - 1:P], mp[:, j:j + 1], brow[:, j, P - 1:P], ALU.max, ALU.add).then_inc(vec.sem, 1)
                    eng.wait_ge(vec.sem, vec.next(q))
                stabilise(q, BLK, P, mp[:, 0:BLK].unsqueeze(2).broadcast_to([HM, BLK, P]), buffers, Mrel[:, :, :], lambda r: rows[r:r + HM, :, :], r_rows)

            def sample_vec():
                q, NT, cs, j, n, w = NQ - 1, BLK + 1, zs, BLK, DECB, DECT
                by_seq = lambda t: t.rearrange("p (b t) -> p b t", b=DECB)
                buffers = tuple(by_seq(srow[:, i, :]) for i in range(4))
                eng.wait_ge(s_in.sem, s_in.at(0, S_IN))
                gates(q, NS, slice(BLK, BLK + 1), n, w, buffers, s_abs, s_lone, s_lf, s_rows)
                before = ms[:, 0, :].unsqueeze(2).broadcast_to([HM, n, w])
                stabilise(q, n, w, before, buffers, by_seq(srow[:, 4, :]), lambda r: by_seq(rows[r:r + HM, 0, 0:NS]), s_rowsok)
                eng.memset(qIm, 0.0).then_inc(vec.sem, 1)
                eng.wait_ge(vec.sem, vec.next(q))
                tt(ms[:, 1, :], buffers[0][:, :, w - 1], buffers[2][:, :, w - 1], ALU.add).then_inc(s_rrows.sem, 1)
                eng.tensor_scalar(nsinkc[:, :], sinkc[:, :], -1.0, None, ALU.mult).then_inc(vec.sem, 1)
                eng.wait_ge(vec.sem, vec.next(q))
                eng.wait_ge(s_sout.sem, s_sout.at(0, 1))
                for m in range(4):
                    eng.tensor_tensor_reduce(s_p[:, m, :], ps[m][:, 0:192], s_bias[:, m, :], 1.0, LEAST, ALU.add, ALU.max, st[:, 124 + m:125 + m]).then_inc(vec.sem, 1)
                    t = vec.more()
                eng.wait_ge(vec.sem, vec.at(q, t))
                eng.scalar_tensor_tensor(st[:, 64:68], st[:, 124:128], -1.0, nsinkc[:, :], ALU.mult, ALU.min).then_inc(s_nmax.sem, 1)
                eng.wait_ge(s_nmax.sem, s_nmax.at(0, 1))
                tt(st[:, 80:84], st[:, 64:68], sinkc[:, :], ALU.add).then_inc(s_esa.sem, 1)
                eng.wait_ge(s_ib.sem, s_ib.at(0, 1))
                tt(DT[0:NS, :, 0:NS], ps[4][0:NS, 0:HM * NS].rearrange("p (h t) -> p h t", h=HM), smask[:, 0, :].unsqueeze(1).broadcast_to([NS, HM, NS]), ALU.add).then_inc(s_dadd.sem, 1)
                eng.wait_ge(s_k2.sem, s_k2.at(0, 1))
                eng.wait_ge(s_ccols.sem, s_ccols.at(0, 3))
                tt(kw[0:NS, :, :], ps[6][0:NS, 128:384].rearrange("p (h d) -> p h d", h=HM), cols[0:NS, 2, 0, :].unsqueeze(2).broadcast_to([NS, HM, DK]), ALU.mult).then_inc(s_kw.sem, 1)
                eng.tensor_copy(knew[:, :], ps[6][0:NS, 384:512]).then_inc(s_new.sem, 1)
                tt(qI[:, :, 0:NS], zT[:, 4:6, zs], ib[:, :, 0:NS], ALU.mult).then_inc(vec.sem, 1)
                eng.wait_ge(vec.sem, vec.next(q))
                for b in range(DECB):
                    c = slice(b * DECT, (b + 1) * DECT)
                    ins = eng.tensor_copy(qIm[:, b, :, c], qI[:, :, c])
                ins.then_inc(s_q.sem, 1)
                eng.wait_ge(s_tout.sem, s_tout.at(0, 1))
                eng.wait_ge(s_d.sem, s_d.at(0, 1))
                for par in range(2):
                    own = lambda t: t[0:NS, :, 0:NS].rearrange("p (i r) t -> p r i t", r=2)[:, par]
                    ins = tt(own(ST), ps[5 + 2 * par][0:NS, 0:2 * NS].rearrange("p (i t) -> p i t", i=2), own(DT), ALU.mult)
                ins.then_inc(s_st.sem, 1)
                eng.wait_ge(s_esok.sem, s_esok.at(0, 1))
                eng.wait_ge(s_sum.sem, s_sum.at(0, 4))
                tt(st[:, 88:92], st[:, 72:76], st[:, 80:84], ALU.add).then_inc(vec.sem, 1)
                eng.wait_ge(vec.sem, vec.next(q))
                eng.reciprocal(st[:, 88:92], st[:, 88:92]).then_inc(vec.sem, 1)
                eng.wait_ge(vec.sem, vec.next(q))
                for m in range(4):
                    eng.tensor_scalar(s_p[:, m, :], s_p[:, m, :], st[:, 88 + m:89 + m], None, ALU.mult).then_inc(s_p_ok.sem, 1)
                eng.wait_ge(s_kw.sem, s_kw.at(0, 1))
                kwf = kw[0:NS, :, :].rearrange("p h d -> p (h d)")
                for b in range(4):
                    eng.tensor_scalar(kwm[0:NS, b, :], kwf, ofseq[:, b:b + 1], None, ALU.mult).then_inc(s_kwm.sem, 1)
                eng.wait_ge(s_ptout.sem, s_ptout.at(0, 1))
                pv = ps[0][:, :].rearrange("p (n k) -> p n k", n=2)
                eng.tensor_copy(s_pt[:, 0:2, 0:P], pv[:, :, 0:P])
                eng.tensor_copy(s_pt[0:NS, 0:2, P:2 * P], pv[0:NS, :, P:2 * P]).then_inc(s_ptv.sem, 1)
                eng.wait_ge(s_nst.sem, s_nst.at(0, 4))
                num = [ps[4 + b][0:NS, 0:2 * (DV + 1)].rearrange("p (h e) -> p h e", h=2) for b in range(2)]
                for b in range(2):
                    tt(st[0:NS, 112 + b:116:2], num[b][:, :, DV], cols[0:NS, 0, 0, b:HM:2], ALU.max).then_inc(vec.sem, 1)
                    t = vec.more()
                eng.wait_ge(vec.sem, vec.at(q, t))
                for b in range(2):
                    eng.scalar_tensor_tensor(st[0:NS, 112 + b:116:2], num[b][:, :, DV], -1.0, st[0:NS, 112 + b:116:2], ALU.mult, ALU.max).then_inc(vec.sem, 1)
                    t = vec.more()
                eng.wait_ge(vec.sem, vec.at(q, t))
                eng.wait_ge(s_eo.sem, s_eo.at(0, 1))
                eng.scalar_tensor_tensor(og[0:NS, :, :], og[0:NS, :, :], 1.0, st[0:NS, 112:116].unsqueeze(2).broadcast_to([NS, HM, DV]), ALU.add, ALU.mult).then_inc(vec.sem, 1)
                eng.wait_ge(vec.sem, vec.next(q))
                eng.reciprocal(og[0:NS, :, :], og[0:NS, :, :]).then_inc(vec.sem, 1)
                eng.wait_ge(vec.sem, vec.next(q))
                for b in range(2):
                    ins = tt(hm[0:NS, b:HM:2, :], num[b][:, :, 0:DV], og[0:NS, b:HM:2, :], ALU.mult)
                ins.then_inc(s_h.sem, 1)
                eng.wait_ge(s_o.sem, s_o.at(0, 1))
                eng.tensor_copy(osg.rearrange("p h (b t) -> p b h t", b=DECB), ps[7][:, 0:4 * NS].rearrange("p (b h t) -> p b h t", b=DECB, h=GQ)).then_inc(s_os.sem, 1)
                for b in range(DECB):
                    if b == 4:
                        for m in range(4):
                            eng.tensor_scalar(kwm[0:NS, m, :], kwf, ofseq[:, 4 + m:5 + m], None, ALU.mult).then_inc(s_kwm.sem, 1)
                    eng.wait_ge(s_c.sem, s_c.at(0, b + 1))
                    for i in range(2):
                        ins = eng.scalar_tensor_tensor(Cs[:, 2 * b + i, :], Cs[:, 2 * b + i, :], ib[:, i, b * DECT + DECT - 1:b * DECT + DECT], ps[b % 4][:, i * (DV + 1):(i + 1) * (DV + 1)], ALU.mult, ALU.add)
                    ins.then_inc(s_cok.sem, 1)
                eng.wait_ge(s_hsq.sem, s_hsq.at(0, 1))
                eng.tensor_reduce(st[0:NS, 100:104], og[0:NS, :, :], AX_X, ALU.add).then_inc(vec.sem, 1)
                eng.wait_ge(vec.sem, vec.next(q))
                eng.wait_ge(s_osq.sem, s_osq.at(0, 1))
                eng.tensor_reduce(osum[:, 0:NS], osq[:, 0:4 * NS].rearrange("p (i t) -> p t i", i=4), AX_X, ALU.add).then_inc(s_osum.sem, 1)
                og4 = ogain[:, 0:4 * NS].rearrange("p (k t) -> p k t", k=4)
                tt(og4, osn.rearrange("p (i t) -> p i t", i=4), gains[:, 1, 0:4].unsqueeze(2).broadcast_to([P, 4, NS]), ALU.mult).then_inc(gained.sem, 1)
                eng.wait_ge(s_oss.sem, s_oss.at(0, 1))
                m = 1 + 2 * j
                eng.tensor_scalar(st[0:NS, 96:97], ps[6][0:NS, 0:1], 1.0 / (H * DH), EPS, ALU.mult, ALU.add).then_inc(var.sem, 1)
                eng.wait_ge(var.sem, var.at(q, m + 1))
                refine(q, m + 1, st[0:NS, 96:97], st[0:NS, 97:98], st[0:NS, 24 + j:25 + j], st[0:NS, 98:99])
                eng.tensor_scalar(st[0:NS, 104:108], st[0:NS, 100:104], 1.0 / DV, EPS, ALU.mult, ALU.add).then_inc(var.sem, 1)
                low_part(q, 2 * NT + 2 * j + 1, a_lo[:, 0:4, cs], og4, a_hi[:, 0:4, cs])
                eng.wait_ge(split.sem, split.at(q, 2 * NT + 2 * j + 1))
                eng.wait_ge(var.sem, var.at(q, m + 2))
                refine(q, m + 2, st[0:NS, 104:108], st[0:NS, 108:112], st[0:NS, 108:112], st[0:NS, 140:144])
                tt(hm[0:NS, :, :], hm[0:NS, :, :], st[0:NS, 108:112].unsqueeze(2).broadcast_to([NS, HM, DV]), ALU.mult).then_inc(s_hn.sem, 1)
                eng.wait_ge(s_hout.sem, s_hout.at(0, 1))
                tt(og4, ps[4][:, 0:4 * NS].rearrange("p (k t) -> p k t", k=4), gains[:, 1, 4:8].unsqueeze(2).broadcast_to([P, 4, NS]), ALU.mult).then_inc(gained.sem, 1)
                eng.wait_ge(gained.sem, gained.at(q, 2 * NT + 2 * j + 2))
                low_part(q, 2 * NT + 2 * j + 2, a_lo[:, 4:8, cs], og4, a_hi[:, 4:8, cs])

            def mix_block(q, NT, j):
                cs = slice(j * P, (j + 1) * P)
                if j:
                    eng.wait_ge(pt_out.sem, pt_out.at(q, 4 * j))
                for h in range(H):
                    if h % GQ == 0:
                        eng.wait_ge(sc_out.sem, sc_out.at(q, 2 * j + h // GQ + 1))
                        eng.memset(st[:, 152 + h // GQ:153 + h // GQ], 0.0)
                    mx, (b, at) = st[:, 124 + h:125 + h], score_at(h)
                    if j:
                        eng.tensor_tensor_reduce(wide[:, h, :], ps[b][:, at:at + 2 * P], bias[:, h, :], 1.0, LEAST, ALU.add, ALU.max, mx).then_inc(sc_read.sem, 1)
                    else:
                        eng.tensor_tensor_reduce(wide[:, h, 0:P], ps[b][:, at:at + P], bias0[:, h, :], 1.0, LEAST, ALU.add, ALU.max, mx).then_inc(vec.sem, 1)
                        eng.wait_ge(vec.sem, vec.next(q))
                        eng.memset(st[:, 144 + h:145 + h], 0.0)
                        eng.tensor_tensor_reduce(wide[:, h, P:2 * P], ps[b][:, at + P:at + 2 * P], bias[:, h, P:2 * P], 1.0, mx, ALU.add, ALU.max, mx).then_inc(sc_read.sem, 1)
                eng.wait_ge(m_out.sem, m_out.at(q, j + 1))
                eng.wait_ge(ib_ok.sem, ib_ok.at(q, j + 1))
                tt(DT[:, :, :], ps[4][:, :].rearrange("p (h t) -> p h t", h=HM), cmask.unsqueeze(1).broadcast_to([P, HM, P]), ALU.add).then_inc(m_add.sem, 1)
                eng.wait_ge(sc_read.sem, sc_read.at(q, H * (j + 1)))
                eng.scalar_tensor_tensor(st[:, 64:72], st[:, 124:132], -1.0, nsink[:, :], ALU.mult, ALU.min).then_inc(negmax.sem, 1)
                eng.wait_ge(negmax.sem, negmax.at(q, j + 1))
                tt(st[:, 80:88], st[:, 64:72], sink[:, :], ALU.add).then_inc(es_arg.sem, 1)
                eng.wait_ge(k_out.sem, k_out.at(q, j + 1))
                eng.wait_ge(c_cols.sem, c_cols.at(q, 3))
                tt(kw[:, :, :], ps[6][:, 0:HM * DK].rearrange("p (h d) -> p h d", h=HM), cols[:, 2, j, :].unsqueeze(2).broadcast_to([P, HM, DK]), ALU.mult).then_inc(kw_ok.sem, 1)
                eng.wait_ge(ib_ok.sem, ib_ok.at(q, j + 1))
                tt(qI[:, :, :], zT[:, 4:6, cs], ib[:, :, :], ALU.mult).then_inc(qi_ok.sem, 1)
                eng.wait_ge(s_out.sem, s_out.at(q, j + 1))
                eng.wait_ge(d_ok.sem, d_ok.at(q, j + 1))
                for par in range(2):
                    own = lambda t: t[:, :, :].rearrange("p (i r) t -> p r i t", r=2)[:, par]
                    ins = tt(own(ST), ps[5 + 2 * par][:, 0:2 * P].rearrange("p (i t) -> p i t", i=2), own(DT), ALU.mult)
                ins.then_inc(s_ok.sem, 1)
                eng.wait_ge(es_ok.sem, es_ok.at(q, j + 1))
                eng.wait_ge(sumexp.sem, sumexp.at(q, H * (j + 1)))
                tt(st[:, 88:96], st[:, 72:80], st[:, 80:88], ALU.add).then_inc(vec.sem, 1)
                eng.wait_ge(vec.sem, vec.next(q))
                eng.reciprocal(st[:, 88:96], st[:, 88:96]).then_inc(vec.sem, 1)
                eng.wait_ge(vec.sem, vec.next(q))
                for h in range(H):
                    eng.tensor_scalar(wide[:, h, :], wide[:, h, :], st[:, 88 + h:89 + h], None, ALU.mult).then_inc(p_ok.sem, 1)
                eng.wait_ge(n_out.sem, n_out.at(q, j + 1))
                eng.wait_ge(c_out.sem, c_out.at(q, j + 1))
                for i in range(2):
                    ins = eng.scalar_tensor_tensor(Cst[:, i, :], Cst[:, i, :], ib[:, i, P - 1:P], ps[6][:, i * (DV + 1):(i + 1) * (DV + 1)], ALU.mult, ALU.add)
                ins.then_inc(c_ok.sem, 1)
                num = [ps[4 + b][:, 0:2 * (DV + 1)].rearrange("p (h e) -> p h e", h=2) for b in range(2)]
                for b in range(2):
                    tt(st[:, 112 + b:116:2], num[b][:, :, DV], cols[:, 0, j, b:HM:2], ALU.max).then_inc(vec.sem, 1)
                    t = vec.more()
                eng.wait_ge(vec.sem, vec.at(q, t))
                for b in range(2):
                    eng.scalar_tensor_tensor(st[:, 112 + b:116:2], num[b][:, :, DV], -1.0, st[:, 112 + b:116:2], ALU.mult, ALU.max).then_inc(vec.sem, 1)
                    t = vec.more()
                eng.wait_ge(vec.sem, vec.at(q, t))
                eng.wait_ge(e_o.sem, e_o.at(q, j + 1))
                eng.scalar_tensor_tensor(og[:, :, :], og[:, :, :], 1.0, st[:, 112:116].unsqueeze(2).broadcast_to([P, HM, DV]), ALU.add, ALU.mult).then_inc(vec.sem, 1)
                eng.wait_ge(vec.sem, vec.next(q))
                eng.reciprocal(og[:, :, :], og[:, :, :]).then_inc(vec.sem, 1)
                eng.wait_ge(vec.sem, vec.next(q))
                for b in range(2):
                    ins = tt(hm[:, b:HM:2, :], num[b][:, :, 0:DV], og[:, b:HM:2, :], ALU.mult)
                ins.then_inc(h_ok.sem, 1)
                for b in range(2):
                    eng.wait_ge(pt_out.sem, pt_out.at(q, 4 * j + b + 1))
                    if j and b == 0:
                        eng.wait_ge(o_out.sem, o_out.at(q, j))
                    eng.tensor_copy(PT[:, b, :], ps[turned_at(b)][:, :]).then_inc(pt_vec.sem, 1)
                eng.wait_ge(h_sq.sem, h_sq.at(q, j + 1))
                eng.tensor_reduce(st[:, 100:104], og[:, :, :], AX_X, ALU.add).then_inc(vec.sem, 1)
                eng.wait_ge(vec.sem, vec.next(q))
                eng.wait_ge(o_sq.sem, o_sq.at(q, j + 1))
                eng.tensor_reduce(osum[:, :], osq[:, :].rearrange("p (i t) -> p t i", i=4), AX_X, ALU.add).then_inc(o_sum.sem, 1)
                tt(ogain[:, :].rearrange("p (i t) -> p i t", i=4), ps[7][:, :].rearrange("p (i t) -> p i t", i=4),
                             gains[:, 1, 0:4].unsqueeze(2).broadcast_to([P, 4, P]), ALU.mult).then_inc(gained.sem, 1)
                eng.wait_ge(o_ss.sem, o_ss.at(q, j + 1))
                n = 1 + 2 * j
                eng.tensor_scalar(st[:, 96:97], ps[3][:, 0:1], 1.0 / (H * DH), EPS, ALU.mult, ALU.add).then_inc(var.sem, 1)
                eng.wait_ge(var.sem, var.at(q, n + 1))
                refine(q, n + 1, st[:, 96:97], st[:, 97:98], st[:, 24 + j:25 + j], st[:, 98:99])
                eng.tensor_scalar(st[:, 104:108], st[:, 100:104], 1.0 / DV, EPS, ALU.mult, ALU.add).then_inc(var.sem, 1)
                hi = a_hi[:, 0:4, cs]
                low_part(q, 2 * NT + 2 * j + 1, a_lo[:, 0:4, cs], ogain[:, :].rearrange("p (k t) -> p k t", k=4), hi)
                eng.wait_ge(split.sem, split.at(q, 2 * NT + 2 * j + 1))
                eng.wait_ge(var.sem, var.at(q, n + 2))
                refine(q, n + 2, st[:, 104:108], st[:, 108:112], st[:, 108:112], st[:, 140:144])
                tt(hm[:, :, :], hm[:, :, :], st[:, 108:112].unsqueeze(2).broadcast_to([P, HM, DV]), ALU.mult).then_inc(hn_ok.sem, 1)
                eng.wait_ge(h_out.sem, h_out.at(q, j + 1))
                tt(ogain[:, :].rearrange("p (i t) -> p i t", i=4), ps[2][:, :].rearrange("p (i t) -> p i t", i=4),
                             gains[:, 1, 4:8].unsqueeze(2).broadcast_to([P, 4, P]), ALU.mult).then_inc(gained.sem, 1)
                eng.wait_ge(gained.sem, gained.at(q, 2 * NT + 2 * j + 2))
                low_part(q, 2 * NT + 2 * j + 2, a_lo[:, 4:8, cs], ogain[:, :].rearrange("p (k t) -> p k t", k=4), a_hi[:, 4:8, cs])

            def quarter(q, last):
                T, tiles, splits = tokens_of(last)
                NT, NN = len(tiles), len(splits)
                vec.n = 0
                norm(q, tiles, 0, 0)
                for u in range(U_T):
                    split_vec(eng, q, u + 1, 0)
                    split_vec(eng, q, u + 1, 1)
                eng.wait_ge(dn_out.sem, dn_out.at(q, 0))
                eng.memset(vm[:, :, :, DV], 1.0).then_inc(vec.sem, 1)
                eng.wait_ge(vec.sem, vec.next(q))
                o = 0
                for i, u in enumerate(range(U_T, U_O)):
                    split_vec(eng, q, u + 1, 0)
                    for n, (j, R) in enumerate(tiles):
                        o += 1
                        eng.wait_ge(tm_out.sem, tm_out.at(q, o))
                        for a, b, s, dst in tm_parts(i):
                            ins = eng.tensor_copy(dst(j, s)[0:R], ps[4 + n % 4][0:R, a:b])
                        ins.then_inc(tm_read.sem, 1)
                        if n == 1:
                            split_vec(eng, q, u + 1, 1)
                eng.wait_ge(tm_read.sem, tm_read.at(q, o))
                prompt_gates(q)
                eng.wait_ge(bias0_ok.sem, bias0_ok.at(q, 0))
                for j in range(BLK):
                    mix_block(q, NT, j)
                if last:
                    sample_vec()
                    eng.wait_ge(kwin_ps.sem, kwin_ps.at(0, 1))
                    eng.tensor_copy(kwin[:, :], ps[6][:, 0:P]).then_inc(kwin_ok.sem, 1)
                o = 0
                for i, u in enumerate(range(U_O, U_M)):
                    split_vec(eng, q, u + 1, 0)
                    for n, (j, R) in enumerate(tiles):
                        o += 1
                        eng.wait_ge(op_out.sem, op_out.at(q, o))
                        xs = x1[0:R, j, i * OPW:(i + 1) * OPW]
                        eng.scalar_tensor_tensor(xs, ps[n % 4][0:R, 0:OPW], st[0:R, 24 + j:25 + j], xs, ALU.mult, ALU.add).then_inc(vec.sem, 1)
                        eng.wait_ge(vec.sem, vec.next(q))
                        tt(xs, ps[n % 4][0:R, OPW:2 * OPW], xs, ALU.add).then_inc(op_read.sem, 1)
                        if n == 1:
                            split_vec(eng, q, u + 1, 1)
                norm(q, tiles, 4 * NT, 1)

                def step(kind, c, half, u, i):
                    end = last and isinstance(i, int) and u == UNITS - 1
                    nq, nu = (q, u + 1) if u + 1 < UNITS else (q + 1, 0)
                    if not end:
                        split_vec(eng, nq, nu, 0, i)
                    if kind == "U":
                        b = chunk_parity[u]

                        def low(l, o, t, off, w):
                            eng.wait_ge(u_high.sem, u_high.at(q, o + 1))
                            tt(u_lo[b][:, half * 2 + t, off:off + w], usq[:, l % 2, 0:w], u_hi[b][:, half * 2 + t, off:off + w].bitcast(F32), ALU.subtract).then_inc(u_split.sem, 1)

                        for t in range(2):
                            for s, (off, w) in enumerate(splits):
                                l = (half * 2 + t) * NN + s
                                o = 4 * NN * c + l
                                eng.wait_ge(up_read.sem, up_read.at(q, o + 1))
                                if not (isinstance(c, int) and c == 0 and l < 2):
                                    eng.wait_ge(u_split.sem, u_split.at(q, o - 1))
                                tt(usq[:, l % 2, 0:w], relu[:, l % 2, 0:w], relu[:, l % 2, 0:w], ALU.mult).then_inc(u_sq.sem, 1)
                                eng.wait_ge(u_sq.sem, u_sq.at(q, o + 1))
                                low(l, o, t, off, w)
                            if t == 0 and not end:
                                split_vec(eng, nq, nu, 1, i)
                    else:
                        eng.wait_ge(dn_read.sem, dn_read.at(q, 2 * NT * c))
                        for n, (j, R) in enumerate(tiles):
                            o = 2 * NT * c + half * NT + n
                            eng.wait_ge(dn_out.sem, dn_out.at(q, o + 1))
                            xs = x1[0:R, j, half * 512:half * 512 + 512]
                            tt(xs, xs, ps[4 + n % 4][0:R, :], ALU.add).then_inc(dn_read.sem, 1)
                            if n == 1 and not end:
                                split_vec(eng, nq, nu, 1, i)

                mlp_walk(eng, q, last, step)
                norm(q, tiles, 0, 2)

            give_first(eng, w_split, dn_read, y_made, pt_vec, c_ok)
            for t, v in ((mp, 0.0), (Cst, 0.0), (kk, 0.0), (vv, 0.0), (rows, 0.0), (st, 1.0), (gz, 0.0)):
                eng.memset(t[(slice(None),) * len(t.shape)], v).then_inc(setup.sem, 1)
            eng.wait_ge(const_in.sem, const_in.at(0, 16 * 10))
            eng.tensor_scalar(nsink[:, :], sink[:, :], -1.0, None, ALU.mult).then_inc(setup.sem, 1)
            eng.memset(bias[NBUCKET:NBUCKET + 1, 4, 0:H], MASKED).then_inc(setup.sem, 1)
            eng.wait_ge(bias_ps.sem, bias_ps.at(0, 1))
            eng.tensor_copy(bias_by_distance, ps[0][0:H, 0:3 * P]).then_inc(bias_sb.sem, 1)
            eng.wait_ge(setup.sem, setup.at(0, 9))
            eng.wait_ge(bias_in.sem, bias_in.at(0, 16 * H))
            eng.wait_ge(setup0.sem, setup0.at(0, 1))
            split_vec(eng, 0, 0, 0)
            split_vec(eng, 0, 0, 1)
            with eng.Fori(0, NQ - 1) as q:
                quarter(q, False)
            assert vec.n == vec.per
            quarter(NQ - 1, True)
            eng.tensor_copy(st[:, 150:151], st[:, 151:152]).then_inc(vec_end.sem, 1)

        @block.tensor
        def _(eng):
            def gemm(out, lhs, rhs, ks):
                last = ks[-1]
                for k in ks:
                    (lh, ll), (rh, rl) = lhs(k), rhs(k)
                    eng.matmul(out, lh, rh, start=(k == ks[0]), stop=False)
                    eng.matmul(out, lh, rl, start=False, stop=False)
                    ins = eng.matmul(out, ll, rh, start=False, stop=(k == last))
                return ins

            def w_at(u, k, a, n):
                b, w = u % UNIT_BUFS, unit_shape(u)[1]
                s = slice(k * w + a, k * w + a + n)
                return w_hi[b][:, s], w_lo[b][:, s]

            def a_at(k, off, n):
                return a_hi[:, k, off:off + n], a_lo[:, k, off:off + n]

            def unit_ready(q, u, i=0):
                eng.wait_ge(w_split.sem, w_split.at(q, 2 * (u + 1) + 16 * i))

            def turn(q, tiles, which):
                NT = len(tiles)
                base = 2 * NT * which
                gbase = (4 * NT) * which
                for m in range(2 * NT):
                    j, R = tiles[m // 2]
                    k = 4 * (m % 2)
                    eng.wait_ge(normed.sem, normed.at(q, NT * which + m // 2 + 1))
                    if m >= 4:
                        eng.wait_ge(gained.sem, gained.at(q, gbase + m - 3))
                    for kk_ in range(4):
                        ins = eng.transpose(ps[4 + m % 4][:, kk_ * R:(kk_ + 1) * R], xn_tile(j)[0:R, (k + kk_) * P:(k + kk_ + 1) * P], ident[0:R, 0:R])
                    ins.then_inc(turned.sem, 1)
                eng.wait_ge(split.sem, split.at(q, gbase + 2 * NT))

            def mix_block(q, NT, j):
                cs = slice(j * P, (j + 1) * P)
                eng.wait_ge(pt_vec.sem, pt_vec.at(q, 2 * j))
                eng.wait_ge(pt_act.sem, pt_act.at(q, 2 * j))
                if j:
                    eng.wait_ge(var.sem, var.at(q, 1 + 2 * j))
                eng.wait_ge(gained.sem, gained.at(q, 2 * NT + 2 * j))
                for h in range(H):
                    g, par = h // GQ, h % 2
                    rs = slice(par * DH, (par + 1) * DH)
                    b, at = score_at(h)
                    ins = eng.matmul(ps[b][:, at:at + 2 * P], zT[rs, h // 2, cs], kk[rs, int(g != par), j * P:j * P + 2 * P], start=True, stop=True)
                    if h % GQ == GQ - 1:
                        ins.then_inc(sc_out.sem, 1)
                if j:
                    eng.wait_ge(h_ok.sem, h_ok.at(q, j))
                for h in range(HM):
                    ins = eng.matmul(ps[4][:, h * P:(h + 1) * P], ident[0:HM, h:h + 1].broadcast_to([HM, P]), Mrel[:, j, :], start=True, stop=True)
                ins.then_inc(m_out.sem, 1)
                for h in range(HM):
                    i, par = h // 2, h % 2
                    rs = slice(par * DK, (par + 1) * DK)
                    ins = eng.matmul(ps[5 + 2 * par][:, i * P:(i + 1) * P], zT[rs, 6 + i, cs], zT[rs, 4 + i, cs], start=True, stop=True)
                ins.then_inc(s_out.sem, 1)
                if j:
                    eng.wait_ge(c_ok.sem, c_ok.at(q, j))
                else:
                    eng.wait_ge(c_cols.sem, c_cols.at(q, 3))
                for i in range(2):
                    ins = eng.transpose(ps[6][:, i * P:(i + 1) * P], zT[:, 6 + i, cs], ident[:, :])
                ins.then_inc(k_out.sem, 1)
                eng.wait_ge(qi_ok.sem, qi_ok.at(q, j + 1))
                eng.wait_ge(s_ok.sem, s_ok.at(q, j + 1))
                eng.wait_ge(c_ok.sem, c_ok.at(q, j))
                for h in range(HM):
                    i, par = h // 2, h % 2
                    rs = slice(par * DK, (par + 1) * DK)
                    out = ps[4 + par][:, i * (DV + 1):(i + 1) * (DV + 1)]
                    eng.matmul(out, ST[:, h, :], vm[:, j, h, :], start=True, stop=False)
                    ins = eng.matmul(out, qI[rs, i, :], Cst[rs, i, :], start=False, stop=True)
                ins.then_inc(n_out.sem, 1)
                eng.wait_ge(kw_ok.sem, kw_ok.at(q, j + 1))
                for h in range(HM):
                    i, par = h // 2, h % 2
                    ins = eng.matmul(ps[6][par * DK:(par + 1) * DK, i * (DV + 1):(i + 1) * (DV + 1)], kw[:, h, :], vm[:, j, h, :], start=True, stop=True)
                ins.then_inc(c_out.sem, 1)
                for b in range(4):
                    g, half = b // 2, b % 2
                    eng.wait_ge(p_ok.sem, p_ok.at(q, H * j + GQ * (g + 1)))
                    for hh in range(GQ):
                        ins = eng.transpose(ps[turned_at(b)][:, hh * P:(hh + 1) * P], wide[:, GQ * g + hh, half * P:(half + 1) * P], ident[:, :])
                    ins.then_inc(pt_out.sem, 1)
                eng.wait_ge(pt_vec.sem, pt_vec.at(q, 2 * j + 2))
                eng.wait_ge(pt_act.sem, pt_act.at(q, 2 * j + 2))
                for g in range(KVH):
                    for par in range(2):
                        for half in range(2):
                            rhs = PT[:, 2 * g + half, :].rearrange("p (i r t) -> p r i t", i=2, r=2)[:, par]
                            ins = eng.matmul(ps[7][par * DH:(par + 1) * DH, 2 * g * P:(2 * g + 2) * P], vv[:, j + half, g * DH:(g + 1) * DH], rhs, start=(half == 0), stop=(half == 1))
                ins.then_inc(o_out.sem, 1)
                eng.wait_ge(o_sum.sem, o_sum.at(q, j + 1))
                eng.matmul(ps[3][:, 0:1], osum[:, :], ones[:, 0:1], start=True, stop=True).then_inc(o_ss.sem, 1)
                eng.wait_ge(hn_ok.sem, hn_ok.at(q, j + 1))
                for h in range(HM):
                    ins = eng.transpose(ps[2][:, h * P:(h + 1) * P], hm[:, h, :], ident[:, :])
                ins.then_inc(h_out.sem, 1)

            def sample_pe():
                q, NT = NQ - 1, BLK + 1
                eng.wait_ge(s_in.sem, s_in.at(0, S_IN))
                eng.wait_ge(s_lf.sem, s_lf.at(0, 1))
                eng.wait_ge(c_ok.sem, c_ok.at(q, BLK))
                eng.wait_ge(pt_vec.sem, pt_vec.at(q, 2 * BLK))
                eng.wait_ge(var.sem, var.at(q, 1 + 2 * BLK))
                eng.wait_ge(gained.sem, gained.at(q, 2 * NT + 2 * BLK))
                out = ps[4][0:HM, 0:NS]
                eng.matmul(out, gz[0:NS, BLK, 0:HM], ident[0:NS, 0:NS], start=True, stop=False)
                eng.matmul(out, lf[0:NS, BLK, :], smask[:, 2, :], start=False, stop=True)
                eng.matmul(ps[5][0:HM, 0:NS], lf[0:NS, BLK, :], smask[:, 1, :], start=True, stop=True).then_inc(s_rows.sem, 1)
                for b in range(DECB):
                    ins = eng.transpose(ps[b // 4][:, (b % 4) * P:(b % 4 + 1) * P], ck[:, b, :], ident[:, :])
                ins.then_inc(s_kout.sem, 1)
                eng.wait_ge(s_rowsok.sem, s_rowsok.at(0, 1))
                eng.transpose(ps[6][0:NS, 0:96], rows[:, 0, 0:NS], ident[0:96, 0:96]).then_inc(s_cols.sem, 1)
                for h in range(HM):
                    ins = eng.matmul(ps[4][:, h * NS:(h + 1) * NS], ident[0:HM, h:h + 1].broadcast_to([HM, P]), srow[:, 4, :], start=True, stop=True)
                ins.then_inc(s_mout.sem, 1)
                eng.wait_ge(s_kok.sem, s_kok.at(0, 1))
                eng.wait_ge(s_qin.sem, s_qin.at(0, 16 * H))
                for half in range(2):
                    for g in range(KVH):
                        rs = slice(g * DH, (g + 1) * DH)
                        bank = ps[2 * g + half]
                        for b4 in range(4):
                            b = half * 4 + b4
                            eng.matmul(bank[b4 * 32:(b4 + 1) * 32, 0:P], qs[rs, b, :, :].rearrange("p h t -> p (h t)"), ckT[rs, b, :], start=True, stop=True)
                            ins = eng.matmul(bank[b4 * 32:(b4 + 1) * 32, P:P + NS], qs[rs, b, :, :].rearrange("p h t -> p (h t)"), kk[rs, 0, P + TQ:P + TMAX], start=True, stop=True)
                ins.then_inc(s_sout.sem, 1)
                for h in range(HM):
                    i, par = h // 2, h % 2
                    rs = slice(par * DK, (par + 1) * DK)
                    ins = eng.matmul(ps[5 + 2 * par][0:NS, i * NS:(i + 1) * NS], zT[rs, 6 + i, zs], zT[rs, 4 + i, zs], start=True, stop=True)
                ins.then_inc(s_tout.sem, 1)
                eng.wait_ge(s_ccols.sem, s_ccols.at(0, 3))
                for i in range(2):
                    eng.transpose(ps[6][0:NS, P + i * P:P + (i + 1) * P], zT[:, 6 + i, zs], ident[:, :])
                eng.transpose(ps[6][0:NS, 3 * P:4 * P], kk[:, 0, P + TQ:P + TMAX], ident[:, :]).then_inc(s_k2.sem, 1)
                eng.wait_ge(s_q.sem, s_q.at(0, 1))
                eng.wait_ge(s_st.sem, s_st.at(0, 1))
                for i in range(2):
                    out = [ps[4 + par][0:NS, i * (DV + 1):(i + 1) * (DV + 1)] for par in range(2)]
                    if i:
                        eng.wait_ge(s_nst.sem, s_nst.at(0, 2 * i))
                    for par in range(2):
                        ins = eng.matmul(out[par], ST[0:NS, 2 * i + par, 0:NS], vm[0:NS, BLK, 2 * i + par, :], start=True, stop=False)
                    ins.then_inc(s_nst.sem, 1)
                    eng.wait_ge(s_nst.sem, s_nst.at(0, 2 * i + 1))
                    for par in range(2):
                        rs = slice(par * DK, (par + 1) * DK)
                        for b in range(DECB):
                            ins = eng.matmul(out[par], qIm[rs, b, i, :], Cs[rs, 2 * b + i, :], start=False, stop=(b == DECB - 1))
                    ins.then_inc(s_nst.sem, 1)
                for g in range(KVH):
                    eng.wait_ge(s_p_ok.sem, s_p_ok.at(0, 4))
                    for half in range(2):
                        m = 2 * g + half
                        eng.transpose(ps[g][:, half * 256:half * 256 + P], s_p[:, m, 0:P], ident[:, :])
                        ins = eng.transpose(ps[g][0:NS, half * 256 + P:half * 256 + 2 * P], s_p[:, m, P:P + NS], ident[:, :])
                    ins.then_inc(s_ptout.sem, 1)
                eng.wait_ge(s_ptv.sem, s_ptv.at(0, 1))
                eng.wait_ge(s_pta.sem, s_pta.at(0, 1))
                for g in range(KVH):
                    rs = slice(g * DH, (g + 1) * DH)
                    for half in range(2):
                        m = 2 * g + half
                        for b4 in range(4):
                            c = half * P + b4 * 32
                            r = slice(b4 * 32, (b4 + 1) * 32)
                            eng.matmul(ps[7][rs, c:c + 32], cv[:, half * 4 + b4, rs], s_pt[:, m, r], start=True, stop=False)
                            ins = eng.matmul(ps[7][rs, c:c + 32], vv[0:NS, BLK + 1, rs], s_pt[0:NS, m, P + b4 * 32:P + (b4 + 1) * 32], start=False, stop=True)
                ins.then_inc(s_o.sem, 1)
                for b in range(DECB):
                    eng.wait_ge(s_kwm.sem, s_kwm.at(0, 4 + 4 * (b // 4)))
                    if b >= 4:
                        eng.wait_ge(s_cok.sem, s_cok.at(0, b - 3))
                    for h in range(HM):
                        i, par = h // 2, h % 2
                        ins = eng.matmul(ps[b % 4][par * DK:(par + 1) * DK, i * (DV + 1):(i + 1) * (DV + 1)], kwm[0:NS, b % 4, h * DK:(h + 1) * DK], vm[0:NS, BLK, h, :], start=True, stop=True)
                    ins.then_inc(s_c.sem, 1)
                eng.wait_ge(s_osum.sem, s_osum.at(0, 1))
                eng.wait_ge(s_new.sem, s_new.at(0, 1))
                eng.matmul(ps[6][0:NS, 0:1], osum[:, 0:NS], ones[:, 0:1], start=True, stop=True).then_inc(s_oss.sem, 1)
                eng.wait_ge(s_hn.sem, s_hn.at(0, 1))
                for h in range(HM):
                    ins = eng.transpose(ps[4][:, h * NS:(h + 1) * NS], hm[0:NS, h, :], ident[0:NS, 0:NS])
                ins.then_inc(s_hout.sem, 1)
                eng.wait_ge(s_cok.sem, s_cok.at(0, DECB))

            def quarter(q, last):
                T, tiles, splits = tokens_of(last)
                NT, NN = len(tiles), len(splits)
                eng.wait_ge(dn_read.sem, dn_read.at(q, 0))
                turn(q, tiles, 0)
                eng.wait_ge(up_read.sem, up_read.at(q, 0))
                o = 0
                for u in range(U_T):
                    unit_ready(q, u)
                    for t, f in enumerate(FM_TILES[u]):
                        for off, w in splits:
                            if o >= 4:
                                eng.wait_ge(fm_read.sem, fm_read.at(q, o - 3))
                            ins = gemm(ps[o % 4][:, 0:w], lambda k: w_at(u, k, t * P, P), lambda k: a_at(k, off, w), range(KT))
                            ins.then_inc(fm_out.sem, 1)
                            o += 1
                o = 0
                for u in range(U_T, U_O):
                    unit_ready(q, u)
                    for n, (j, R) in enumerate(tiles):
                        if o >= NT or n >= 4:
                            eng.wait_ge(tm_read.sem, tm_read.at(q, o - n + (n - 4 if n >= 4 else (n + 4 if n + 4 < NT else n) - NT) + 1))
                        ins = gemm(ps[4 + n % 4][0:R, 0:TMW], lambda k: a_at(k, j * P, R), lambda k: w_at(u, k, 0, TMW), range(KT))
                        ins.then_inc(tm_out.sem, 1)
                        o += 1
                eng.wait_ge(tm_read.sem, tm_read.at(q, 4 * NT))
                eng.wait_ge(lf_ok.sem, lf_ok.at(q, 1))
                for j in range(BLK):
                    out = ps[4][0:HM, j * P:(j + 1) * P]
                    eng.matmul(out, gz[:, j, 0:HM], ident[:, :], start=True, stop=False)
                    eng.matmul(out, lf[:, j, :], ntriu[:, :], start=False, stop=True)
                    ins = eng.matmul(ps[5][0:HM, j * P:(j + 1) * P], lf[:, j, :], triu[:, :], start=True, stop=True)
                ins.then_inc(g_rows.sem, 1)
                eng.wait_ge(r_rows.sem, r_rows.at(q, 1))
                for j in range(BLK):
                    ins = eng.transpose(ps[6][:, j * 96:(j + 1) * 96], rows[:, j, :], ident[0:96, 0:96])
                ins.then_inc(g_cols.sem, 1)
                eng.wait_ge(fm_read.sem, fm_read.at(q, N_FM * NN))
                eng.wait_ge(swapped.sem, swapped.at(q, 32))
                eng.wait_ge(carried.sem, carried.at(q, 0))
                for j in range(BLK):
                    mix_block(q, NT, j)
                if last:
                    sample_pe()
                    eng.wait_ge(var.sem, var.at(q, 2 * NT))
                    eng.transpose(ps[6][:, 0:P], kk[:, 0, TQ:TQ + P], ident[:, :]).then_inc(kwin_ps.sem, 1)
                eng.wait_ge(pt_vec.sem, pt_vec.at(q, 2 * BLK))
                eng.wait_ge(var.sem, var.at(q, 1 + 2 * NT))
                eng.wait_ge(split.sem, split.at(q, 4 * NT))
                o = 0
                for i, u in enumerate(range(U_O, U_M)):
                    unit_ready(q, u)
                    for n, (j, R) in enumerate(tiles):
                        if o >= NT or n >= 4:
                            eng.wait_ge(op_read.sem, op_read.at(q, o - n + (n - 4 if n >= 4 else (n + 4 if n + 4 < NT else n) - NT) + 1))
                        for part in range(2):
                            ins = gemm(ps[n % 4][0:R, part * OPW:(part + 1) * OPW], lambda k: a_at(k, j * P, R), lambda k: w_at(u, k, 0, OPW), range(4 * part, 4 * part + 4))
                        ins.then_inc(op_out.sem, 1)
                        o += 1
                if last:
                    eng.wait_ge(kwin_ok.sem, kwin_ok.at(0, 1))
                turn(q, tiles, 1)
                eng.wait_ge(op_read.sem, op_read.at(q, 4 * NT))

                def step(kind, c, half, u, i):
                    unit_ready(q, u, i)
                    b = chunk_parity[u]
                    if kind == "U":
                        for t in range(2):
                            for s, (off, w) in enumerate(splits):
                                l = (half * 2 + t) * NN + s
                                o = 4 * NN * c + l
                                if not (isinstance(c, int) and c == 0 and l < 4):
                                    eng.wait_ge(up_read.sem, up_read.at(q, o - 3))
                                ins = gemm(ps[l % 4][:, 0:w], lambda k: w_at(u, k, t * P, P), lambda k: a_at(k, off, w), range(KT))
                                ins.then_inc(up_out.sem, 1)
                    else:
                        eng.wait_ge(u_split.sem, u_split.at(q, 4 * NN * (c + 1)))
                        for n, (j, R) in enumerate(tiles):
                            o = 2 * NT * c + half * NT + n
                            if n < 4 and half == 0:
                                eng.wait_ge(dn_read.sem, dn_read.at(q, 2 * NT * c))
                            else:
                                eng.wait_ge(dn_read.sem, dn_read.at(q, o - (4 if n >= 4 else NT + n - (n + 4 if n + 4 < NT else n)) + 1))
                            ins = gemm(ps[4 + n % 4][0:R, :], lambda k: (u_hi[b][:, k, j * P:j * P + R], u_lo[b][:, k, j * P:j * P + R]), lambda k: w_at(u, k, 0, 512), range(4))
                            ins.then_inc(dn_out.sem, 1)

                mlp_walk(eng, q, last, step)

            give_first(eng, up_out, dn_out)
            eng.wait_ge(const_in.sem, const_in.at(0, 16 * 10))
            eng.wait_ge(setup.sem, setup.at(0, 9))
            eng.matmul(ps[0][0:H, 0:3 * P], rel_rows, bucket, start=True, stop=True).then_inc(bias_ps.sem, 1)
            eng.wait_ge(bias_sb.sem, bias_sb.at(0, 1))
            with eng.Fori(0, NQ - 1) as q:
                quarter(q, False)
            quarter(NQ - 1, True)


_INS = ['x_prompt', 'x_sample', 'cache_k_win', 'cache_v_win', 'state_C', 'state_n', 'state_m', 'rel_bias',
        'norm_mix', 'w_in', 'b_gates', 'attn_sinks', 'norm_attn_out', 'norm_mlstm_out', 'w_out', 'norm_mlp',
        'w_up', 'w_down', 'norm_final']
_OUTS = [(1, SEQ, D), (DECB, DECT, D), (1, 1, WIN, KVH, DH), (1, 1, WIN, KVH, DH), (1, 1, HM, DK, DV),
         (1, 1, HM, DK), (1, 1, HM), (1, DECB, WIN, KVH, DH), (1, DECB, WIN, KVH, DH),
         (1, DECB, HM, DK, DV), (1, DECB, HM, DK), (1, DECB, HM)]


def constants():
    import numpy as np

    i = np.arange(P)
    square = np.zeros((P, 5, P), np.float32)
    square[:, 0] = i[:, None] == i[None, :]
    square[:, 1] = i[:, None] <= i[None, :]
    square[:, 2] = -square[:, 1]
    square[:, 3] = np.where(i[:, None] <= i[None, :], 0.0, MASKED)
    square[:, 4] = 1.0
    bucket = np.zeros((NBUCKET + 1, 3 * P), np.float32)
    exact = NBUCKET // 2
    for n in range(3 * P):
        d = 2 * P - 1 - n
        if not 0 <= d <= WIN:
            row = NBUCKET
        elif d < exact:
            row = d
        else:
            row = min(exact + int(math.log(d / exact) / math.log(128 / exact) * (NBUCKET - exact)), NBUCKET - 1)
        bucket[row, n] = 1.0
    s = np.arange(NS)
    same = s[:, None] // DECT == s[None, :] // DECT
    causal = same & (s[:, None] <= s[None, :])
    sample = np.zeros((NS, 200), np.float32)
    sample[:, 0:64] = np.where(causal, 0.0, MASKED)
    sample[:, 64:128] = causal
    sample[:, 128:192] = -sample[:, 64:128]
    sample[:, 192:200] = s[:, None] // DECT == np.arange(DECB)[None, :]
    return {"c_square": square, "c_bucket": bucket, "c_sample": sample}


def kernel(**inputs):
    import numpy as _np
    import concourse.bacc as _bacc
    from concourse import mybir as _mybir
    from concourse.bass_utils import run_bass_kernel_spmd as _run

    nc = _bacc.Bacc("TRN2", target_bir_lowering=False, num_devices=1)
    arrays, args = {}, []
    for name, a in [(n, inputs[n]) for n in _INS] + list(constants().items()):
        a = _np.ascontiguousarray(a)
        arrays[f"in_{name}_dram"] = a
        args.append(nc.dram_tensor(f"in_{name}_dram", a.shape, _mybir.dt.from_np(a.dtype), kind="ExternalInput").ap())
    for i, shape in enumerate(_OUTS):
        args.append(nc.dram_tensor(f"out_{i}_dram", shape, F32, kind="ExternalOutput").ap())
    hymba_layer(nc, *args)
    r = _run(nc, [arrays], core_ids=[0])
    return tuple(r.results[0][f"out_{i}_dram"] for i in range(len(_OUTS)))
```

```python
import math
from contextlib import ExitStack

import concourse.bass as bass
from concourse import mybir

F32 = mybir.dt.float32
F32R = mybir.dt.float32r
ALU = mybir.AluOpType
ACT = mybir.ActivationFunctionType
AX_X = mybir.AxisListType.X

P = 128
D = 1024
KT = D // P
SEQ = 2048
DECB, DECT = 8, 8
NS = DECB * DECT
H, KVH, DH = 8, 2, 64
GQ = H // KVH
WIN = 128
HM, DK, DV = 4, 64, 128
FF = 4 * D
NBUCKET = 32
EPS = 1e-6
LEAST = -3e38
MASKED = -1e30

C_QA, C_KA, C_VA, C_QM, C_KM, C_VM = 0, 512, 640, 768, 1024, 1280
C_GATES = 2304

NQ = 4
TQ = SEQ // NQ
BLK = TQ // P
TMAX = TQ + NS

FM_TILES = [(0, 1), (2, 3), (4,), (5, 6), (7,), (8,)]
FM_COLS = [C_QA, C_QA + 256, C_KA, C_QM, C_KM, C_KM + P]
N_FM = 9
TMW = 290
N_TM = 4
AHEAD = P + 2 * HM
FC = 512
NC = FF // FC
U_F, U_T, U_O, U_M = 0, 6, 10, 14
UNITS = U_M + 4 * NC
PIECES = 2 * UNITS
RAW = 2
UNIT_BUFS = 2
WMAX = KT * TMW


def unit_of(u):
    if u < U_T:
        return "F", u, P * len(FM_TILES[u])
    if u < U_O:
        return "T", u - U_T, TMW
    if u < U_M:
        return "O", u - U_O, 512
    return "M", u - U_M, 256


def dmas_of(u):
    return 3 if u == U_T else 1


LANDED, _n = [], [0] * RAW
for _p in range(PIECES):
    _n[_p % RAW] += dmas_of(_p // 2)
    LANDED.append(_n[_p % RAW])
LANDED_PER = list(_n)


S_IN = 16 * (1 + 16 + 3 + 4 + 32)

PER_VEC, PER_ACT = 70, 1


class Signal:

    def __init__(self, sem, per, first=0):
        self.sem, self.per, self.first = sem, per, first
        self.n = 0

    def at(self, q, n):
        v = q * self.per + n + self.first
        assert not isinstance(v, int) or v > 0
        return v

    def more(self):
        self.n += 1
        return self.n

    def next(self, q):
        return self.at(q, self.more())


def tokens_of(last):
    if last:
        return TMAX, [(j, P) for j in range(BLK)] + [(BLK, NS)], [(0, TMAX // 2), (TMAX // 2, TMAX // 2)]
    return TQ, [(j, P) for j in range(BLK)], [(0, TQ)]


MLP_HEAD = [("U", 0)]
MLP_BODY = 3
MLP_TAIL = [("U", NC - 1), ("D", NC - 2), ("D", NC - 1)]


def hymba_layer(nc, x_prompt, x_sample, cache_k_win, cache_v_win, state_C, state_n, state_m, rel_bias,
                norm_mix, w_in, b_gates, attn_sinks, norm_attn_out, norm_mlstm_out, w_out, norm_mlp,
                w_up, w_down, norm_final, c_square, c_bucket, c_sample,
                y_prompt, y_sample, kwin_prompt, vwin_prompt, C_prompt, n_prompt, m_prompt,
                kwin_sample, vwin_sample, C_sample, n_sample, m_sample):
    ctx = ExitStack()
    with ctx:
        def sb(name, shape, dt=F32, where=ctx):
            return where.enter_context(nc.sbuf_tensor(name, shape, dt))

        raw = [sb(f"w_raw{s}", [P, WMAX // 2]) for s in range(RAW)]
        w_hi = [sb(f"w_hi{b}", [P, WMAX], F32R) for b in range(UNIT_BUFS)]
        w_lo = [sb(f"w_lo{b}", [P, WMAX], F32R) for b in range(UNIT_BUFS)]
        a_hi = sb("a_hi", [P, KT, TMAX], F32R)
        a_lo = sb("a_lo", [P, KT, TMAX], F32R)
        x1 = sb("x1", [P, BLK + 1, D])
        square = sb("square", [P, 5, P])
        ident, triu, ntriu, cmask, ones = (square[:, i, :] for i in range(5))
        bias = sb("bias", [P, H, 2 * P])
        bias0 = sb("bias0", [P, H, P])
        gains = sb("gains", [P, 3, KT])
        g_final = sb("g_final", [P, D])
        nsink = sb("nsink", [P, H])
        sink = sb("sink", [P, H])
        bgate = sb("bgate", [P, 2 * HM])
        kk = sb("kk", [P, 2, P + TMAX])
        vv = sb("vv", [P, BLK + 2, KVH * DH])
        Cst = sb("Cst", [P, 2, DV + 1])
        mp = sb("mp", [HM, BLK + 1])
        wide = sb("wide", [P, H, 2 * P])
        PT = sb("PT", [P, 4, 4 * P])
        st = sb("st", [P, 240])
        rows = sb("rows", [96, BLK, P])
        kwin = sb("kwin", [P, KVH * DH])
        Mrel = sb("Mrel", [HM, BLK, P])
        gz = sb("gz", [P, BLK + 1, 2 * HM])
        lf = sb("lf", [P, BLK + 1, HM])
        cols = sb("cols", [P, 3, BLK, HM])
        knew = sb("knew", [NS, KVH * DH])
        ms = sb("ms", [HM, 2, DECB])
        sinkc = sb("sinkc", [P, 4])
        nsinkc = sb("nsinkc", [P, 4])
        srow = sb("srow", [HM, 5, NS])
        phase = ExitStack()
        zT = sb("zT", [P, 8, TMAX], where=phase)
        vm = sb("vm", [P, BLK + 1, HM, DV + 1], where=phase)
        om = sb("om", [P, BLK + 1, HM * DV], where=phase)
        DT = sb("DT", [P, HM, P], where=phase)
        ST = sb("ST", [P, HM, P], where=phase)
        ib = sb("ib", [P, 2, P], where=phase)
        qI = sb("qI", [P, 2, P], where=phase)
        kw = sb("kw", [P, HM, DK], where=phase)
        hm = sb("hm", [P, HM, DV], where=phase)
        og = sb("og", [P, HM, DV], where=phase)
        Mrow, grow, brow, Mswap = (t[0:HM, :, :] for t in (DT, ST, hm, og))
        ogain = sb("ogain", [P, 4 * P], where=phase)
        osq = sb("osq", [P, 4 * P], where=phase)
        osum = sb("osum", [P, P], where=phase)
        phase.close()
        phase = ExitStack()
        u_hi = [sb(f"u_hi{b}", [P, 4, TMAX], F32R, phase) for b in range(2)]
        u_lo = [sb(f"u_lo{b}", [P, 4, TMAX], F32R, phase) for b in range(2)]
        relu = sb("relu", [P, 2, TMAX], where=phase)
        usq = sb("usq", [P, 2, TMAX], where=phase)
        phase.close()
        def flat(t):
            return t[(slice(None),) * len(t.shape)].rearrange("p a b c -> p (a b c)" if len(t.shape) == 4 else "p a b -> p (a b)")

        s_p = flat(wide)[:, 0:768].rearrange("p (n k) -> p n k", n=4)
        ck = flat(wide)[:, 1024:2048].rearrange("p (b c) -> p b c", b=DECB)
        s_pt = flat(PT)[:, 0:1024].rearrange("p (n k) -> p n k", n=4)
        kwm = flat(PT)[:, 1024:2048].rearrange("p (b c) -> p b c", b=4)
        s_bias = flat(bias)[:, 0:768].rearrange("p (n k) -> p n k", n=4)
        ckT = flat(bias)[:, 1024:2048].rearrange("p (b c) -> p b c", b=DECB)
        qIm = flat(bias0).rearrange("p (b i t) -> p b i t", b=DECB, i=2)
        Cs = vm[:, 0:BLK, :, :].rearrange("p j h e -> p (j h) e")
        omf = flat(om)
        cv = omf[:, 0:1024].rearrange("p (b c) -> p b c", b=DECB)
        qs = omf[:, 1024:1280].rearrange("p (b h t) -> p b h t", b=DECB, h=GQ)
        osn = omf[:, 1280:1536]
        osg = omf[:, 1536:1792].rearrange("p (h t) -> p h t", h=GQ)
        smask = omf[0:NS, 1792:1984].rearrange("p (n t) -> p n t", n=3)
        ofseq = omf[0:NS, 1984:1992]
        zs = slice(TQ, TMAX)
        ps = [ctx.enter_context(nc.psum_tensor(f"ps{b}", [P, 512], F32)) for b in range(8)]
        bias_dram = nc.dram_tensor("bias_rows", [H, P, 3 * P], F32, kind="Internal").ap()

        def signal(name, per, first=0):
            return Signal(ctx.enter_context(nc.semaphore(name)), per, first)

        const_in = signal("const_in", 0)
        setup = signal("setup", 0)
        bias_sb = signal("bias_sb", 0)
        bias_out = signal("bias_out", 0)
        bias_in = signal("bias_in", 0)
        w_landed = [signal(f"w_landed{s}", 16 * LANDED_PER[s]) for s in range(RAW)]
        w_high = signal("w_high", PIECES)
        w_split = signal("w_split", PIECES, RAW)
        x_in = [signal(f"x_in{j}", 16 * (j < BLK)) for j in range(BLK + 1)]
        nx_in = [signal("nx_in0", 32, 16), signal("nx_in1", 32)]
        nx_ssq, nx_var, nx_root = signal("nx_ssq", BLK, 1), signal("nx_var", 2, 1), signal("nx_root", 2, 1)
        nx_vec = signal("nx_vec", 8, 4)
        nx_normed, nx_turned = signal("nx_normed", BLK, 1), signal("nx_turned", 2 * BLK, 2)
        nx_gained, nx_high, nx_split = signal("nx_gained", 2 * BLK, 2), signal("nx_high", 2 * BLK, 2), signal("nx_split", 2 * BLK, 2)
        ssq = signal("ssq", 2 * BLK, 1)
        var = signal("var", 4)
        guess = signal("guess", 4)
        normed = signal("normed", BLK)
        turned = signal("turned", 2 * BLK)
        gained = signal("gained", 4 * BLK)
        high = signal("high", 4 * BLK)
        split = signal("split", 4 * BLK)
        fm_out, fm_read = signal("fm_out", N_FM), signal("fm_read", N_FM)
        swapped = signal("swapped", 32)
        tm_out, tm_read = signal("tm_out", 4 * BLK), signal("tm_read", 4 * BLK)
        op_out, op_read = signal("op_out", 4 * BLK), signal("op_read", 4 * BLK)
        up_out, up_read = signal("up_out", 4 * NC, 1), signal("up_read", 4 * NC, 1)
        u_sq = signal("u_sq", 4 * NC)
        u_high, u_split = signal("u_high", 4 * NC), signal("u_split", 4 * NC)
        dn_out, dn_read = signal("dn_out", 2 * BLK * NC, 1), signal("dn_read", 2 * BLK * NC, 1)
        y_made = signal("y_made", BLK, 1)
        y_out = [signal(f"y_out{j}", 16 * 2, 1) for j in range(2)]
        fin_out = signal("fin_out", 0)
        f_abs, l_one, lf_ok = signal("f_abs", 1), signal("l_one", 1), signal("lf_ok", 1)
        g_read, sig_ok = signal("g_read", 1), signal("sig_ok", 1)
        g_rows, r_rows, g_cols, c_cols = signal("g_rows", 1), signal("r_rows", 1), signal("g_cols", 1), signal("c_cols", 3)
        sc_out, sc_read = signal("sc_out", 2 * BLK), signal("sc_read", H * BLK)
        negmax, sumexp, es_arg, es_ok = signal("negmax", BLK), signal("sumexp", H * BLK), signal("es_arg", BLK), signal("es_ok", BLK)
        p_ok = signal("p_ok", H * BLK)
        pt_out, pt_vec, pt_act = signal("pt_out", 4 * BLK), signal("pt_vec", 2 * BLK, 1), signal("pt_act", 2 * BLK, 1)
        o_out, o_sq, o_sum, o_ss = signal("o_out", BLK), signal("o_sq", BLK), signal("o_sum", BLK), signal("o_ss", BLK)
        m_out, m_add, ib_ok, d_ok = signal("m_out", BLK), signal("m_add", BLK), signal("ib_ok", BLK), signal("d_ok", BLK)
        s_out, s_ok = signal("s_out", BLK), signal("s_ok", BLK)
        k_out, kw_ok = signal("k_out", BLK), signal("kw_ok", BLK)
        qi_ok, n_out = signal("qi_ok", BLK), signal("n_out", BLK)
        c_out, c_ok = signal("c_out", BLK), signal("c_ok", BLK, 1)
        h_ok, h_sq, hn_ok, h_out = signal("h_ok", BLK), signal("h_sq", BLK), signal("hn_ok", BLK), signal("h_out", BLK)
        carried = signal("carried", 2, 1)
        (s_in, s_bias0, s_abs, s_lone, s_lf, s_rows, s_rowsok, s_rrows, s_cols, s_ccols, s_kout, s_kok, s_qin, s_sout, s_nmax, s_sum,
         s_esa, s_esok, s_mout, s_ib, s_dadd, s_d, s_tout, s_k2, s_st, s_q, s_kw, s_eo, s_h, s_hsq, s_hn, s_hout,
         s_p_ok, s_ptout, s_ptv, s_pta, s_o, s_os, s_on, s_osq, s_osum, s_oss, s_kwm, s_c, s_cok, s_new, s_res, s_nst, s_gread) = (
            signal("s_" + n, 0) for n in (
                "in bias0 abs lone lf rows rowsok rrows cols ccols kout kok qin sout nmax sum "
                "esa esok mout ib dadd d tout k2 st q kw eo h hsq hn hout "
                "p_ok ptout ptv pta o os on osq osum oss kwm c cok new res nst gread").split())
        bias_ps, bias0_made, bias0_ok, vec_end = signal("bias_ps", 0), signal("bias0_made", 0), signal("bias0_ok", 1, 1), signal("vec_end", 0)
        kwin_ps, kwin_ok = signal("kwin_ps", 0), signal("kwin_ok", 0)
        vec = signal("vec", PER_VEC)
        act = signal("act", PER_ACT)

        bucket = bias[0:NBUCKET + 1, 0:2, :].rearrange("p a b -> p (a b)")[:, 0:3 * P]
        bias_by_distance = bias[0:H, 2:4, :].rearrange("p a b -> p (a b)")[:, 0:3 * P]
        rel_rows = bias[0:NBUCKET + 1, 4, 0:H]

        def unit_shape(u):
            kind, i, w = unit_of(u)
            return (4, 512) if kind == "O" or kind == "M" and mlp_unit(i)[0] == "D" else (KT, w)

        def mlp_unit(m):
            order = MLP_HEAD + [(k, c) for i in range(MLP_BODY) for k, c in (("U", 2 * i + 1), ("D", 2 * i), ("U", 2 * i + 2), ("D", 2 * i + 1))] + MLP_TAIL
            kind, c = order[m // 2]
            return kind, c, m % 2

        chunk_parity = {}
        kinds = MLP_HEAD + [(k, c) for i in range(MLP_BODY) for k, c in (("U", 2 * i + 1), ("D", 2 * i), ("U", 2 * i + 2), ("D", 2 * i + 1))] + MLP_TAIL
        for n, (kind, c) in enumerate(kinds):
            chunk_parity[U_M + 2 * n] = chunk_parity[U_M + 2 * n + 1] = c % 2

        block = ctx.enter_context(nc.Block())

        def give_first(eng, *signals):
            for sig in signals:
                eng.sem_inc(sig.sem, sig.first)

        @block.sync
        def _(sp):
            for dst, src in ((square[:, :, :], c_square), (bias[0:NBUCKET, 4, 0:H], rel_bias), (bucket, c_bucket),
                             (g_final[:, :], norm_final.partition_broadcast(P)),
                             (sink[:, :], attn_sinks[0, :].partition_broadcast(P)),
                             (bgate[:, :], b_gates[0, :].partition_broadcast(P))):
                sp.dma_start(dst, src).then_inc(const_in.sem, 16)
            with nc.allow_non_contiguous_dma("a few gains, one element a row"):
                for dst, g in ((gains[:, 0, :], norm_mix), (gains[:, 2, :], norm_mlp), (gains[:, 1, 0:4], norm_attn_out), (gains[:, 1, 4:8], norm_mlstm_out)):
                    sp.dma_start(dst, g[0, :].rearrange("(k p) -> p k", p=P)).then_inc(const_in.sem, 16)
            def load(q, p, src, shift=0):
                s = p % RAW
                sp.wait_ge(w_split.sem, w_split.at(q, p + 1 - RAW + shift))
                n = src.shape[1] * src.shape[2]
                dst = raw[s][:, 0:n].rearrange("p (a b) -> p a b", b=src.shape[2])
                sp.dma_start(dst, src).then_inc(w_landed[s].sem, 16)

            def mlp_piece(q, p, kind, c, half, k, shift=0):
                if kind == "U":
                    src = w_up[0, k * 512:(k + 1) * 512, bass.ds(c * FC + half * 256, 256)].rearrange("(a p) n -> p a n", p=P)
                else:
                    src = w_down[0, bass.ds(c * FC + k * 256, 256), half * 512:(half + 1) * 512].rearrange("(a p) n -> p a n", p=P)
                load(q, p, src, shift)

            def quarter(q):
                for u in range(U_M):
                    kind, i, w = unit_of(u)
                    for k in range(2):
                        p = 2 * u + k
                        r = slice(k * 512, (k + 1) * 512)
                        if kind == "F":
                            src = w_in[0, r, FM_COLS[i]:FM_COLS[i] + w]
                        elif kind == "O":
                            at = i // 2 * 512 + k * 256
                            src = w_out[0, at:at + 256, i % 2 * 512:(i % 2 + 1) * 512]
                        elif i:
                            c = C_VM + i * TMW - AHEAD
                            src = w_in[0, r, c:c + TMW]
                        else:
                            s = p % RAW
                            sp.wait_ge(w_split.sem, w_split.at(q, p + 1 - RAW))
                            dst = raw[s][:, 0:4 * TMW].rearrange("p (a b) -> p a b", b=TMW)
                            for a, b, c in ((0, P, C_VA), (P, AHEAD, C_GATES), (AHEAD, TMW, C_VM)):
                                sp.dma_start(dst[:, :, a:b], w_in[0, r, c:c + b - a].rearrange("(a p) n -> p a n", p=P)).then_inc(w_landed[s].sem, 16)
                            continue
                        load(q, p, src.rearrange("(a p) n -> p a n", p=P))
                p = 2 * U_M
                for m in range(2):
                    for k in range(2):
                        mlp_piece(q, p, "U", 0, m, k)
                        p += 1
                with sp.Fori(0, MLP_BODY) as i:
                    at = p
                    for kind, c in (("U", 2 * i + 1), ("D", 2 * i), ("U", 2 * i + 2), ("D", 2 * i + 1)):
                        for half in range(2):
                            for k in range(2):
                                mlp_piece(q, at, kind, c, half, k, 16 * i)
                                at += 1
                p += 16 * MLP_BODY
                for kind, c in MLP_TAIL:
                    for half in range(2):
                        for k in range(2):
                            mlp_piece(q, p, kind, c, half, k)
                            p += 1

            with sp.Fori(0, NQ - 1) as q:
                quarter(q)
            quarter(NQ - 1)

        def split_len(u):
            a, b = unit_shape(u)
            return a * b // 2

        def mlp_walk(eng, q, last, step):
            u = U_M
            for kind, c in MLP_HEAD:
                for half in range(2):
                    step(kind, c, half, u, 0)
                    u += 1
            with eng.Fori(0, MLP_BODY) as i:
                v = u
                for kind, c in (("U", 2 * i + 1), ("D", 2 * i), ("U", 2 * i + 2), ("D", 2 * i + 1)):
                    for half in range(2):
                        step(kind, c, half, v, i)
                        v += 1
            u += 8 * MLP_BODY
            for kind, c in MLP_TAIL:
                for half in range(2):
                    step(kind, c, half, u, 0)
                    u += 1

        def y_tile(j):
            if j % 4 < 2:
                return xn_tile(j)
            return PT[:, 2 * (j % 2):2 * (j % 2) + 2, :].rearrange("p a b -> p (a b)")

        def xn_tile(j):
            return wide[:, 4 * (j % 2):4 * (j % 2) + 4, :].rearrange("p a b -> p (a b)")

        def score_at(h):
            return 2 * (h % 2) + h // GQ, (h // 2) % 2 * 2 * P

        def turned_at(b):
            return b // 2 + 2 * (b % 2)

        def norm_count(which, NT):
            return which + 2 + 2 * (NT > BLK)

        def o_plan(last):
            return [(0, 0)] * BLK if last else [(1, 1)] * (BLK - 1) + [(1, 0)]

        def ahead(j):
            return (NS, 0, zs) if j < 0 else (P, j % 2, slice(j * P, (j + 1) * P))

        def ahead_stats(b, k):
            return st[:, 224 + 4 * k:225 + 4 * k] if b < 0 else st[:, 224 + 4 * k + 2 * b:226 + 4 * k + 2 * b]

        def tmp_tile(n):
            return PT[:, n % 2, :]

        @block.gpsimd
        def _(pool):
            pool.wait_ge(bias_sb.sem, 1)
            pool.dma_start(bias_dram, bias_by_distance.unsqueeze(1).broadcast_to([H, P, 3 * P])).then_inc(bias_out.sem, 16)
            pool.memset(bias0[:, :, :], MASKED).then_inc(bias0_made.sem, 1)
            pool.wait_ge(bias_out.sem, 16)
            for h in range(H):
                src = bass.AP(bias_dram.tensor, h * 3 * P * P + P - 1, [[3 * P - 1, P], [1, 2 * P]])
                pool.dma_start(bias[:, h, :], src).then_inc(bias_in.sem, 16)

            for dst, src in ((kwin_sample, cache_k_win), (vwin_sample, cache_v_win)):
                pool.dma_start(dst[0, :, 0:WIN - DECT].rearrange("b w g d -> b (w g d)"), src[0, :, DECT:WIN].rearrange("b w g d -> b (w g d)")).then_inc(fin_out.sem, 16)
            with nc.allow_non_contiguous_dma("a few values for the sample group"):
                pool.dma_start(ms[:, 0, :], state_m[0].rearrange("b h -> h b")).then_inc(s_in.sem, 16)
                for b4 in range(4):
                    for n in range(4):
                        src = bass.AP(attn_sinks.tensor, n // 2 * GQ, [[1, GQ], [0, DECT], [1, 1]])
                        pool.dma_start(sinkc[b4 * 32:(b4 + 1) * 32, n:n + 1], src).then_inc(s_in.sem, 16)
            QL = NQ - 1
            pool.wait_ge(pt_out.sem, pt_out.at(QL, 4 * BLK))
            pool.memset(s_bias, MASKED).then_inc(s_bias0.sem, 1)
            pool.dma_start(ck, cache_k_win[0].rearrange("b w g d -> w b (g d)")).then_inc(s_in.sem, 16)
            with nc.allow_non_contiguous_dma("n, and short rows of the bias"):
                pool.wait_ge(s_bias0.sem, s_bias0.at(0, 1))
                W3 = 3 * P
                for g in range(KVH):
                    for half in range(2):
                        for b4 in range(4):
                            rs = slice(b4 * 32, (b4 + 1) * 32)
                            at = g * GQ * P * W3 + P - 1
                            src = bass.AP(bias_dram.tensor, at, [[P * W3, GQ], [W3 - 1, DECT], [1, P]])
                            pool.dma_start(s_bias[rs, 2 * g + half, 0:P], src).then_inc(s_in.sem, 16)
                            src = bass.AP(bias_dram.tensor, at + P, [[P * W3, GQ], [W3 - 1, DECT], [1, DECT]])
                            c = P + (half * 4 + b4) * DECT
                            pool.dma_start(s_bias[rs, 2 * g + half, c:c + DECT], src).then_inc(s_in.sem, 16)
                pool.wait_ge(c_ok.sem, c_ok.at(QL, BLK))
                for par in range(2):
                    rs = slice(par * DK, (par + 1) * DK)
                    pool.dma_start(Cs[rs, :, 0:DV], state_C[0].rearrange("b h d e -> (b h) d e").rearrange("(n g) d e -> g d n e", g=2)[par]).then_inc(s_in.sem, 16)
                    pool.dma_start(Cs[rs, :, DV], state_n[0].rearrange("b h d -> (b h) d").rearrange("(n g) d -> g d n", g=2)[par]).then_inc(s_in.sem, 16)
                pool.wait_ge(h_out.sem, h_out.at(QL, BLK))
                pool.dma_start(cv, cache_v_win[0].rearrange("b w g d -> w b (g d)")).then_inc(s_in.sem, 16)
                pool.dma_start(omf[0:NS, 1792:1992], c_sample).then_inc(s_in.sem, 16)
                pool.wait_ge(s_new.sem, s_new.at(0, 1))
                for dst, src in ((kwin_sample, knew[:, :]), (vwin_sample, vv[0:NS, BLK + 1, :])):
                    pool.dma_start(dst[0, :, WIN - DECT:WIN].rearrange("b w g d -> b w (g d)"), src).then_inc(fin_out.sem, 16)
                pool.wait_ge(s_rrows.sem, s_rrows.at(0, 1))
                pool.dma_start(m_sample[0].rearrange("b h -> h b"), ms[:, 1, :]).then_inc(fin_out.sem, 16)
                pool.wait_ge(s_cok.sem, s_cok.at(0, DECB))
                for par in range(2):
                    rs = slice(par * DK, (par + 1) * DK)
                    pool.dma_start(C_sample[0].rearrange("b h d e -> (b h) d e").rearrange("(n g) d e -> g d n e", g=2)[par], Cs[rs, :, 0:DV]).then_inc(s_res.sem, 16)
                    pool.dma_start(n_sample[0].rearrange("b h d -> (b h) d").rearrange("(n g) d -> g d n", g=2)[par], Cs[rs, :, DV]).then_inc(s_res.sem, 16)
            pool.wait_ge(vec_end.sem, vec_end.at(0, 1))
            with nc.allow_non_contiguous_dma("a few state values"):
                for par in range(2):
                    rowsp = Cst[par * DK:(par + 1) * DK, :, :]
                    pool.dma_start(C_prompt[0, 0].rearrange("(i g) d e -> g d i e", g=2)[par], rowsp[:, :, 0:DV]).then_inc(fin_out.sem, 16)
                    pool.dma_start(n_prompt[0, 0].rearrange("(i g) d -> g d i", g=2)[par], rowsp[:, :, DV]).then_inc(fin_out.sem, 16)
                pool.dma_start(m_prompt[0].rearrange("a h -> h a"), mp[:, BLK:BLK + 1]).then_inc(fin_out.sem, 16)
            pool.dma_start(kwin_prompt[0, 0].rearrange("t g d -> t (g d)"), kwin[:, :]).then_inc(fin_out.sem, 16)
            pool.dma_start(vwin_prompt[0, 0].rearrange("t g d -> t (g d)"), vv[:, BLK, :]).then_inc(fin_out.sem, 16)
            pool.wait_ge(fin_out.sem, 16 * 12)
            pool.wait_ge(s_res.sem, 16 * 4)
            pool.wait_ge(y_out[0].sem, y_out[0].at(NQ - 1, 16 * 3))
            pool.wait_ge(y_out[1].sem, y_out[1].at(NQ - 1, 16 * 2))

        @block.scalar
        def _(eng):
            def unit_used(eng, q, last, u, i):
                T, tiles, splits = tokens_of(last)
                NT, NN = len(tiles), len(splits)
                kind, n, w = unit_of(u)
                if kind == "F":
                    eng.wait_ge(fm_out.sem, fm_out.at(q, NN * sum(len(t) for t in FM_TILES[:n + 1])))
                elif kind == "T":
                    eng.wait_ge(tm_out.sem, tm_out.at(q, NT * (n + 1)))
                elif kind == "O":
                    eng.wait_ge(op_out.sem, op_out.at(q, NT * (n + 1)))
                else:
                    kind, c, half = mlp_unit(n)
                    if kind == "U":
                        eng.wait_ge(up_out.sem, up_out.at(q, 4 * NN * c + 2 * NN * (half + 1) + 8 * NN * i))
                    else:
                        eng.wait_ge(dn_out.sem, dn_out.at(q, 2 * NT * c + NT * (half + 1) + 4 * NT * i))

            def split_act(eng, q, last, u, k, i=0):
                p = 2 * u + k
                n = split_len(u)
                eng.wait_ge(w_landed[p % RAW].sem, w_landed[p % RAW].at(q, 16 * LANDED[p] + 16 * 16 // RAW * i))
                if k == 0:
                    before = u - UNIT_BUFS
                    if u == 0 and not (isinstance(q, int) and q == 0):
                        unit_used(eng, q - 1, last, UNITS - 2, 0)
                    elif u == 1:
                        eng.wait_ge(dn_out.sem, dn_out.at(q, 0))
                    elif before == U_M + 1 and not isinstance(i, int):
                        unit_used(eng, q, last, before, 0)
                        eng.wait_ge(dn_out.sem, dn_out.at(q, 4 * len(tokens_of(last)[1]) * i))
                    elif u > 1:
                        unit_used(eng, q, last, before, i)
                b = u % UNIT_BUFS
                eng.activation(w_hi[b][:, k * n:(k + 1) * n], raw[p % RAW][:, 0:n], ACT.Copy).then_inc(w_high.sem, 1)

            def exp(out, in_, **kw):
                return eng.activation(out, in_, ACT.Exp, **kw)

            def guess_rsqrt(q, n, v, y):
                eng.wait_ge(var.sem, var.at(q, n))
                eng.activation(y, v, ACT.Sqrt).then_inc(guess.sem, 1)

            def high_part(q, n, dst, src):
                eng.wait_ge(gained.sem, gained.at(q, n))
                eng.activation(dst, src, ACT.Copy).then_inc(high.sem, 1)

            def norm(q, tiles, base, which):
                NT = len(tiles)
                for j, R in tiles:
                    if which == 1:
                        eng.wait_ge(op_read.sem, op_read.at(q, 4 * NT))
                    else:
                        eng.wait_ge(dn_read.sem, dn_read.at(q, 2 * NC * NT))
                    eng.wait_ge(ssq.sem, ssq.at(q, NT * (which - 1) + j))
                    eng.activation(PT[0:R, 2:4, :].rearrange("p a b -> p (a b)"), x1[0:R, j, :], ACT.Square, accum_out=st[0:R, j:j + 1]).then_inc(ssq.sem, 1)
                guess_rsqrt(q, norm_count(which, NT), st[:, 8:8 + BLK + 1], st[:, 16:16 + BLK + 1])
                if which == 2:
                    return
                for m in range(2 * NT):
                    j, R = tiles[m // 2]
                    k = 4 * (m % 2)
                    high_part(q, base + m + 1, a_hi[:, k:k + 4, j * P:j * P + R], tmp_tile(m)[:, 0:4 * R].rearrange("p (k t) -> p k t", k=4))

            def load_ahead(q, j):
                R, slot, _ = ahead(j)
                if j >= 0:
                    eng.wait_ge(nx_turned.sem, nx_turned.at(q, max(2 * (j - 1), 0)))
                src = x_sample.rearrange("b t d -> (b t) d") if j < 0 else x_prompt[0, bass.ds(q * TQ + j * P, P), :]
                eng.dma_start(xn_tile(slot)[0:R, :], src).then_inc(nx_in[slot].sem, 16)

            def stats_ahead(q, b):
                js = (-1,) if b < 0 else (2 * b, 2 * b + 1)
                for j in js:
                    R, slot, _ = ahead(j)
                    eng.wait_ge(nx_in[slot].sem, nx_in[slot].at(q, 16 * (j // 2 + 1)))
                    if j >= 0:
                        eng.wait_ge(nx_ssq.sem, nx_ssq.at(q, j))
                    at = 224 + max(j, 0)
                    eng.activation(PT[0:R, 2:4, :].rearrange("p a b -> p (a b)"), xn_tile(slot)[0:R, :], ACT.Square, accum_out=st[0:R, at:at + 1]).then_inc(nx_ssq.sem, 1)
                eng.wait_ge(nx_var.sem, nx_var.at(q, b + 1))
                eng.activation(ahead_stats(b, 2), ahead_stats(b, 1), ACT.Sqrt).then_inc(nx_root.sem, 1)

            def high_ahead(q, b):
                for j in ((-1,) if b < 0 else (2 * b, 2 * b + 1)):
                    R, _, cs = ahead(j)
                    for m in range(2):
                        eng.wait_ge(nx_gained.sem, nx_gained.at(q, 2 * j + m + 1))
                        eng.activation(a_hi[:, 4 * m:4 * m + 4, cs], tmp_tile(m)[:, 0:4 * R].rearrange("p (k t) -> p k t", k=4), ACT.Copy).then_inc(nx_high.sem, 1)

            def squares(q, j):
                eng.wait_ge(h_ok.sem, h_ok.at(q, j + 1))
                if j:
                    eng.wait_ge(h_sq.sem, h_sq.at(q, j))
                else:
                    eng.wait_ge(o_sum.sem, o_sum.at(q, BLK))
                for h in range(HM):
                    ins = eng.activation(osq[:, h * DV:(h + 1) * DV], om[:, j, h * DV:(h + 1) * DV], ACT.Square, accum_out=st[:, 160 + HM * j + h:161 + HM * j + h])
                ins.then_inc(h_sq.sem, 1)

            def quarter(q, last):
                T, tiles, splits = tokens_of(last)
                NT, NN = len(tiles), len(splits)
                act.n = 0
                for j in range(BLK):
                    eng.wait_ge(y_made.sem, y_made.at(q, 0))
                    eng.dma_start(x1[:, j, :], x_prompt[0, bass.ds(q * TQ + j * P, P), :]).then_inc(x_in[j].sem, 16)
                eng.wait_ge(up_out.sem, up_out.at(q, 0))
                eng.wait_ge(dn_out.sem, dn_out.at(q, 0))
                o = 0
                for u in range(U_T):
                    if u:
                        split_act(eng, q, last, u + 1, 0)
                        split_act(eng, q, last, u + 1, 1)
                    for f in FM_TILES[u]:
                        for off, w in splits:
                            o += 1
                            eng.wait_ge(fm_out.sem, fm_out.at(q, o))
                            dst = kk[:, 0, P + off:P + off + w] if f == 4 else zT[:, f - (f > 4), off:off + w]
                            scale = 0.125 if f < 4 or f > 6 else 1.0
                            eng.activation(dst, ps[(o - 1) % 4][:, 0:w], ACT.Copy, scale=scale).then_inc(fm_read.sem, 1)
                    if 4 in FM_TILES[u]:
                        for g in range(2):
                            eng.wait_ge(fm_read.sem, fm_read.at(q, 5 * NN))
                            eng.dma_start(kk[g * DH:(g + 1) * DH, 1, P:P + T], kk[(1 - g) * DH:(2 - g) * DH, 0, P:P + T]).then_inc(swapped.sem, 16)
                def tm_split(o, n):
                    for m in range(o, o + n):
                        if m % NT == 0 and m < 4 * NT:
                            split_act(eng, q, last, U_T + m // NT + 1, 0)
                            split_act(eng, q, last, U_T + m // NT + 1, 1)

                def op_split(o, n):
                    for m in range(o, o + n):
                        if m % NT == 0:
                            split_act(eng, q, last, U_O + m // NT + 1, 0)
                            split_act(eng, q, last, U_O + m // NT + 1, 1)

                tm_split(0, NT)
                o = NT
                eng.wait_ge(f_abs.sem, f_abs.at(q, 1))
                e1 = st[:, 32:32 + BLK * HM].rearrange("p (j h) -> p j h", h=HM)
                exp(e1, lf[:, 0:BLK, :], scale=-1.0).then_inc(act.sem, 1)
                eng.wait_ge(act.sem, act.next(q))
                eng.activation(e1, e1, ACT.Ln, bias=1.0).then_inc(l_one.sem, 1)
                for j in range(BLK):
                    cs = slice(j * P, (j + 1) * P)
                    eng.wait_ge(negmax.sem, negmax.at(q, j + 1))
                    for h in range(H):
                        exp(wide[:, h, :], wide[:, h, :], bias=st[:, 64 + h:65 + h], accum_out=st[:, 72 + h:73 + h]).then_inc(sumexp.sem, 1)
                    eng.wait_ge(es_arg.sem, es_arg.at(q, j + 1))
                    exp(st[:, 80:88], st[:, 80:88]).then_inc(es_ok.sem, 1)
                    tm_split(o, 3)
                    o += 3
                    if j:
                        eng.wait_ge(o_out.sem, o_out.at(q, j))
                    else:
                        eng.wait_ge(y_out[0].sem, y_out[0].at(q, 0))
                        eng.wait_ge(y_out[1].sem, y_out[1].at(q, 0))
                    for b in (2, 3):
                        eng.wait_ge(pt_out.sem, pt_out.at(q, 4 * j + b + 1))
                        eng.activation(PT[:, b, :], ps[turned_at(b)][:, :], ACT.Copy).then_inc(pt_act.sem, 1)
                    eng.wait_ge(o_out.sem, o_out.at(q, j + 1))
                    if j:
                        eng.wait_ge(o_sum.sem, o_sum.at(q, j))
                    eng.activation(osq[:, :], ps[7][:, :], ACT.Square).then_inc(o_sq.sem, 1)
                tm_split(o, 4 * NT - o)
                eng.wait_ge(g_cols.sem, g_cols.at(q, 1))
                gc = ps[6][:, 0:BLK * 96].rearrange("p (j r) -> p j r", r=96)
                exp(cols[:, 0, :, :], gc[:, :, 0:HM]).then_inc(c_cols.sem, 1)
                eng.activation(cols[:, 1, :, :], gc[:, :, 32:32 + HM], ACT.Copy).then_inc(c_cols.sem, 1)
                exp(cols[:, 2, :, :], gc[:, :, 64:64 + HM]).then_inc(c_cols.sem, 1)
                eng.wait_ge(tm_out.sem, tm_out.at(q, 4 * NT))
                for j in range(BLK):
                    cs = slice(j * P, (j + 1) * P)
                    high_part(q, j + 1, a_hi[:, 0:4, cs], zT[:, 0:4, cs])
                o, plan = 0, o_plan(last)
                for j in range(BLK):
                    eng.wait_ge(m_out.sem, m_out.at(q, j + 1))
                    if j:
                        eng.wait_ge(qi_ok.sem, qi_ok.at(q, j))
                    if j > 1:
                        eng.wait_ge(c_ok.sem, c_ok.at(q, j - 1))
                    for par in range(2):
                        rs = slice(par * DK, (par + 1) * DK)
                        src = ps[4][rs, :].rearrange("p (i g t) -> p g i t", g=2, i=2)[:, par]
                        exp(ib[rs, :, :], src)
                        ins = exp(st[rs, 116 + 2 * (j % 2):118 + 2 * (j % 2)], src[:, :, P - 1])
                    ins.then_inc(ib_ok.sem, 1)
                    if j == 0:
                        guess_rsqrt(q, 1, st[:, 96:96 + BLK], st[:, 104:104 + BLK])
                    eng.wait_ge(m_add.sem, m_add.at(q, j + 1))
                    eng.wait_ge(c_cols.sem, c_cols.at(q, 3))
                    for h in range(HM):
                        ins = exp(DT[:, h, :], DT[:, h, :], bias=cols[:, 1, j, h:h + 1])
                    ins.then_inc(d_ok.sem, 1)
                    if j == 0:
                        eng.wait_ge(tm_read.sem, tm_read.at(q, 4 * NT))
                        eng.activation(om[:, 0:BLK, :], om[:, 0:BLK, :], ACT.Sigmoid).then_inc(sig_ok.sem, 1)
                    else:
                        squares(q, j - 1)
                    op_split(o, sum(plan[j]))
                    o += sum(plan[j])
                squares(q, BLK - 1)
                if not last:
                    op_split(o, 2 * NT - o)
                guess_rsqrt(q, 2, st[:, 176:192], st[:, 192:208])
                for j in range(BLK):
                    high_part(q, BLK + j + 1, a_hi[:, 4:8, j * P:(j + 1) * P], ogain[:, :].rearrange("p (k t) -> p k t", k=4))
                    if j == 1 and not last:
                        op_split(2 * NT, 1)
                if last:
                    sample_act()
                if not last:
                    eng.activation(bias0[:, :, :], bias[:, :, 0:P], ACT.Copy).then_inc(bias0_ok.sem, 1)
                    eng.activation(kk[:, :, 0:P], kk[:, :, TQ:TQ + P], ACT.Copy).then_inc(carried.sem, 1)
                    eng.activation(vv[:, 0, :], vv[:, BLK, :], ACT.Copy).then_inc(carried.sem, 1)
                op_split(0 if last else 2 * NT + 1, 4 * NT if last else 2 * NT - 1)
                norm(q, tiles, 2 * NT, 1)

                def step(kind, c, half, u, i):
                    end = last and isinstance(i, int) and u == UNITS - 1
                    nq, nu = (q, u + 1) if u + 1 < UNITS else (q + 1, 0)
                    if not end:
                        split_act(eng, nq, last, nu, 0, i)
                        split_act(eng, nq, last, nu, 1, i)
                    if u == UNITS - 5 and not last:
                        load_ahead(q + 1, 0)
                        load_ahead(q + 1, 1)
                    if u == UNITS - 4 and not last:
                        stats_ahead(q + 1, 0)
                    if u == UNITS - 3 and not last:
                        high_ahead(q + 1, 0)
                        load_ahead(q + 1, 2)
                        load_ahead(q + 1, 3)
                    if u == UNITS - 2 and not last:
                        stats_ahead(q + 1, 1)
                    if u == UNITS - 1 and not last:
                        high_ahead(q + 1, 1)
                    if kind == "U":
                        b = chunk_parity[u]
                        if not (isinstance(c, int) and c < 2):
                            eng.wait_ge(dn_out.sem, dn_out.at(q, 2 * NT * (c - 1)))
                        for t in range(2):
                            for s, (off, w) in enumerate(splits):
                                l = (half * 2 + t) * NN + s
                                o = 4 * NN * c + l
                                eng.wait_ge(up_out.sem, up_out.at(q, o + 1))
                                if not (isinstance(c, int) and c == 0 and l < 2):
                                    eng.wait_ge(u_sq.sem, u_sq.at(q, o - 1))
                                    eng.wait_ge(u_high.sem, u_high.at(q, o - 1))
                                eng.activation(relu[:, l % 2, 0:w], ps[l % 4][:, 0:w], ACT.Relu).then_inc(up_read.sem, 1)
                                eng.wait_ge(up_read.sem, up_read.at(q, o + 1))
                                eng.activation(u_hi[b][:, half * 2 + t, off:off + w], relu[:, l % 2, 0:w], ACT.Square).then_inc(u_high.sem, 1)

                mlp_walk(eng, q, last, step)
                if not last:
                    split_act(eng, q + 1, False, 1, 0)
                    split_act(eng, q + 1, False, 1, 1)
                norm(q, tiles, 0, 2)
                for j, R in tiles:
                    dst = y_sample.rearrange("b t d -> (b t) d") if j == BLK else y_prompt[0, bass.ds(q * TQ + j * P, P), :]
                    eng.wait_ge(y_made.sem, y_made.at(q, j + 1))
                    eng.dma_start(dst, y_tile(j)[0:R, :]).then_inc(y_out[j % 2].sem, 16)

            def sample_act():
                q, NT, cs, j = NQ - 1, BLK + 1, zs, BLK
                eng.wait_ge(s_abs.sem, s_abs.at(0, 1))
                e1 = st[0:NS, 32:32 + HM]
                exp(e1, lf[0:NS, BLK, :], scale=-1.0).then_inc(act.sem, 1)
                t = act.more()
                eng.wait_ge(act.sem, act.at(q, t))
                eng.activation(e1, e1, ACT.Ln, bias=1.0).then_inc(s_lone.sem, 1)
                eng.wait_ge(s_in.sem, s_in.at(0, S_IN))
                for h in range(H):
                    g, par = h // GQ, h % 2
                    eng.dma_start(qs[g * DH:(g + 1) * DH, :, h % GQ, :], zT[par * DH:(par + 1) * DH, h // 2, zs].rearrange("p (b t) -> p b t", b=DECB)).then_inc(s_qin.sem, 16)
                eng.wait_ge(s_kout.sem, s_kout.at(0, 1))
                for b in range(2):
                    ins = eng.activation(ckT[:, 4 * b:4 * b + 4, :].rearrange("p b c -> p (b c)"), ps[b][:, :], ACT.Copy)
                ins.then_inc(s_kok.sem, 1)
                eng.wait_ge(s_cols.sem, s_cols.at(0, 1))
                gc = ps[6][0:NS, 0:96]
                exp(cols[0:NS, 0, 0, :], gc[:, 0:HM]).then_inc(s_ccols.sem, 1)
                eng.activation(cols[0:NS, 1, 0, :], gc[:, 32:32 + HM], ACT.Copy).then_inc(s_ccols.sem, 1)
                exp(cols[0:NS, 2, 0, :], gc[:, 64:64 + HM]).then_inc(s_ccols.sem, 1)
                eng.wait_ge(s_mout.sem, s_mout.at(0, 1))
                for par in range(2):
                    rs = slice(par * DK, (par + 1) * DK)
                    ins = exp(ib[rs, :, 0:NS], ps[4][rs, 0:HM * NS].rearrange("p (i g t) -> p g i t", g=2, i=2)[:, par])
                ins.then_inc(s_ib.sem, 1)
                eng.wait_ge(s_dadd.sem, s_dadd.at(0, 1))
                eng.wait_ge(s_ccols.sem, s_ccols.at(0, 3))
                for h in range(HM):
                    ins = exp(DT[0:NS, h, 0:NS], DT[0:NS, h, 0:NS], bias=cols[0:NS, 1, 0, h:h + 1])
                ins.then_inc(s_d.sem, 1)
                eng.wait_ge(s_nmax.sem, s_nmax.at(0, 1))
                for n in range(4):
                    exp(s_p[:, n, :], s_p[:, n, :], bias=st[:, 64 + n:65 + n], accum_out=st[:, 72 + n:73 + n]).then_inc(s_sum.sem, 1)
                eng.wait_ge(s_esa.sem, s_esa.at(0, 1))
                exp(st[:, 80:84], st[:, 80:84]).then_inc(s_esok.sem, 1)
                exp(og[0:NS, :, :].rearrange("p h e -> p (h e)"), om[0:NS, BLK, :], scale=-1.0).then_inc(s_eo.sem, 1)
                eng.wait_ge(s_ptout.sem, s_ptout.at(0, 2))
                pv = ps[1][:, :].rearrange("p (n k) -> p n k", n=2)
                eng.activation(s_pt[:, 2:4, 0:P], pv[:, :, 0:P], ACT.Copy)
                eng.activation(s_pt[0:NS, 2:4, P:2 * P], pv[0:NS, :, P:2 * P], ACT.Copy).then_inc(s_pta.sem, 1)
                eng.wait_ge(s_h.sem, s_h.at(0, 1))
                eng.activation(og[0:NS, :, :], hm[0:NS, :, :], ACT.Square).then_inc(s_hsq.sem, 1)
                eng.wait_ge(s_os.sem, s_os.at(0, 1))
                for h in range(H):
                    g, par = h // GQ, h % 2
                    eng.dma_start(osn[par * DH:(par + 1) * DH, (h // 2) * NS:(h // 2 + 1) * NS], osg[g * DH:(g + 1) * DH, h % GQ, :]).then_inc(s_on.sem, 16)
                eng.wait_ge(s_on.sem, s_on.at(0, 16 * H))
                eng.activation(osq[:, 0:4 * NS], osn[:, :], ACT.Square).then_inc(s_osq.sem, 1)
                high_part(q, 2 * j + 1, a_hi[:, 0:4, cs], ogain[:, 0:4 * NS].rearrange("p (k t) -> p k t", k=4))
                guess_rsqrt(q, 3, st[0:NS, 96:97], st[0:NS, 97:98])
                guess_rsqrt(q, 4, st[0:NS, 104:108], st[0:NS, 108:112])
                high_part(q, 2 * j + 2, a_hi[:, 4:8, cs], ogain[:, 0:4 * NS].rearrange("p (k t) -> p k t", k=4))
                eng.wait_ge(s_res.sem, s_res.at(0, 16 * 4))

            give_first(eng, ssq, up_read, pt_act, carried, bias0_ok, *y_out)
            split_act(eng, 0, False, 0, 0)
            split_act(eng, 0, False, 0, 1)
            eng.dma_start(x1[0:NS, BLK, :], x_sample.rearrange("b t d -> (b t) d")).then_inc(x_in[BLK].sem, 16)
            load_ahead(0, -1)
            eng.wait_ge(setup.sem, setup.at(0, 9))
            stats_ahead(0, -1)
            high_ahead(0, -1)
            load_ahead(0, 0)
            load_ahead(0, 1)
            for b in range(2):
                stats_ahead(0, b)
                high_ahead(0, b)
                if b == 0:
                    load_ahead(0, 2)
                    load_ahead(0, 3)
            split_act(eng, 0, False, 1, 0)
            split_act(eng, 0, False, 1, 1)
            with eng.Fori(0, NQ - 1) as q:
                quarter(q, False)
            assert act.n == act.per
            quarter(NQ - 1, True)

        @block.vector
        def _(eng):
            def split_vec(eng, q, u, k, i=0):
                p = 2 * u + k
                n = split_len(u)
                b = u % UNIT_BUFS
                eng.wait_ge(w_high.sem, w_high.at(q, p + 1 + 16 * i))
                eng.tensor_tensor(w_lo[b][:, k * n:(k + 1) * n], raw[p % RAW][:, 0:n],
                                             w_hi[b][:, k * n:(k + 1) * n].bitcast(F32), ALU.subtract).then_inc(w_split.sem, 1)

            def tt(out, a, b, op):
                return eng.tensor_tensor(out, a, b, op)

            def refine(q, n, v, y, out, tmp):
                eng.wait_ge(guess.sem, guess.at(q, n))
                eng.reciprocal(y, y).then_inc(vec.sem, 1)
                eng.wait_ge(vec.sem, vec.next(q))
                tt(tmp, y, y, ALU.mult).then_inc(vec.sem, 1)
                eng.wait_ge(vec.sem, vec.next(q))
                tt(tmp, tmp, v, ALU.mult).then_inc(vec.sem, 1)
                eng.wait_ge(vec.sem, vec.next(q))
                eng.tensor_scalar(tmp, tmp, -0.5, 1.5, ALU.mult, ALU.add).then_inc(vec.sem, 1)
                eng.wait_ge(vec.sem, vec.next(q))
                tt(out, y, tmp, ALU.mult).then_inc(vec.sem, 1)
                eng.wait_ge(vec.sem, vec.next(q))

            def low_part(q, n, dst, src, hi):
                eng.wait_ge(high.sem, high.at(q, n))
                tt(dst, src, hi.bitcast(F32), ALU.subtract).then_inc(split.sem, 1)

            def norm(q, tiles, base, which):
                NT = len(tiles)
                eng.wait_ge(ssq.sem, ssq.at(q, NT * which))
                eng.tensor_scalar(st[:, 8:8 + BLK + 1], st[:, 0:BLK + 1], 1.0 / D, EPS, ALU.mult, ALU.add).then_inc(var.sem, 1)
                n = norm_count(which, NT)
                eng.wait_ge(var.sem, var.at(q, n))
                refine(q, n, st[:, 8:8 + BLK + 1], st[:, 16:16 + BLK + 1], st[:, 132:132 + BLK + 1], st[:, 140:140 + BLK + 1])
                if which == 2:
                    for j, R in tiles:
                        if j == BLK:
                            eng.wait_ge(y_out[0].sem, y_out[0].at(q, 32))
                        eng.scalar_tensor_tensor(y_tile(j)[0:R, :], x1[0:R, j, :], st[0:R, 132 + j:133 + j], g_final[0:R, :], ALU.mult, ALU.mult).then_inc(y_made.sem, 1)
                    return

                def rows_normed(j, R):
                    if j >= 2:
                        eng.wait_ge(turned.sem, turned.at(q, 2 * (j - 1)))
                    eng.tensor_scalar(xn_tile(j)[0:R, :], x1[0:R, j, :], st[0:R, 132 + j:133 + j], None, ALU.mult).then_inc(normed.sem, 1)

                def low(m):
                    j, R = tiles[m // 2]
                    k = 4 * (m % 2)
                    s = slice(j * P, j * P + R)
                    low_part(q, base + m + 1, a_lo[:, k:k + 4, s], tmp_tile(m)[:, 0:4 * R].rearrange("p (k t) -> p k t", k=4), a_hi[:, k:k + 4, s])

                rows_normed(*tiles[0])
                rows_normed(*tiles[1])
                for m in range(2 * NT):
                    j, R = tiles[m // 2]
                    k = 4 * (m % 2)
                    eng.wait_ge(turned.sem, turned.at(q, m + 1))
                    b = 4 + m % 4
                    gain = gains[:, 2, k:k + 4].unsqueeze(2).broadcast_to([P, 4, R])
                    if m >= 2:
                        eng.wait_ge(split.sem, split.at(q, base + m - 1))
                    tt(tmp_tile(m)[:, 0:4 * R].rearrange("p (k t) -> p k t", k=4), ps[b][:, 0:4 * R].rearrange("p (k t) -> p k t", k=4), gain, ALU.mult).then_inc(gained.sem, 1)
                    if m:
                        low(m - 1)
                    if m % 2 and m // 2 + 2 < NT:
                        rows_normed(*tiles[m // 2 + 2])
                low(2 * NT - 1)

            def tm_parts(i):
                a, b = i * TMW, (i + 1) * TMW
                ends = [(0, P, lambda j, s: vv[:, j + 1, s]), (P, AHEAD, lambda j, s: gz[:, j, s])]
                for h in range(HM):
                    ends.append((AHEAD + P * h, AHEAD + P * (h + 1), lambda j, s, h=h: vm[:, j, h, s]))
                ends.append((AHEAD + HM * P, AHEAD + 2 * HM * P, lambda j, s: om[:, j, s]))
                for lo, hi, dst in ends:
                    if max(a, lo) < min(b, hi):
                        yield max(a, lo) - a, min(b, hi) - a, slice(max(a, lo) - lo, min(b, hi) - lo), dst

            def gates(q, R, tiles, absd):
                nt = tiles.stop - tiles.start
                tt(gz[0:R, tiles, :], gz[0:R, tiles, :], bgate[0:R, :].unsqueeze(1).broadcast_to([R, nt, 2 * HM]), ALU.add).then_inc(vec.sem, 1)
                eng.wait_ge(vec.sem, vec.next(q))
                f = gz[0:R, tiles, HM:2 * HM]
                eng.scalar_tensor_tensor(lf[0:R, tiles, :], f, -1.0, f, ALU.mult, ALU.max).then_inc(absd.sem, 1)

            def log_forget(q, R, tiles, l_one, lf_ok):
                nt = tiles.stop - tiles.start
                eng.wait_ge(l_one.sem, l_one.at(q, 1))
                e1 = st[0:R, 32:32 + nt * HM].rearrange("p (j h) -> p j h", h=HM)
                eng.scalar_tensor_tensor(lf[0:R, tiles, :], gz[0:R, tiles, HM:2 * HM], 0.0, e1, ALU.min, ALU.subtract).then_inc(lf_ok.sem, 1)

            def take_rows(q, n, gbank, bbank, buffers, g_rows, g_read):
                eng.wait_ge(g_rows.sem, g_rows.at(q, 1))
                eng.tensor_copy(buffers[1], gbank.rearrange("p (j t) -> p j t", j=n))
                eng.tensor_copy(buffers[2], bbank.rearrange("p (j t) -> p j t", j=n)).then_inc(g_read.sem, 1)
                eng.wait_ge(g_read.sem, g_read.at(q, 1))

            def scan(q, w, buffers, steps):
                for r in steps:
                    if r < w.bit_length() - 1:
                        src = buffers[1] if r == 0 else (buffers[0], buffers[3])[(r - 1) % 2]
                        s, dst = 1 << r, (buffers[0], buffers[3])[r % 2]
                        eng.tensor_copy(dst[:, :, 0:s], src[:, :, 0:s])
                        tt(dst[:, :, s:w], src[:, :, s:w], src[:, :, 0:w - s], ALU.max).then_inc(vec.sem, 1)
                        eng.wait_ge(vec.sem, vec.next(q))

            def stabilise(q, n, w, before, buffers, rel, out, ready):
                Mrow, grow, brow, _ = buffers
                tt(Mrow, Mrow, before, ALU.max).then_inc(vec.sem, 1)
                eng.wait_ge(vec.sem, vec.next(q))
                tt(rel, before, Mrow, ALU.subtract).then_inc(vec.sem, 1)
                eng.wait_ge(vec.sem, vec.next(q))
                eng.scalar_tensor_tensor(out(0), Mrow, -1.0, brow, ALU.mult, ALU.subtract).then_inc(vec.sem, 1)
                eng.wait_ge(vec.sem, vec.next(q))
                tt(out(32), grow, before, ALU.subtract).then_inc(vec.sem, 1)
                eng.wait_ge(vec.sem, vec.next(q))
                tt(out(64), grow, Mrow[:, :, w - 1:w].broadcast_to([HM, n, w]), ALU.subtract).then_inc(ready.sem, 1)

            def running_max(q):
                buffers = (Mrow, grow, brow, Mswap)
                eng.tensor_copy(mp[:, 0:1], mp[:, BLK:BLK + 1]).then_inc(vec.sem, 1)
                eng.wait_ge(vec.sem, vec.next(q))
                for j in range(BLK):
                    eng.scalar_tensor_tensor(mp[:, j + 1:j + 2], Mrow[:, j, P - 1:P], mp[:, j:j + 1], brow[:, j, P - 1:P], ALU.max, ALU.add).then_inc(vec.sem, 1)
                    eng.wait_ge(vec.sem, vec.next(q))
                stabilise(q, BLK, P, mp[:, 0:BLK].unsqueeze(2).broadcast_to([HM, BLK, P]), buffers, Mrel[:, :, :], lambda r: rows[r:r + HM, :, :], r_rows)

            def sample_vec():
                q, NT, cs, j, n, w = NQ - 1, BLK + 1, zs, BLK, DECB, DECT
                by_seq = lambda t: t.rearrange("p (b t) -> p b t", b=DECB)
                buffers = tuple(by_seq(srow[:, i, :]) for i in range(4))
                eng.wait_ge(s_in.sem, s_in.at(0, S_IN))
                gates(q, NS, slice(BLK, BLK + 1), s_abs)
                log_forget(q, NS, slice(BLK, BLK + 1), s_lone, s_lf)
                take_rows(q, n, ps[4][0:HM, 0:NS], ps[5][0:HM, 0:NS], buffers, s_rows, s_gread)
                scan(q, w, buffers, range(3))
                before = ms[:, 0, :].unsqueeze(2).broadcast_to([HM, n, w])
                stabilise(q, n, w, before, buffers, by_seq(srow[:, 4, :]), lambda r: by_seq(rows[r:r + HM, 0, 0:NS]), s_rowsok)
                eng.memset(qIm, 0.0).then_inc(vec.sem, 1)
                eng.wait_ge(vec.sem, vec.next(q))
                tt(ms[:, 1, :], buffers[0][:, :, w - 1], buffers[2][:, :, w - 1], ALU.add).then_inc(s_rrows.sem, 1)
                eng.tensor_scalar(nsinkc[:, :], sinkc[:, :], -1.0, None, ALU.mult).then_inc(vec.sem, 1)
                eng.wait_ge(vec.sem, vec.next(q))
                eng.wait_ge(s_sout.sem, s_sout.at(0, 1))
                for m in range(4):
                    eng.tensor_tensor_reduce(s_p[:, m, :], ps[m][:, 0:192], s_bias[:, m, :], 1.0, LEAST, ALU.add, ALU.max, st[:, 124 + m:125 + m]).then_inc(vec.sem, 1)
                    t = vec.more()
                eng.wait_ge(vec.sem, vec.at(q, t))
                eng.scalar_tensor_tensor(st[:, 64:68], st[:, 124:128], -1.0, nsinkc[:, :], ALU.mult, ALU.min).then_inc(s_nmax.sem, 1)
                eng.wait_ge(s_nmax.sem, s_nmax.at(0, 1))
                tt(st[:, 80:84], st[:, 64:68], sinkc[:, :], ALU.add).then_inc(s_esa.sem, 1)
                eng.wait_ge(s_ib.sem, s_ib.at(0, 1))
                tt(DT[0:NS, :, 0:NS], ps[4][0:NS, 0:HM * NS].rearrange("p (h t) -> p h t", h=HM), smask[:, 0, :].unsqueeze(1).broadcast_to([NS, HM, NS]), ALU.add).then_inc(s_dadd.sem, 1)
                eng.wait_ge(s_k2.sem, s_k2.at(0, 1))
                eng.wait_ge(s_ccols.sem, s_ccols.at(0, 3))
                tt(kw[0:NS, :, :], ps[6][0:NS, 128:384].rearrange("p (h d) -> p h d", h=HM), cols[0:NS, 2, 0, :].unsqueeze(2).broadcast_to([NS, HM, DK]), ALU.mult).then_inc(s_kw.sem, 1)
                eng.tensor_copy(knew[:, :], ps[6][0:NS, 384:512]).then_inc(s_new.sem, 1)
                tt(qI[:, :, 0:NS], zT[:, 4:6, zs], ib[:, :, 0:NS], ALU.mult).then_inc(vec.sem, 1)
                eng.wait_ge(vec.sem, vec.next(q))
                for b in range(DECB):
                    c = slice(b * DECT, (b + 1) * DECT)
                    ins = eng.tensor_copy(qIm[:, b, :, c], qI[:, :, c])
                ins.then_inc(s_q.sem, 1)
                eng.wait_ge(s_tout.sem, s_tout.at(0, 1))
                eng.wait_ge(s_d.sem, s_d.at(0, 1))
                for par in range(2):
                    own = lambda t: t[0:NS, :, 0:NS].rearrange("p (i r) t -> p r i t", r=2)[:, par]
                    ins = tt(own(ST), ps[5 + 2 * par][0:NS, 0:2 * NS].rearrange("p (i t) -> p i t", i=2), own(DT), ALU.mult)
                ins.then_inc(s_st.sem, 1)
                eng.wait_ge(s_esok.sem, s_esok.at(0, 1))
                eng.wait_ge(s_sum.sem, s_sum.at(0, 4))
                tt(st[:, 88:92], st[:, 72:76], st[:, 80:84], ALU.add).then_inc(vec.sem, 1)
                eng.wait_ge(vec.sem, vec.next(q))
                eng.reciprocal(st[:, 88:92], st[:, 88:92]).then_inc(vec.sem, 1)
                eng.wait_ge(vec.sem, vec.next(q))
                for m in range(4):
                    eng.tensor_scalar(s_p[:, m, :], s_p[:, m, :], st[:, 88 + m:89 + m], None, ALU.mult).then_inc(s_p_ok.sem, 1)
                eng.wait_ge(s_kw.sem, s_kw.at(0, 1))
                kwf = kw[0:NS, :, :].rearrange("p h d -> p (h d)")
                for b in range(4):
                    eng.tensor_scalar(kwm[0:NS, b, :], kwf, ofseq[:, b:b + 1], None, ALU.mult).then_inc(s_kwm.sem, 1)
                eng.wait_ge(s_ptout.sem, s_ptout.at(0, 1))
                pv = ps[0][:, :].rearrange("p (n k) -> p n k", n=2)
                eng.tensor_copy(s_pt[:, 0:2, 0:P], pv[:, :, 0:P])
                eng.tensor_copy(s_pt[0:NS, 0:2, P:2 * P], pv[0:NS, :, P:2 * P]).then_inc(s_ptv.sem, 1)
                eng.wait_ge(s_nst.sem, s_nst.at(0, 4))
                num = [ps[4 + b][0:NS, 0:2 * (DV + 1)].rearrange("p (h e) -> p h e", h=2) for b in range(2)]
                for b in range(2):
                    tt(st[0:NS, 112 + b:116:2], num[b][:, :, DV], cols[0:NS, 0, 0, b:HM:2], ALU.max).then_inc(vec.sem, 1)
                    t = vec.more()
                eng.wait_ge(vec.sem, vec.at(q, t))
                for b in range(2):
                    eng.scalar_tensor_tensor(st[0:NS, 112 + b:116:2], num[b][:, :, DV], -1.0, st[0:NS, 112 + b:116:2], ALU.mult, ALU.max).then_inc(vec.sem, 1)
                    t = vec.more()
                eng.wait_ge(vec.sem, vec.at(q, t))
                eng.wait_ge(s_eo.sem, s_eo.at(0, 1))
                eng.scalar_tensor_tensor(og[0:NS, :, :], og[0:NS, :, :], 1.0, st[0:NS, 112:116].unsqueeze(2).broadcast_to([NS, HM, DV]), ALU.add, ALU.mult).then_inc(vec.sem, 1)
                eng.wait_ge(vec.sem, vec.next(q))
                eng.reciprocal(og[0:NS, :, :], og[0:NS, :, :]).then_inc(vec.sem, 1)
                eng.wait_ge(vec.sem, vec.next(q))
                for b in range(2):
                    ins = tt(hm[0:NS, b:HM:2, :], num[b][:, :, 0:DV], og[0:NS, b:HM:2, :], ALU.mult)
                ins.then_inc(s_h.sem, 1)
                eng.wait_ge(s_o.sem, s_o.at(0, 1))
                eng.tensor_copy(osg.rearrange("p h (b t) -> p b h t", b=DECB), ps[7][:, 0:4 * NS].rearrange("p (b h t) -> p b h t", b=DECB, h=GQ)).then_inc(s_os.sem, 1)
                for b in range(DECB):
                    if b == 4:
                        for m in range(4):
                            eng.tensor_scalar(kwm[0:NS, m, :], kwf, ofseq[:, 4 + m:5 + m], None, ALU.mult).then_inc(s_kwm.sem, 1)
                    eng.wait_ge(s_c.sem, s_c.at(0, b + 1))
                    for i in range(2):
                        ins = eng.scalar_tensor_tensor(Cs[:, 2 * b + i, :], Cs[:, 2 * b + i, :], ib[:, i, b * DECT + DECT - 1:b * DECT + DECT], ps[b % 4][:, i * (DV + 1):(i + 1) * (DV + 1)], ALU.mult, ALU.add)
                    ins.then_inc(s_cok.sem, 1)
                eng.wait_ge(s_hsq.sem, s_hsq.at(0, 1))
                eng.tensor_reduce(st[0:NS, 100:104], og[0:NS, :, :], AX_X, ALU.add).then_inc(vec.sem, 1)
                eng.wait_ge(vec.sem, vec.next(q))
                eng.wait_ge(s_osq.sem, s_osq.at(0, 1))
                eng.tensor_reduce(osum[:, 0:NS], osq[:, 0:4 * NS].rearrange("p (i t) -> p t i", i=4), AX_X, ALU.add).then_inc(s_osum.sem, 1)
                og4 = ogain[:, 0:4 * NS].rearrange("p (k t) -> p k t", k=4)
                tt(og4, osn.rearrange("p (i t) -> p i t", i=4), gains[:, 1, 0:4].unsqueeze(2).broadcast_to([P, 4, NS]), ALU.mult).then_inc(gained.sem, 1)
                eng.wait_ge(s_oss.sem, s_oss.at(0, 1))
                m = 2
                eng.tensor_scalar(st[0:NS, 96:97], ps[6][0:NS, 0:1], 1.0 / (H * DH), EPS, ALU.mult, ALU.add).then_inc(var.sem, 1)
                eng.wait_ge(var.sem, var.at(q, m + 1))
                refine(q, m + 1, st[0:NS, 96:97], st[0:NS, 97:98], st[0:NS, 24 + j:25 + j], st[0:NS, 98:99])
                eng.tensor_scalar(st[0:NS, 104:108], st[0:NS, 100:104], 1.0 / DV, EPS, ALU.mult, ALU.add).then_inc(var.sem, 1)
                low_part(q, 2 * j + 1, a_lo[:, 0:4, cs], og4, a_hi[:, 0:4, cs])
                eng.wait_ge(split.sem, split.at(q, 2 * j + 1))
                eng.wait_ge(var.sem, var.at(q, m + 2))
                refine(q, m + 2, st[0:NS, 104:108], st[0:NS, 108:112], st[0:NS, 108:112], st[0:NS, 140:144])
                tt(hm[0:NS, :, :], hm[0:NS, :, :], st[0:NS, 108:112].unsqueeze(2).broadcast_to([NS, HM, DV]), ALU.mult).then_inc(s_hn.sem, 1)
                eng.wait_ge(s_hout.sem, s_hout.at(0, 1))
                tt(og4, ps[4][:, 0:4 * NS].rearrange("p (k t) -> p k t", k=4), gains[:, 1, 4:8].unsqueeze(2).broadcast_to([P, 4, NS]), ALU.mult).then_inc(gained.sem, 1)
                eng.wait_ge(gained.sem, gained.at(q, 2 * j + 2))
                low_part(q, 2 * j + 2, a_lo[:, 4:8, cs], og4, a_hi[:, 4:8, cs])

            def scale_ahead(q, b):
                eng.wait_ge(nx_ssq.sem, nx_ssq.at(q, 2 * b + 2))
                eng.tensor_scalar(ahead_stats(b, 1), ahead_stats(b, 0), 1.0 / D, EPS, ALU.mult, ALU.add).then_inc(nx_var.sem, 1)
                eng.wait_ge(nx_root.sem, nx_root.at(q, b + 1))
                y, tmp = ahead_stats(b, 2), ahead_stats(b, 3)
                eng.reciprocal(y, y).then_inc(nx_vec.sem, 1)
                eng.wait_ge(nx_vec.sem, nx_vec.at(q, 4 * b + 1))
                tt(tmp, y, y, ALU.mult).then_inc(nx_vec.sem, 1)
                eng.wait_ge(nx_vec.sem, nx_vec.at(q, 4 * b + 2))
                eng.scalar_tensor_tensor(tmp, tmp, -0.5, ahead_stats(b, 1), ALU.mult, ALU.mult).then_inc(nx_vec.sem, 1)
                eng.wait_ge(nx_vec.sem, nx_vec.at(q, 4 * b + 3))
                eng.scalar_tensor_tensor(y, tmp, 1.5, y, ALU.add, ALU.mult).then_inc(nx_vec.sem, 1)
                eng.wait_ge(nx_vec.sem, nx_vec.at(q, 4 * b + 4))
                for n, j in enumerate((-1,) if b < 0 else (2 * b, 2 * b + 1)):
                    R, slot, _ = ahead(j)
                    rows_ = xn_tile(slot)[0:R, :]
                    eng.tensor_scalar(rows_, rows_, y[0:R, n:n + 1], None, ALU.mult).then_inc(nx_normed.sem, 1)

            def take_ahead(q, b):
                for j in ((-1,) if b < 0 else (2 * b, 2 * b + 1)):
                    R, _, cs = ahead(j)
                    for m in range(2):
                        n = 2 * j + m
                        tmp = tmp_tile(m)[:, 0:4 * R].rearrange("p (k t) -> p k t", k=4)
                        eng.wait_ge(nx_turned.sem, nx_turned.at(q, n + 1))
                        if j >= 0:
                            eng.wait_ge(nx_split.sem, nx_split.at(q, n - 1))
                        gain = gains[:, 0, 4 * m:4 * m + 4].unsqueeze(2).broadcast_to([P, 4, R])
                        tt(tmp, ps[n % 4][:, 0:4 * R].rearrange("p (k t) -> p k t", k=4), gain, ALU.mult).then_inc(nx_gained.sem, 1)
                        eng.wait_ge(nx_high.sem, nx_high.at(q, n + 1))
                        tt(a_lo[:, 4 * m:4 * m + 4, cs], tmp, a_hi[:, 4 * m:4 * m + 4, cs].bitcast(F32), ALU.subtract).then_inc(nx_split.sem, 1)

            def score_max(q, j):
                if j:
                    eng.wait_ge(pt_out.sem, pt_out.at(q, 4 * j))
                for h in range(H):
                    if h % GQ == 0:
                        eng.wait_ge(sc_out.sem, sc_out.at(q, 2 * j + h // GQ + 1))
                        eng.memset(st[:, 152 + h // GQ:153 + h // GQ], 0.0)
                    mx, (b, at) = st[:, 124 + h:125 + h], score_at(h)
                    if j:
                        eng.tensor_tensor_reduce(wide[:, h, :], ps[b][:, at:at + 2 * P], bias[:, h, :], 1.0, LEAST, ALU.add, ALU.max, mx).then_inc(sc_read.sem, 1)
                    else:
                        eng.tensor_tensor_reduce(wide[:, h, 0:P], ps[b][:, at:at + P], bias0[:, h, :], 1.0, LEAST, ALU.add, ALU.max, mx).then_inc(vec.sem, 1)
                        eng.wait_ge(vec.sem, vec.next(q))
                        eng.memset(st[:, 144 + h:145 + h], 0.0)
                        eng.tensor_tensor_reduce(wide[:, h, P:2 * P], ps[b][:, at + P:at + 2 * P], bias[:, h, P:2 * P], 1.0, mx, ALU.add, ALU.max, mx).then_inc(sc_read.sem, 1)
                eng.wait_ge(sc_read.sem, sc_read.at(q, H * (j + 1)))
                eng.scalar_tensor_tensor(st[:, 64:72], st[:, 124:132], -1.0, nsink[:, :], ALU.mult, ALU.min).then_inc(negmax.sem, 1)
                eng.wait_ge(negmax.sem, negmax.at(q, j + 1))
                tt(st[:, 80:88], st[:, 64:72], sink[:, :], ALU.add).then_inc(es_arg.sem, 1)

            def divide(q, j):
                eng.wait_ge(es_ok.sem, es_ok.at(q, j + 1))
                eng.wait_ge(sumexp.sem, sumexp.at(q, H * (j + 1)))
                tt(st[:, 88:96], st[:, 72:80], st[:, 80:88], ALU.add).then_inc(vec.sem, 1)
                eng.wait_ge(vec.sem, vec.next(q))
                eng.reciprocal(st[:, 88:96], st[:, 88:96]).then_inc(vec.sem, 1)
                eng.wait_ge(vec.sem, vec.next(q))
                for h in range(H):
                    eng.tensor_scalar(wide[:, h, :], wide[:, h, :], st[:, 88 + h:89 + h], None, ALU.mult).then_inc(p_ok.sem, 1)

            def take_turned(q, j):
                for b in range(2):
                    eng.wait_ge(pt_out.sem, pt_out.at(q, 4 * j + b + 1))
                    if j and b == 0:
                        eng.wait_ge(o_out.sem, o_out.at(q, j))
                    eng.tensor_copy(PT[:, b, :], ps[turned_at(b)][:, :]).then_inc(pt_vec.sem, 1)

            def take_values(q, NT, j):
                eng.wait_ge(o_sq.sem, o_sq.at(q, j + 1))
                if j:
                    eng.wait_ge(o_ss.sem, o_ss.at(q, j))
                eng.tensor_reduce(osum[:, :], osq[:, :].rearrange("p (i t) -> p t i", i=4), AX_X, ALU.add).then_inc(o_sum.sem, 1)
                tt(zT[:, 0:4, j * P:(j + 1) * P], ps[7][:, :].rearrange("p (i t) -> p i t", i=4), gains[:, 1, 0:4].unsqueeze(2).broadcast_to([P, 4, P]), ALU.mult).then_inc(gained.sem, 1)

            def relate(q, j):
                eng.wait_ge(m_out.sem, m_out.at(q, j + 1))
                eng.wait_ge(ib_ok.sem, ib_ok.at(q, j + 1))
                tt(DT[:, :, :], ps[4][:, :].rearrange("p (h t) -> p h t", h=HM), cmask.unsqueeze(1).broadcast_to([P, HM, P]), ALU.add).then_inc(m_add.sem, 1)
                if j:
                    eng.wait_ge(n_out.sem, n_out.at(q, j))
                tt(qI[:, :, :], zT[:, 4:6, j * P:(j + 1) * P], ib[:, :, :], ALU.mult).then_inc(qi_ok.sem, 1)

            def weigh(q, j):
                eng.wait_ge(s_out.sem, s_out.at(q, j + 1))
                eng.wait_ge(d_ok.sem, d_ok.at(q, j + 1))
                for par in range(2):
                    own = lambda t: t[:, :, :].rearrange("p (i r) t -> p r i t", r=2)[:, par]
                    ins = tt(own(ST), ps[5 + 2 * par][:, 0:2 * P].rearrange("p (i t) -> p i t", i=2), own(DT), ALU.mult)
                ins.then_inc(s_ok.sem, 1)
                eng.wait_ge(s_ok.sem, s_ok.at(q, j + 1))

            def heads(q, j):
                eng.wait_ge(n_out.sem, n_out.at(q, j + 1))
                num = [ps[2 + b][:, 0:2 * (DV + 1)].rearrange("p (h e) -> p h e", h=2) for b in range(2)]
                for b in range(2):
                    ins = tt(st[:, 112 + b:116:2], num[b][:, :, DV], cols[:, 0, j, b:HM:2], ALU.max)
                ins.then_inc(vec.sem, 1)
                eng.wait_ge(vec.sem, vec.next(q))
                for b in range(2):
                    ins = eng.scalar_tensor_tensor(st[:, 112 + b:116:2], num[b][:, :, DV], -1.0, st[:, 112 + b:116:2], ALU.mult, ALU.max)
                ins.then_inc(vec.sem, 1)
                eng.wait_ge(vec.sem, vec.next(q))
                eng.reciprocal(st[:, 112:116], st[:, 112:116]).then_inc(vec.sem, 1)
                eng.wait_ge(vec.sem, vec.next(q))
                eng.wait_ge(sig_ok.sem, sig_ok.at(q, 1))
                om4 = om[:, j, :].rearrange("p (h e) -> p h e", h=HM)
                tt(og[:, :, :], om4, st[:, 112:116].unsqueeze(2).broadcast_to([P, HM, DV]), ALU.mult).then_inc(vec.sem, 1)
                eng.wait_ge(vec.sem, vec.next(q))
                for b in range(2):
                    ins = tt(om4[:, b:HM:2, :], num[b][:, :, 0:DV], og[:, b:HM:2, :], ALU.mult)
                ins.then_inc(h_ok.sem, 1)

            def update_state(q, j):
                eng.wait_ge(c_out.sem, c_out.at(q, j + 1))
                for i in range(2):
                    at = 116 + 2 * (j % 2) + i
                    ins = eng.scalar_tensor_tensor(Cst[:, i, :], Cst[:, i, :], st[:, at:at + 1], ps[6][:, i * (DV + 1):(i + 1) * (DV + 1)], ALU.mult, ALU.add)
                ins.then_inc(c_ok.sem, 1)

            def scale_heads(q, j):
                om4 = om[:, j, :].rearrange("p (h e) -> p h e", h=HM)
                r = st[:, 192 + HM * j:192 + HM * (j + 1)].unsqueeze(2).broadcast_to([P, HM, DV])
                tt(om4, om4, r, ALU.mult).then_inc(hn_ok.sem, 1)

            def gain_heads(q, NT, j):
                og4 = ogain[:, :].rearrange("p (i t) -> p i t", i=4)
                eng.wait_ge(h_out.sem, h_out.at(q, j + 1))
                eng.wait_ge(split.sem, split.at(q, BLK + j))
                tt(og4, ps[2 + j % 2][:, :].rearrange("p (i t) -> p i t", i=4), gains[:, 1, 4:8].unsqueeze(2).broadcast_to([P, 4, P]), ALU.mult).then_inc(gained.sem, 1)

            def low_heads(q, NT, j):
                cs = slice(j * P, (j + 1) * P)
                eng.wait_ge(gained.sem, gained.at(q, BLK + j + 1))
                low_part(q, BLK + j + 1, a_lo[:, 4:8, cs], ogain[:, :].rearrange("p (k t) -> p k t", k=4), a_hi[:, 4:8, cs])

            def quarter(q, last):
                T, tiles, splits = tokens_of(last)
                NT, NN = len(tiles), len(splits)
                vec.n = 0
                for u in range(1, U_T):
                    split_vec(eng, q, u + 1, 0)
                    split_vec(eng, q, u + 1, 1)
                eng.wait_ge(dn_out.sem, dn_out.at(q, 0))
                eng.memset(vm[:, :, :, DV], 1.0).then_inc(vec.sem, 1)
                eng.wait_ge(vec.sem, vec.next(q))
                def tm_step(o):
                    i, n = divmod(o, NT)
                    j, R = tiles[n]
                    eng.wait_ge(tm_out.sem, tm_out.at(q, o + 1))
                    for a, b, s, dst in tm_parts(i):
                        ins = eng.tensor_copy(dst(j, s)[0:R], ps[4 + o % 2][0:R, a:b])
                    ins.then_inc(tm_read.sem, 1)

                def tm_split(o, n):
                    for m in range(o, o + n):
                        if m % NT == 0 and m < 4 * NT:
                            split_vec(eng, q, U_T + m // NT + 1, 0)
                            split_vec(eng, q, U_T + m // NT + 1, 1)

                def op_step(o):
                    i, n = divmod(o, NT)
                    j, R = tiles[n]
                    eng.wait_ge(op_out.sem, op_out.at(q, o + 1))
                    xs = x1[0:R, j, i % 2 * 512:i % 2 * 512 + 512]
                    src = ps[o % 2][0:R, :]
                    if i == 0:
                        eng.wait_ge(x_in[j].sem, x_in[j].at(0 if j == BLK else q, 16))
                    if i < 2:
                        eng.scalar_tensor_tensor(xs, src, st[0:R, 24 + j:25 + j], xs, ALU.mult, ALU.add).then_inc(op_read.sem, 1)
                    else:
                        if o == 2 * NT:
                            eng.wait_ge(op_read.sem, op_read.at(q, o))
                        tt(xs, src, xs, ALU.add).then_inc(op_read.sem, 1)
                    if n == 0:
                        split_vec(eng, q, U_O + i + 1, 0)
                        split_vec(eng, q, U_O + i + 1, 1)

                tm_split(0, 1)
                for o in range(NT):
                    tm_step(o)
                eng.wait_ge(tm_read.sem, tm_read.at(q, NT))
                gates(q, P, slice(0, BLK), f_abs)
                eng.wait_ge(bias0_ok.sem, bias0_ok.at(q, 0))
                eng.wait_ge(y_out[0].sem, y_out[0].at(q, 0))
                eng.wait_ge(y_out[1].sem, y_out[1].at(q, 0))
                score_max(q, 0)
                log_forget(q, P, slice(0, BLK), l_one, lf_ok)
                o, buffers = NT, (Mrow, grow, brow, Mswap)
                for j in range(BLK):
                    if j == 0:
                        take_rows(q, BLK, ps[6][0:HM, :], ps[7][0:HM, :], buffers, g_rows, g_read)
                    tm_step(o)
                    tm_step(o + 1)
                    divide(q, j)
                    scan(q, P, buffers, range(3 * j, 3 * j + 3))
                    take_turned(q, j)
                    if j == 2:
                        running_max(q)
                    tm_step(o + 2)
                    tm_split(o, 3)
                    o += 3
                    if j + 1 < BLK:
                        score_max(q, j + 1)
                    take_values(q, NT, j)
                tm_split(o, 4 * NT - o)
                for o in range(o, 4 * NT):
                    tm_step(o)
                eng.wait_ge(o_ss.sem, o_ss.at(q, BLK))
                eng.tensor_scalar(st[:, 96:96 + BLK], ps[6][:, 400:400 + BLK], 1.0 / (H * DH), EPS, ALU.mult, ALU.add).then_inc(var.sem, 1)
                eng.wait_ge(gained.sem, gained.at(q, BLK))
                for j in range(BLK):
                    cs = slice(j * P, (j + 1) * P)
                    low_part(q, j + 1, a_lo[:, 0:4, cs], zT[:, 0:4, cs], a_hi[:, 0:4, cs])
                relate(q, 0)
                eng.wait_ge(var.sem, var.at(q, 1))
                refine(q, 1, st[:, 96:96 + BLK], st[:, 104:104 + BLK], st[:, 24:24 + BLK], st[:, 140:140 + BLK])
                weigh(q, 0)
                o, plan = 0, o_plan(last)
                for j in range(BLK):
                    for _ in range(plan[j][0]):
                        op_step(o)
                        o += 1
                    eng.wait_ge(k_out.sem, k_out.at(q, j + 1))
                    if j:
                        eng.wait_ge(c_out.sem, c_out.at(q, j))
                    tt(kw[:, :, :], ps[6][:, 0:HM * DK].rearrange("p (h d) -> p h d", h=HM), cols[:, 2, j, :].unsqueeze(2).broadcast_to([P, HM, DK]), ALU.mult).then_inc(kw_ok.sem, 1)
                    heads(q, j)
                    if j + 1 < BLK:
                        relate(q, j + 1)
                    for _ in range(plan[j][1]):
                        op_step(o)
                        o += 1
                    update_state(q, j)
                    if j + 1 < BLK:
                        weigh(q, j + 1)
                if not last:
                    for o in range(o, 2 * NT):
                        op_step(o)
                eng.wait_ge(h_sq.sem, h_sq.at(q, BLK))
                eng.tensor_scalar(st[:, 176:192], st[:, 160:176], 1.0 / DV, EPS, ALU.mult, ALU.add).then_inc(var.sem, 1)
                eng.wait_ge(var.sem, var.at(q, 2))
                refine(q, 2, st[:, 176:192], st[:, 192:208], st[:, 192:208], st[:, 208:224])
                scale_heads(q, 0)
                scale_heads(q, 1)
                for j in range(BLK):
                    gain_heads(q, NT, j)
                    if j + 2 < BLK:
                        scale_heads(q, j + 2)
                    low_heads(q, NT, j)
                    if j and not last:
                        op_step(2 * NT + j - 1)
                if last:
                    sample_vec()
                    eng.wait_ge(kwin_ps.sem, kwin_ps.at(0, 1))
                    eng.tensor_copy(kwin[:, :], ps[6][:, 0:P]).then_inc(kwin_ok.sem, 1)
                for o in range(0 if last else 2 * NT + BLK - 1, 4 * NT):
                    op_step(o)
                eng.wait_ge(op_read.sem, op_read.at(q, 4 * NT))
                norm(q, tiles, 2 * NT, 1)

                def step(kind, c, half, u, i):
                    end = last and isinstance(i, int) and u == UNITS - 1
                    nq, nu = (q, u + 1) if u + 1 < UNITS else (q + 1, 0)
                    if not end:
                        split_vec(eng, nq, nu, 0, i)
                    if u == UNITS - 4 and not last:
                        scale_ahead(q + 1, 0)
                    if u == UNITS - 3 and not last:
                        take_ahead(q + 1, 0)
                    if u == UNITS - 2 and not last:
                        scale_ahead(q + 1, 1)
                    if u == UNITS - 1 and not last:
                        take_ahead(q + 1, 1)
                    if kind == "U":
                        b = chunk_parity[u]

                        def low(l, o, t, off, w):
                            eng.wait_ge(u_high.sem, u_high.at(q, o + 1))
                            tt(u_lo[b][:, half * 2 + t, off:off + w], usq[:, l % 2, 0:w], u_hi[b][:, half * 2 + t, off:off + w].bitcast(F32), ALU.subtract).then_inc(u_split.sem, 1)

                        for t in range(2):
                            for s, (off, w) in enumerate(splits):
                                l = (half * 2 + t) * NN + s
                                o = 4 * NN * c + l
                                eng.wait_ge(up_read.sem, up_read.at(q, o + 1))
                                if not (isinstance(c, int) and c == 0 and l < 2):
                                    eng.wait_ge(u_split.sem, u_split.at(q, o - 1))
                                tt(usq[:, l % 2, 0:w], relu[:, l % 2, 0:w], relu[:, l % 2, 0:w], ALU.mult).then_inc(u_sq.sem, 1)
                                eng.wait_ge(u_sq.sem, u_sq.at(q, o + 1))
                                low(l, o, t, off, w)
                            if t == 0 and not end:
                                split_vec(eng, nq, nu, 1, i)
                    else:
                        eng.wait_ge(dn_read.sem, dn_read.at(q, 2 * NT * c))
                        for n, (j, R) in enumerate(tiles):
                            o = 2 * NT * c + half * NT + n
                            eng.wait_ge(dn_out.sem, dn_out.at(q, o + 1))
                            xs = x1[0:R, j, half * 512:half * 512 + 512]
                            tt(xs, xs, ps[4 + n % 4][0:R, :], ALU.add).then_inc(dn_read.sem, 1)
                            if n == 1 and not end:
                                split_vec(eng, nq, nu, 1, i)

                mlp_walk(eng, q, last, step)
                if not last:
                    split_vec(eng, q + 1, 1, 0)
                    split_vec(eng, q + 1, 1, 1)
                norm(q, tiles, 0, 2)

            give_first(eng, w_split, dn_read, y_made, pt_vec, c_ok)
            for t, v in ((mp, 0.0), (Cst, 0.0), (kk, 0.0), (vv, 0.0), (rows, 0.0), (st, 1.0), (gz, 0.0)):
                eng.memset(t[(slice(None),) * len(t.shape)], v).then_inc(setup.sem, 1)
            eng.wait_ge(const_in.sem, const_in.at(0, 16 * 10))
            eng.tensor_scalar(nsink[:, :], sink[:, :], -1.0, None, ALU.mult).then_inc(setup.sem, 1)
            eng.memset(bias[NBUCKET:NBUCKET + 1, 4, 0:H], MASKED).then_inc(setup.sem, 1)
            eng.wait_ge(bias_ps.sem, bias_ps.at(0, 1))
            eng.tensor_copy(bias_by_distance, ps[0][0:H, 0:3 * P]).then_inc(bias_sb.sem, 1)
            eng.wait_ge(setup.sem, setup.at(0, 9))
            eng.wait_ge(bias_in.sem, bias_in.at(0, 16 * H))
            eng.wait_ge(bias0_made.sem, bias0_made.at(0, 1))
            split_vec(eng, 0, 0, 0)
            split_vec(eng, 0, 0, 1)
            for b in (-1, 0, 1):
                scale_ahead(0, b)
                take_ahead(0, b)
            split_vec(eng, 0, 1, 0)
            split_vec(eng, 0, 1, 1)
            with eng.Fori(0, NQ - 1) as q:
                quarter(q, False)
            assert vec.n == vec.per
            quarter(NQ - 1, True)
            eng.tensor_copy(st[:, 150:151], st[:, 151:152]).then_inc(vec_end.sem, 1)

        @block.tensor
        def _(eng):
            def gemm(out, lhs, rhs, ks):
                last = ks[-1]
                for k in ks:
                    (lh, ll), (rh, rl) = lhs(k), rhs(k)
                    eng.matmul(out, lh, rh, start=(k == ks[0]), stop=False)
                    eng.matmul(out, lh, rl, start=False, stop=False)
                    ins = eng.matmul(out, ll, rh, start=False, stop=(k == last))
                return ins

            def w_at(u, k, a, n):
                b, w = u % UNIT_BUFS, unit_shape(u)[1]
                s = slice(k * w + a, k * w + a + n)
                return w_hi[b][:, s], w_lo[b][:, s]

            def a_at(k, off, n):
                return a_hi[:, k, off:off + n], a_lo[:, k, off:off + n]

            def unit_ready(q, u, i=0):
                eng.wait_ge(w_split.sem, w_split.at(q, 2 * (u + 1) + 16 * i))

            def turn(q, tiles, which):
                NT = len(tiles)
                for m in range(2 * NT):
                    j, R = tiles[m // 2]
                    k = 4 * (m % 2)
                    eng.wait_ge(normed.sem, normed.at(q, m // 2 + 1))
                    if m >= 4:
                        eng.wait_ge(gained.sem, gained.at(q, 2 * NT + m - 3))
                    for kk_ in range(4):
                        ins = eng.transpose(ps[4 + m % 4][:, kk_ * R:(kk_ + 1) * R], xn_tile(j)[0:R, (k + kk_) * P:(k + kk_ + 1) * P], ident[0:R, 0:R])
                    ins.then_inc(turned.sem, 1)
                eng.wait_ge(split.sem, split.at(q, 2 * NT + 2 * NT))

            def turn_ahead(q, b):
                for j in ((-1,) if b < 0 else (2 * b, 2 * b + 1)):
                    R, slot, _ = ahead(j)
                    eng.wait_ge(nx_normed.sem, nx_normed.at(q, j + 1))
                    for m in range(2):
                        n = 2 * j + m
                        if j >= 1:
                            eng.wait_ge(nx_gained.sem, nx_gained.at(q, n - 3))
                        for k in range(4):
                            ins = eng.transpose(ps[n % 4][:, k * R:(k + 1) * R], xn_tile(slot)[0:R, (4 * m + k) * P:(4 * m + k + 1) * P], ident[0:R, 0:R])
                        ins.then_inc(nx_turned.sem, 1)

            def scores(q, j):
                cs = slice(j * P, (j + 1) * P)
                eng.wait_ge(pt_vec.sem, pt_vec.at(q, 2 * j))
                eng.wait_ge(pt_act.sem, pt_act.at(q, 2 * j))
                for h in range(H):
                    g, par = h // GQ, h % 2
                    rs = slice(par * DH, (par + 1) * DH)
                    b, at = score_at(h)
                    ins = eng.matmul(ps[b][:, at:at + 2 * P], zT[rs, h // 2, cs], kk[rs, int(g != par), j * P:j * P + 2 * P], start=True, stop=True)
                    if h % GQ == GQ - 1:
                        ins.then_inc(sc_out.sem, 1)

            def turn_probs(q, j):
                for b in range(4):
                    g, half = b // 2, b % 2
                    eng.wait_ge(p_ok.sem, p_ok.at(q, H * j + GQ * (g + 1)))
                    for hh in range(GQ):
                        ins = eng.transpose(ps[turned_at(b)][:, hh * P:(hh + 1) * P], wide[:, GQ * g + hh, half * P:(half + 1) * P], ident[:, :])
                    ins.then_inc(pt_out.sem, 1)

            def values(q, NT, j):
                eng.wait_ge(pt_vec.sem, pt_vec.at(q, 2 * j + 2))
                eng.wait_ge(pt_act.sem, pt_act.at(q, 2 * j + 2))
                eng.wait_ge(gained.sem, gained.at(q, j))
                for g in range(KVH):
                    for par in range(2):
                        for half in range(2):
                            rhs = PT[:, 2 * g + half, :].rearrange("p (i r t) -> p r i t", i=2, r=2)[:, par]
                            ins = eng.matmul(ps[7][par * DH:(par + 1) * DH, 2 * g * P:(2 * g + 2) * P], vv[:, j + half, g * DH:(g + 1) * DH], rhs, start=(half == 0), stop=(half == 1))
                ins.then_inc(o_out.sem, 1)

            def sum_squares(q, j):
                eng.wait_ge(o_sum.sem, o_sum.at(q, j + 1))
                eng.matmul(ps[6][:, 400 + j:401 + j], osum[:, :], ones[:, 0:1], start=True, stop=True).then_inc(o_ss.sem, 1)

            def relate(q, NT, j):
                cs = slice(j * P, (j + 1) * P)
                if j:
                    eng.wait_ge(m_add.sem, m_add.at(q, j))
                    eng.wait_ge(s_ok.sem, s_ok.at(q, j))
                else:
                    eng.wait_ge(gained.sem, gained.at(q, BLK))
                for h in range(HM):
                    ins = eng.matmul(ps[4][:, h * P:(h + 1) * P], ident[0:HM, h:h + 1].broadcast_to([HM, P]), Mrel[:, j, :], start=True, stop=True)
                ins.then_inc(m_out.sem, 1)
                for h in range(HM):
                    i, par = h // 2, h % 2
                    rs = slice(par * DK, (par + 1) * DK)
                    ins = eng.matmul(ps[5 + 2 * par][:, i * P:(i + 1) * P], zT[rs, 6 + i, cs], zT[rs, 4 + i, cs], start=True, stop=True)
                ins.then_inc(s_out.sem, 1)

            def turn_keys(q, j):
                if j:
                    eng.wait_ge(c_ok.sem, c_ok.at(q, j))
                else:
                    eng.wait_ge(var.sem, var.at(q, 1))
                for i in range(2):
                    ins = eng.transpose(ps[6][:, i * P:(i + 1) * P], zT[:, 6 + i, j * P:(j + 1) * P], ident[:, :])
                ins.then_inc(k_out.sem, 1)

            def numerators(q, j):
                eng.wait_ge(qi_ok.sem, qi_ok.at(q, j + 1))
                eng.wait_ge(s_ok.sem, s_ok.at(q, j + 1))
                eng.wait_ge(c_ok.sem, c_ok.at(q, j))
                if j:
                    eng.wait_ge(h_ok.sem, h_ok.at(q, j))
                for h in range(HM):
                    i, par = h // 2, h % 2
                    rs = slice(par * DK, (par + 1) * DK)
                    out = ps[2 + par][:, i * (DV + 1):(i + 1) * (DV + 1)]
                    eng.matmul(out, ST[:, h, :], vm[:, j, h, :], start=True, stop=False)
                    ins = eng.matmul(out, qI[rs, i, :], Cst[rs, i, :], start=False, stop=True)
                ins.then_inc(n_out.sem, 1)

            def state_sums(q, j):
                eng.wait_ge(kw_ok.sem, kw_ok.at(q, j + 1))
                for h in range(HM):
                    i, par = h // 2, h % 2
                    ins = eng.matmul(ps[6][par * DK:(par + 1) * DK, i * (DV + 1):(i + 1) * (DV + 1)], kw[:, h, :], vm[:, j, h, :], start=True, stop=True)
                ins.then_inc(c_out.sem, 1)

            def turn_heads(q, NT, j):
                eng.wait_ge(hn_ok.sem, hn_ok.at(q, j + 1))
                if j > 1:
                    eng.wait_ge(gained.sem, gained.at(q, BLK + j - 1))
                for h in range(HM):
                    ins = eng.transpose(ps[2 + j % 2][:, h * P:(h + 1) * P], om[:, j, h * DV:(h + 1) * DV], ident[:, :])
                ins.then_inc(h_out.sem, 1)

            def sample_pe():
                q, NT = NQ - 1, BLK + 1
                eng.wait_ge(s_in.sem, s_in.at(0, S_IN))
                eng.wait_ge(s_lf.sem, s_lf.at(0, 1))
                eng.wait_ge(c_ok.sem, c_ok.at(q, BLK))
                eng.wait_ge(pt_vec.sem, pt_vec.at(q, 2 * BLK))
                eng.wait_ge(var.sem, var.at(q, 2))
                eng.wait_ge(gained.sem, gained.at(q, 2 * BLK))
                out = ps[4][0:HM, 0:NS]
                eng.matmul(out, gz[0:NS, BLK, 0:HM], ident[0:NS, 0:NS], start=True, stop=False)
                eng.matmul(out, lf[0:NS, BLK, :], smask[:, 2, :], start=False, stop=True)
                eng.matmul(ps[5][0:HM, 0:NS], lf[0:NS, BLK, :], smask[:, 1, :], start=True, stop=True).then_inc(s_rows.sem, 1)
                for b in range(DECB):
                    ins = eng.transpose(ps[b // 4][:, (b % 4) * P:(b % 4 + 1) * P], ck[:, b, :], ident[:, :])
                ins.then_inc(s_kout.sem, 1)
                eng.wait_ge(s_rowsok.sem, s_rowsok.at(0, 1))
                eng.transpose(ps[6][0:NS, 0:96], rows[:, 0, 0:NS], ident[0:96, 0:96]).then_inc(s_cols.sem, 1)
                for h in range(HM):
                    ins = eng.matmul(ps[4][:, h * NS:(h + 1) * NS], ident[0:HM, h:h + 1].broadcast_to([HM, P]), srow[:, 4, :], start=True, stop=True)
                ins.then_inc(s_mout.sem, 1)
                eng.wait_ge(s_kok.sem, s_kok.at(0, 1))
                eng.wait_ge(s_qin.sem, s_qin.at(0, 16 * H))
                for half in range(2):
                    for g in range(KVH):
                        rs = slice(g * DH, (g + 1) * DH)
                        bank = ps[2 * g + half]
                        for b4 in range(4):
                            b = half * 4 + b4
                            eng.matmul(bank[b4 * 32:(b4 + 1) * 32, 0:P], qs[rs, b, :, :].rearrange("p h t -> p (h t)"), ckT[rs, b, :], start=True, stop=True)
                            ins = eng.matmul(bank[b4 * 32:(b4 + 1) * 32, P:P + NS], qs[rs, b, :, :].rearrange("p h t -> p (h t)"), kk[rs, 0, P + TQ:P + TMAX], start=True, stop=True)
                ins.then_inc(s_sout.sem, 1)
                for h in range(HM):
                    i, par = h // 2, h % 2
                    rs = slice(par * DK, (par + 1) * DK)
                    ins = eng.matmul(ps[5 + 2 * par][0:NS, i * NS:(i + 1) * NS], zT[rs, 6 + i, zs], zT[rs, 4 + i, zs], start=True, stop=True)
                ins.then_inc(s_tout.sem, 1)
                eng.wait_ge(s_ccols.sem, s_ccols.at(0, 3))
                for i in range(2):
                    eng.transpose(ps[6][0:NS, P + i * P:P + (i + 1) * P], zT[:, 6 + i, zs], ident[:, :])
                eng.transpose(ps[6][0:NS, 3 * P:4 * P], kk[:, 0, P + TQ:P + TMAX], ident[:, :]).then_inc(s_k2.sem, 1)
                eng.wait_ge(s_q.sem, s_q.at(0, 1))
                eng.wait_ge(s_st.sem, s_st.at(0, 1))
                for i in range(2):
                    out = [ps[4 + par][0:NS, i * (DV + 1):(i + 1) * (DV + 1)] for par in range(2)]
                    if i:
                        eng.wait_ge(s_nst.sem, s_nst.at(0, 2 * i))
                    for par in range(2):
                        ins = eng.matmul(out[par], ST[0:NS, 2 * i + par, 0:NS], vm[0:NS, BLK, 2 * i + par, :], start=True, stop=False)
                    ins.then_inc(s_nst.sem, 1)
                    eng.wait_ge(s_nst.sem, s_nst.at(0, 2 * i + 1))
                    for par in range(2):
                        rs = slice(par * DK, (par + 1) * DK)
                        for b in range(DECB):
                            ins = eng.matmul(out[par], qIm[rs, b, i, :], Cs[rs, 2 * b + i, :], start=False, stop=(b == DECB - 1))
                    ins.then_inc(s_nst.sem, 1)
                for g in range(KVH):
                    eng.wait_ge(s_p_ok.sem, s_p_ok.at(0, 4))
                    for half in range(2):
                        m = 2 * g + half
                        eng.transpose(ps[g][:, half * 256:half * 256 + P], s_p[:, m, 0:P], ident[:, :])
                        ins = eng.transpose(ps[g][0:NS, half * 256 + P:half * 256 + 2 * P], s_p[:, m, P:P + NS], ident[:, :])
                    ins.then_inc(s_ptout.sem, 1)
                eng.wait_ge(s_ptv.sem, s_ptv.at(0, 1))
                eng.wait_ge(s_pta.sem, s_pta.at(0, 1))
                for g in range(KVH):
                    rs = slice(g * DH, (g + 1) * DH)
                    for half in range(2):
                        m = 2 * g + half
                        for b4 in range(4):
                            c = half * P + b4 * 32
                            r = slice(b4 * 32, (b4 + 1) * 32)
                            eng.matmul(ps[7][rs, c:c + 32], cv[:, half * 4 + b4, rs], s_pt[:, m, r], start=True, stop=False)
                            ins = eng.matmul(ps[7][rs, c:c + 32], vv[0:NS, BLK + 1, rs], s_pt[0:NS, m, P + b4 * 32:P + (b4 + 1) * 32], start=False, stop=True)
                ins.then_inc(s_o.sem, 1)
                for b in range(DECB):
                    eng.wait_ge(s_kwm.sem, s_kwm.at(0, 4 + 4 * (b // 4)))
                    if b >= 4:
                        eng.wait_ge(s_cok.sem, s_cok.at(0, b - 3))
                    for h in range(HM):
                        i, par = h // 2, h % 2
                        ins = eng.matmul(ps[b % 4][par * DK:(par + 1) * DK, i * (DV + 1):(i + 1) * (DV + 1)], kwm[0:NS, b % 4, h * DK:(h + 1) * DK], vm[0:NS, BLK, h, :], start=True, stop=True)
                    ins.then_inc(s_c.sem, 1)
                eng.wait_ge(s_osum.sem, s_osum.at(0, 1))
                eng.wait_ge(s_new.sem, s_new.at(0, 1))
                eng.matmul(ps[6][0:NS, 0:1], osum[:, 0:NS], ones[:, 0:1], start=True, stop=True).then_inc(s_oss.sem, 1)
                eng.wait_ge(s_hn.sem, s_hn.at(0, 1))
                for h in range(HM):
                    ins = eng.transpose(ps[4][:, h * NS:(h + 1) * NS], hm[0:NS, h, :], ident[0:NS, 0:NS])
                ins.then_inc(s_hout.sem, 1)
                eng.wait_ge(s_cok.sem, s_cok.at(0, DECB))

            def quarter(q, last):
                T, tiles, splits = tokens_of(last)
                NT, NN = len(tiles), len(splits)
                eng.wait_ge(nx_split.sem, nx_split.at(q, 2 * BLK))
                o = 0
                for u in range(U_T):
                    unit_ready(q, u)
                    for t, f in enumerate(FM_TILES[u]):
                        for off, w in splits:
                            if o >= 4:
                                eng.wait_ge(fm_read.sem, fm_read.at(q, o - 3))
                            ins = gemm(ps[o % 4][:, 0:w], lambda k: w_at(u, k, t * P, P), lambda k: a_at(k, off, w), range(KT))
                            ins.then_inc(fm_out.sem, 1)
                            o += 1
                def tm_step(o):
                    i, n = divmod(o, NT)
                    j, R = tiles[n]
                    if n == 0:
                        unit_ready(q, U_T + i)
                    if o >= 2:
                        eng.wait_ge(tm_read.sem, tm_read.at(q, o - 1))
                    gemm(ps[4 + o % 2][0:R, 0:TMW], lambda k: a_at(k, j * P, R), lambda k: w_at(U_T + i, k, 0, TMW), range(KT)).then_inc(tm_out.sem, 1)

                def op_step(o):
                    i, n = divmod(o, NT)
                    j, R = tiles[n]
                    if n == 0:
                        unit_ready(q, U_O + i)
                    if o >= 2:
                        eng.wait_ge(op_read.sem, op_read.at(q, o - 1))
                    if i == 0 and not last:
                        eng.wait_ge(split.sem, split.at(q, n + 1))
                    gemm(ps[o % 2][0:R, :], lambda k: a_at(k + i // 2 * 4, j * P, R), lambda k: w_at(U_O + i, k, 0, 512), range(4)).then_inc(op_out.sem, 1)

                eng.wait_ge(dn_read.sem, dn_read.at(q, 0))
                for o in range(NT):
                    tm_step(o)
                o = NT
                eng.wait_ge(fm_read.sem, fm_read.at(q, N_FM * NN))
                eng.wait_ge(swapped.sem, swapped.at(q, 32))
                eng.wait_ge(carried.sem, carried.at(q, 0))
                scores(q, 0)
                eng.wait_ge(lf_ok.sem, lf_ok.at(q, 1))
                for j in range(BLK):
                    out = ps[6][0:HM, j * P:(j + 1) * P]
                    eng.matmul(out, gz[:, j, 0:HM], ident[:, :], start=True, stop=False)
                    eng.matmul(out, lf[:, j, :], ntriu[:, :], start=False, stop=True)
                    ins = eng.matmul(ps[7][0:HM, j * P:(j + 1) * P], lf[:, j, :], triu[:, :], start=True, stop=True)
                ins.then_inc(g_rows.sem, 1)
                for j in range(BLK):
                    tm_step(o)
                    tm_step(o + 1)
                    if j:
                        sum_squares(q, j - 1)
                    turn_probs(q, j)
                    if j == BLK - 1:
                        eng.wait_ge(r_rows.sem, r_rows.at(q, 1))
                        for i in range(BLK):
                            ins = eng.transpose(ps[6][:, i * 96:(i + 1) * 96], rows[:, i, :], ident[0:96, 0:96])
                        ins.then_inc(g_cols.sem, 1)
                    tm_step(o + 2)
                    o += 3
                    if j + 1 < BLK:
                        scores(q, j + 1)
                    if j == 0:
                        eng.wait_ge(g_read.sem, g_read.at(q, 1))
                    values(q, NT, j)
                for o in range(o, 4 * NT):
                    tm_step(o)
                eng.wait_ge(c_cols.sem, c_cols.at(q, 3))
                sum_squares(q, BLK - 1)
                eng.wait_ge(tm_read.sem, tm_read.at(q, 4 * NT))
                relate(q, NT, 0)
                o, plan = 0, o_plan(last)
                for j in range(BLK):
                    for _ in range(plan[j][0]):
                        op_step(o)
                        o += 1
                    turn_keys(q, j)
                    numerators(q, j)
                    if j + 1 < BLK:
                        relate(q, NT, j + 1)
                    for _ in range(plan[j][1]):
                        op_step(o)
                        o += 1
                    state_sums(q, j)
                if not last:
                    for o in range(o, 2 * NT):
                        op_step(o)
                for j in range(BLK):
                    turn_heads(q, NT, j)
                    if j and not last:
                        eng.wait_ge(split.sem, split.at(q, BLK + j))
                        op_step(2 * NT + j - 1)
                if last:
                    sample_pe()
                    eng.wait_ge(var.sem, var.at(q, 4))
                    eng.transpose(ps[6][:, 0:P], kk[:, 0, TQ:TQ + P], ident[:, :]).then_inc(kwin_ps.sem, 1)
                eng.wait_ge(split.sem, split.at(q, 2 * NT if last else 2 * BLK))
                for o in range(0 if last else 2 * NT + BLK - 1, 4 * NT):
                    op_step(o)
                if last:
                    eng.wait_ge(kwin_ok.sem, kwin_ok.at(0, 1))
                turn(q, tiles, 1)
                eng.wait_ge(op_read.sem, op_read.at(q, 4 * NT))

                def step(kind, c, half, u, i):
                    if u == UNITS - 3 and not last:
                        eng.wait_ge(up_read.sem, up_read.at(q + 1, 0))
                        turn_ahead(q + 1, 0)
                    if u == UNITS - 1 and not last:
                        turn_ahead(q + 1, 1)
                    unit_ready(q, u, i)
                    b = chunk_parity[u]
                    if kind == "U":
                        for t in range(2):
                            for s, (off, w) in enumerate(splits):
                                l = (half * 2 + t) * NN + s
                                o = 4 * NN * c + l
                                if not (isinstance(c, int) and c == 0 and l < 4):
                                    eng.wait_ge(up_read.sem, up_read.at(q, o - 3))
                                ins = gemm(ps[l % 4][:, 0:w], lambda k: w_at(u, k, t * P, P), lambda k: a_at(k, off, w), range(KT))
                                ins.then_inc(up_out.sem, 1)
                    else:
                        eng.wait_ge(u_split.sem, u_split.at(q, 4 * NN * (c + 1)))
                        for n, (j, R) in enumerate(tiles):
                            o = 2 * NT * c + half * NT + n
                            if n < 4 and half == 0:
                                eng.wait_ge(dn_read.sem, dn_read.at(q, 2 * NT * c))
                            else:
                                eng.wait_ge(dn_read.sem, dn_read.at(q, o - (4 if n >= 4 else NT + n - (n + 4 if n + 4 < NT else n)) + 1))
                            ins = gemm(ps[4 + n % 4][0:R, :], lambda k: (u_hi[b][:, k, j * P:j * P + R], u_lo[b][:, k, j * P:j * P + R]), lambda k: w_at(u, k, 0, 512), range(4))
                            ins.then_inc(dn_out.sem, 1)

                mlp_walk(eng, q, last, step)

            give_first(eng, up_out, dn_out)
            eng.wait_ge(const_in.sem, const_in.at(0, 16 * 10))
            eng.wait_ge(setup.sem, setup.at(0, 9))
            eng.matmul(ps[0][0:H, 0:3 * P], rel_rows, bucket, start=True, stop=True).then_inc(bias_ps.sem, 1)
            eng.wait_ge(bias_sb.sem, bias_sb.at(0, 1))
            for b in (-1, 0, 1):
                turn_ahead(0, b)
            with eng.Fori(0, NQ - 1) as q:
                quarter(q, False)
            quarter(NQ - 1, True)


_INS = ['x_prompt', 'x_sample', 'cache_k_win', 'cache_v_win', 'state_C', 'state_n', 'state_m', 'rel_bias',
        'norm_mix', 'w_in', 'b_gates', 'attn_sinks', 'norm_attn_out', 'norm_mlstm_out', 'w_out', 'norm_mlp',
        'w_up', 'w_down', 'norm_final']
_OUTS = [(1, SEQ, D), (DECB, DECT, D), (1, 1, WIN, KVH, DH), (1, 1, WIN, KVH, DH), (1, 1, HM, DK, DV),
         (1, 1, HM, DK), (1, 1, HM), (1, DECB, WIN, KVH, DH), (1, DECB, WIN, KVH, DH),
         (1, DECB, HM, DK, DV), (1, DECB, HM, DK), (1, DECB, HM)]


def constants():
    import numpy as np

    i = np.arange(P)
    square = np.zeros((P, 5, P), np.float32)
    square[:, 0] = i[:, None] == i[None, :]
    square[:, 1] = i[:, None] <= i[None, :]
    square[:, 2] = -square[:, 1]
    square[:, 3] = np.where(i[:, None] <= i[None, :], 0.0, MASKED)
    square[:, 4] = 1.0
    bucket = np.zeros((NBUCKET + 1, 3 * P), np.float32)
    exact = NBUCKET // 2
    for n in range(3 * P):
        d = 2 * P - 1 - n
        if not 0 <= d <= WIN:
            row = NBUCKET
        elif d < exact:
            row = d
        else:
            row = min(exact + int(math.log(d / exact) / math.log(128 / exact) * (NBUCKET - exact)), NBUCKET - 1)
        bucket[row, n] = 1.0
    s = np.arange(NS)
    same = s[:, None] // DECT == s[None, :] // DECT
    causal = same & (s[:, None] <= s[None, :])
    sample = np.zeros((NS, 200), np.float32)
    sample[:, 0:64] = np.where(causal, 0.0, MASKED)
    sample[:, 64:128] = causal
    sample[:, 128:192] = -sample[:, 64:128]
    sample[:, 192:200] = s[:, None] // DECT == np.arange(DECB)[None, :]
    return {"c_square": square, "c_bucket": bucket, "c_sample": sample}


def kernel(**inputs):
    import numpy as _np
    import concourse.bacc as _bacc
    from concourse import mybir as _mybir
    from concourse.bass_utils import run_bass_kernel_spmd as _run

    nc = _bacc.Bacc("TRN2", target_bir_lowering=False, num_devices=1)
    arrays, args = {}, []
    for name, a in [(n, inputs[n]) for n in _INS] + list(constants().items()):
        a = _np.ascontiguousarray(a)
        arrays[f"in_{name}_dram"] = a
        args.append(nc.dram_tensor(f"in_{name}_dram", a.shape, _mybir.dt.from_np(a.dtype), kind="ExternalInput").ap())
    for i, shape in enumerate(_OUTS):
        args.append(nc.dram_tensor(f"out_{i}_dram", shape, F32, kind="ExternalOutput").ap())
    hymba_layer(nc, *args)
    r = _run(nc, [arrays], core_ids=[0])
    return tuple(r.results[0][f"out_{i}_dram"] for i in range(len(_OUTS)))
```
